# Optimizing a Trainium2 kernel written in Bass

```python
import jax, jax.numpy as jnp
from jax import lax
import numpy as np

D_MODEL = 1024
BATCH = 1
SEQ = 512
DEPTH = 1

D_MIX = D_MODEL
HG_HEADS = 4
HG_DK = 128
HG_DV = 128
HG_WIDTH = HG_HEADS * HG_DV
HG_CHUNK = 64
SA_HEADS = 4
SA_HEAD_DIM = 64
SA_WIDTH = SA_HEADS * SA_HEAD_DIM
IDX_HEADS = 8
IDX_DIM = 32
IDX_TOPK_MAX = 256
IDX_TOPK_DIV = 4
Q_BLOCK = 128
CV_WIDTH = D_MIX - HG_WIDTH - SA_WIDTH
CV_WIDTH_FILTER = 31
D_FF = 4 * D_MODEL
N_MOD = 6
EPS = 1e-6
NEG_BIG = -1e30
TINY = 1e-30

IN_SIZES = (
    HG_HEADS * HG_DK,
    HG_HEADS * HG_DK,
    HG_WIDTH,
    HG_WIDTH,
    SA_WIDTH,
    SA_WIDTH,
    SA_WIDTH,
    IDX_HEADS * IDX_DIM,
    IDX_DIM,
    IDX_HEADS,
    2 * CV_WIDTH,
)
D_IN = sum(IN_SIZES)


def rmsnorm(x, w):
    xf = x.astype(jnp.float32)
    y = xf * lax.rsqrt(jnp.mean(xf * xf, axis=-1, keepdims=True) + EPS)
    return (y * w.astype(jnp.float32)).astype(x.dtype)

def hgrn2_lower_bounds(lb_logits):
    p = jax.nn.softmax(lb_logits.astype(jnp.float32), axis=0)
    return jnp.cumsum(p, axis=0) - p[0]

def hgrn2_mixer(q_raw, f_raw, i_in, g_raw, lb, onorm_w):
    f32 = jnp.float32
    dt = q_raw.dtype
    bsz, L, _ = q_raw.shape
    lb = lb.astype(f32)
    fr = f_raw.astype(f32)
    q = jax.nn.silu(q_raw.astype(f32)) * (HG_DK ** -0.5)
    f = lb + (1.0 - lb) * jax.nn.sigmoid(fr)
    log_f = jnp.log(jnp.maximum(f, TINY))
    k = (1.0 - lb) * jax.nn.sigmoid(-fr)
    v = i_in.astype(f32)
    n_chunks = L // HG_CHUNK

    def to_chunks(t, d):
        return t.reshape(bsz, n_chunks, HG_CHUNK, HG_HEADS, d).transpose(1, 0, 3, 2, 4)

    causal = jnp.tril(jnp.ones((HG_CHUNK, HG_CHUNK), dtype=bool))

    def step(S, xs):
        qc, kc, gc, vc = xs
        G = jnp.cumsum(gc, axis=-2)
        o_inter = jnp.einsum('bhik,bhkv->bhiv', qc * jnp.exp(G), S)
        diff = G[:, :, :, None, :] - G[:, :, None, :, :]
        decay = jnp.exp(jnp.where(causal[:, :, None], diff, NEG_BIG))
        A = jnp.einsum('bhik,bhijk,bhjk->bhij', qc, decay, kc)
        o_intra = jnp.einsum('bhij,bhjv->bhiv', A, vc)
        G_last = G[:, :, -1:, :]
        S_new = jnp.exp(G_last[:, :, 0, :])[..., None] * S + jnp.einsum(
            'bhjk,bhjv->bhkv', kc * jnp.exp(G_last - G), vc)
        return S_new, o_inter + o_intra

    S0 = jnp.zeros((bsz, HG_HEADS, HG_DK, HG_DV), f32)
    _, o = lax.scan(step, S0, (to_chunks(q, HG_DK), to_chunks(k, HG_DK),
                               to_chunks(log_f, HG_DK), to_chunks(v, HG_DV)))
    o = o.transpose(1, 0, 3, 2, 4).reshape(bsz, L, HG_HEADS, HG_DV)
    o = o * lax.rsqrt(jnp.mean(o * o, axis=-1, keepdims=True) + EPS)
    o = o * onorm_w.astype(f32).reshape(HG_HEADS, HG_DV)
    o = o.reshape(bsz, L, HG_WIDTH) * jax.nn.silu(g_raw.astype(f32))
    return o.astype(dt)

def dsa_mixer(q, k, v, q_idx, k_idx, w_idx):
    f32 = jnp.float32
    dt = q.dtype
    bsz, L, _ = q.shape
    topk = min(IDX_TOPK_MAX, L // IDX_TOPK_DIV)
    n_blk = L // Q_BLOCK
    q = q.reshape(bsz, L, SA_HEADS, SA_HEAD_DIM)
    k = k.reshape(bsz, L, SA_HEADS, SA_HEAD_DIM)
    v = v.reshape(bsz, L, SA_HEADS, SA_HEAD_DIM)
    q_idx = q_idx.reshape(bsz, L, IDX_HEADS, IDX_DIM)
    w_idx = w_idx.astype(f32) * (IDX_HEADS ** -0.5)
    k_idx_f = k_idx.astype(f32)
    key_pos = jnp.arange(L, dtype=jnp.int32)

    def blocks(t):
        return t.reshape(bsz, n_blk, Q_BLOCK, *t.shape[2:]).swapaxes(0, 1)

    def one_block(xs):
        qb, qib, wb, t0 = xs
        qpos = t0 + jnp.arange(Q_BLOCK, dtype=jnp.int32)
        s = jnp.einsum('bqhd,bsd->bqhs', qib.astype(f32), k_idx_f) * (IDX_DIM ** -0.5)
        score = jnp.einsum('bqh,bqhs->bqs', wb, jax.nn.relu(s))
        admissible = key_pos[None, :] <= qpos[:, None]
        score = jnp.where(admissible[None], score, NEG_BIG)
        _, sel = lax.top_k(score, topk)
        valid = sel <= qpos[None, :, None]
        kg = jax.vmap(lambda kk, ii: kk[ii])(k, sel)
        vg = jax.vmap(lambda vv, ii: vv[ii])(v, sel)
        logits = jnp.einsum('bqhd,bqkhd->bqhk', qb.astype(f32), kg.astype(f32)) * (SA_HEAD_DIM ** -0.5)
        logits = jnp.where(valid[:, :, None, :], logits, NEG_BIG)
        p = jax.nn.softmax(logits, axis=-1)
        o = jnp.einsum('bqhk,bqkhd->bqhd', p, vg.astype(f32))
        return o.reshape(bsz, Q_BLOCK, SA_WIDTH).astype(dt)

    t0s = jnp.arange(n_blk, dtype=jnp.int32) * Q_BLOCK
    out = lax.map(one_block, (blocks(q), blocks(q_idx), blocks(w_idx), t0s))
    return out.swapaxes(0, 1).reshape(bsz, L, SA_WIDTH)

def conv_module(u, cv_w, cv_b, ln_w, ln_b):
    f32 = jnp.float32
    dt = u.dtype
    a, b = jnp.split(u, 2, axis=-1)
    h = a * jax.nn.sigmoid(b)
    h = lax.conv_general_dilated(
        h, cv_w[:, None, :], window_strides=(1,),
        padding=[(CV_WIDTH_FILTER - 1, 0)],
        dimension_numbers=('NWC', 'WIO', 'NWC'),
        feature_group_count=CV_WIDTH) + cv_b
    hf = h.astype(f32)
    mu = jnp.mean(hf, axis=-1, keepdims=True)
    var = jnp.mean(jnp.square(hf - mu), axis=-1, keepdims=True)
    hf = (hf - mu) * lax.rsqrt(var + EPS) * ln_w.astype(f32) + ln_b.astype(f32)
    return jax.nn.silu(hf).astype(dt)

def first_inputs(seed: int = 0) -> dict:
    key = jax.random.key(seed)
    ks = jax.random.split(key, 17)
    f32 = jnp.float32
    n = lambda k, shape, s: jax.random.normal(k, shape, f32) * s
    return {
        "x": n(ks[0], (BATCH, SEQ, D_MODEL), 1.0),
        "c": n(ks[1], (BATCH, D_MODEL), 1.0),
        "ada_w": n(ks[2], (DEPTH, D_MODEL, N_MOD * D_MODEL), 0.5 * D_MODEL ** -0.5),
        "ada_b": n(ks[3], (DEPTH, N_MOD * D_MODEL), 0.02),
        "norm_mix_w": 1.0 + n(ks[4], (DEPTH, D_MODEL), 0.05),
        "norm_mlp_w": 1.0 + n(ks[5], (DEPTH, D_MODEL), 0.05),
        "w_in": n(ks[6], (DEPTH, D_MODEL, D_IN), D_MODEL ** -0.5),
        "hg_lb_logits": n(ks[7], (DEPTH, HG_HEADS * HG_DK), 1.0),
        "hg_onorm_w": 1.0 + n(ks[8], (DEPTH, HG_WIDTH), 0.05),
        "cv_w": n(ks[9], (DEPTH, CV_WIDTH_FILTER, CV_WIDTH), CV_WIDTH_FILTER ** -0.5),
        "cv_b": n(ks[10], (DEPTH, CV_WIDTH), 0.02),
        "cv_ln_w": 1.0 + n(ks[11], (DEPTH, CV_WIDTH), 0.05),
        "cv_ln_b": n(ks[12], (DEPTH, CV_WIDTH), 0.02),
        "w_out": n(ks[13], (DEPTH, D_MIX, D_MODEL), D_MIX ** -0.5),
        "mlp_w1": n(ks[14], (DEPTH, D_MODEL, D_FF), D_MODEL ** -0.5),
        "mlp_w2": n(ks[15], (DEPTH, D_FF, D_MODEL), D_FF ** -0.5),
        "final_norm_w": 1.0 + n(ks[16], (D_MODEL,), 0.05),
    }

def first_block(x, c, ada_w, ada_b, norm_mix_w, norm_mlp_w, w_in, hg_lb_logits, hg_onorm_w,
              cv_w, cv_b, cv_ln_w, cv_ln_b, w_out, mlp_w1, mlp_w2, final_norm_w):
    offsets = np.cumsum(IN_SIZES)[:-1].tolist()
    lower_bounds = hgrn2_lower_bounds(hg_lb_logits)
    c_act = jax.nn.silu(c)
    for l in range(DEPTH):
        mod = c_act @ ada_w[l] + ada_b[l]
        sh1, sc1, g1, sh2, sc2, g2 = [m[:, None, :] for m in jnp.split(mod, N_MOD, axis=-1)]

        h = rmsnorm(x, norm_mix_w[l]) * (1.0 + sc1) + sh1
        proj = h @ w_in[l]
        (hq, hf, hi, hg, sq, sk, sv, iq, ik, iw, cu) = jnp.split(proj, offsets, axis=-1)
        o_a = hgrn2_mixer(hq, hf, hi, hg, lower_bounds[l], hg_onorm_w[l])
        o_b = dsa_mixer(sq, sk, sv, iq, ik, iw)
        o_c = conv_module(cu, cv_w[l], cv_b[l], cv_ln_w[l], cv_ln_b[l])
        mix = jnp.concatenate([o_a, o_b, o_c], axis=-1) @ w_out[l]
        x = x + g1 * mix

        h = rmsnorm(x, norm_mlp_w[l]) * (1.0 + sc2) + sh2
        ff = jnp.square(jax.nn.relu(h @ mlp_w1[l])) @ mlp_w2[l]
        x = x + g2 * ff
    return rmsnorm(x, final_norm_w)


DEPTH_2 = 2

N_MIXERS = 2
RMS_EPS = 1e-6
LN_EPS = 1e-5
CHUNK = 128
A_WIDTH = 2 * D_MODEL
A_GROUPS = 8
A_GROUP_DIM = A_WIDTH // A_GROUPS
B_WIDTH = 3 * D_MODEL // 2
B_HEADS = 12
B_HEAD_DIM = B_WIDTH // B_HEADS
CONV_WIDTH = 4
RG_C = 8.0

N_A_LAYERS = (DEPTH_2 + 1) // 2
N_B_LAYERS = DEPTH_2 // 2


def rms_norm(x, w):
    xf = x.astype(jnp.float32)
    y = xf * lax.rsqrt(jnp.mean(xf * xf, axis=-1, keepdims=True) + RMS_EPS)
    return (y * w.astype(jnp.float32)).astype(x.dtype)

def layer_norm(x, w, b):
    xf = x.astype(jnp.float32)
    mu = jnp.mean(xf, axis=-1, keepdims=True)
    var = jnp.mean(jnp.square(xf - mu), axis=-1, keepdims=True)
    y = (xf - mu) * lax.rsqrt(var + LN_EPS)
    return (y * w.astype(jnp.float32) + b.astype(jnp.float32)).astype(x.dtype)

def chunked_sgu_mixer(h, w_in, ln_w, ln_b, w_s, b_s, w_out):
    B, S, _ = h.shape
    z = h @ w_in
    u, v, g = jnp.split(z, 3, axis=-1)
    u = jax.nn.gelu(u)
    v = layer_norm(jax.nn.gelu(v), ln_w, ln_b)
    v = v.reshape(B, S // CHUNK, CHUNK, A_GROUPS, A_GROUP_DIM)
    causal = jnp.tril(jnp.ones((CHUNK, CHUNK), dtype=w_s.dtype))
    w_causal = w_s * causal[None]
    s = jnp.einsum('gts,bnsgc->bntgc', w_causal, v) + b_s.T[None, None, :, :, None]
    y = u * s.reshape(B, S, A_WIDTH) * jax.nn.silu(g)
    return y @ w_out

def _linear_combine(left, right):
    a_l, b_l = left
    a_r, b_r = right
    return a_l * a_r, a_r * b_l + b_r

def rglru_mixer(h, w_in, conv_w, conv_b, gate_a_w, gate_a_b, gate_x_w, gate_x_b, lam, w_out):
    B, S, _ = h.shape
    xb, g = jnp.split(h @ w_in, 2, axis=-1)
    xp = jnp.pad(xb, ((0, 0), (CONV_WIDTH - 1, 0), (0, 0)))
    xc = conv_b + conv_w[CONV_WIDTH - 1] * xp[:, CONV_WIDTH - 1:CONV_WIDTH - 1 + S]
    for k in range(CONV_WIDTH - 1):
        xc = xc + conv_w[k] * xp[:, k:k + S]
    xh = xc.reshape(B, S, B_HEADS, B_HEAD_DIM)
    r = jax.nn.sigmoid(jnp.einsum('bshi,hij->bshj', xh, gate_a_w).reshape(B, S, B_WIDTH) + gate_a_b)
    i = jax.nn.sigmoid(jnp.einsum('bshi,hij->bshj', xh, gate_x_w).reshape(B, S, B_WIDTH) + gate_x_b)
    log_a = -RG_C * r.astype(jnp.float32) * jax.nn.softplus(-lam.astype(jnp.float32))
    a = jnp.exp(log_a)
    mult = jnp.sqrt(-jnp.expm1(2.0 * log_a))
    bterm = mult * (i * xc).astype(jnp.float32)
    _, hseq = lax.associative_scan(_linear_combine, (a, bterm), axis=1)
    y = hseq.astype(h.dtype) * jax.nn.silu(g)
    return y @ w_out

def second_inputs(seed: int = 0) -> dict:
    key = jax.random.key(seed)
    ks = jax.random.split(key, 20)
    f32 = jnp.float32
    x = jax.random.normal(ks[0], (BATCH, SEQ, D_MODEL), f32)
    norm_w = 1.0 + 0.05 * jax.random.normal(ks[1], (DEPTH_2, D_MODEL), f32)
    a_w_in = jax.random.normal(ks[2], (N_A_LAYERS, D_MODEL, 3 * A_WIDTH), f32) * D_MODEL ** -0.5
    a_ln_w = 1.0 + 0.05 * jax.random.normal(ks[3], (N_A_LAYERS, A_WIDTH), f32)
    a_ln_b = 0.02 * jax.random.normal(ks[4], (N_A_LAYERS, A_WIDTH), f32)
    a_w_s = jax.random.normal(ks[5], (N_A_LAYERS, A_GROUPS, CHUNK, CHUNK), f32) * CHUNK ** -0.5
    a_b_s = 1.0 + 0.05 * jax.random.normal(ks[6], (N_A_LAYERS, A_GROUPS, CHUNK), f32)
    a_w_out = jax.random.normal(ks[7], (N_A_LAYERS, A_WIDTH, D_MODEL), f32) * A_WIDTH ** -0.5
    b_w_in = jax.random.normal(ks[8], (N_B_LAYERS, D_MODEL, 2 * B_WIDTH), f32) * D_MODEL ** -0.5
    b_conv_w = jax.random.normal(ks[9], (N_B_LAYERS, CONV_WIDTH, B_WIDTH), f32) * CONV_WIDTH ** -0.5
    b_conv_b = 0.02 * jax.random.normal(ks[10], (N_B_LAYERS, B_WIDTH), f32)
    b_gate_a_w = jax.random.normal(ks[11], (N_B_LAYERS, B_HEADS, B_HEAD_DIM, B_HEAD_DIM), f32) * B_HEAD_DIM ** -0.5
    b_gate_a_b = 0.02 * jax.random.normal(ks[12], (N_B_LAYERS, B_WIDTH), f32)
    b_gate_x_w = jax.random.normal(ks[13], (N_B_LAYERS, B_HEADS, B_HEAD_DIM, B_HEAD_DIM), f32) * B_HEAD_DIM ** -0.5
    b_gate_x_b = 0.02 * jax.random.normal(ks[14], (N_B_LAYERS, B_WIDTH), f32)
    a_c = jax.random.uniform(ks[15], (N_B_LAYERS, B_WIDTH), f32, minval=0.9, maxval=0.999)
    a0 = a_c ** (1.0 / RG_C)
    b_lambda = jnp.log(a0) - jnp.log1p(-a0)
    b_w_out = jax.random.normal(ks[16], (N_B_LAYERS, B_WIDTH, D_MODEL), f32) * B_WIDTH ** -0.5
    norm_f_w = 1.0 + 0.05 * jax.random.normal(ks[17], (D_MODEL,), f32)
    return {
        "x": x, "norm_w": norm_w,
        "a_w_in": a_w_in, "a_ln_w": a_ln_w, "a_ln_b": a_ln_b,
        "a_w_s": a_w_s, "a_b_s": a_b_s, "a_w_out": a_w_out,
        "b_w_in": b_w_in, "b_conv_w": b_conv_w, "b_conv_b": b_conv_b,
        "b_gate_a_w": b_gate_a_w, "b_gate_a_b": b_gate_a_b,
        "b_gate_x_w": b_gate_x_w, "b_gate_x_b": b_gate_x_b,
        "b_lambda": b_lambda, "b_w_out": b_w_out,
        "norm_f_w": norm_f_w,
    }

def second_block(x, norm_w, a_w_in, a_ln_w, a_ln_b, a_w_s, a_b_s, a_w_out,
              b_w_in, b_conv_w, b_conv_b, b_gate_a_w, b_gate_a_b,
              b_gate_x_w, b_gate_x_b, b_lambda, b_w_out, norm_f_w):
    for layer in range(DEPTH_2):
        h = rms_norm(x, norm_w[layer])
        j = layer // N_MIXERS
        if layer % N_MIXERS == 0:
            y = chunked_sgu_mixer(h, a_w_in[j], a_ln_w[j], a_ln_b[j], a_w_s[j], a_b_s[j], a_w_out[j])
        else:
            y = rglru_mixer(h, b_w_in[j], b_conv_w[j], b_conv_b[j], b_gate_a_w[j], b_gate_a_b[j],
                            b_gate_x_w[j], b_gate_x_b[j], b_lambda[j], b_w_out[j])
        x = x + y
    return rms_norm(x, norm_f_w)


def setup_inputs(seed=0):
    out = dict(first_inputs(seed))
    for name, value in second_inputs(seed + 1).items():
        if name != "x":
            out[name + "_2"] = value
    return out


def reference(
    x, c, ada_w, ada_b, norm_mix_w, norm_mlp_w, w_in, hg_lb_logits, hg_onorm_w, cv_w, cv_b,
    cv_ln_w, cv_ln_b, w_out, mlp_w1, mlp_w2, final_norm_w, norm_w_2, a_w_in_2, a_ln_w_2,
    a_ln_b_2, a_w_s_2, a_b_s_2, a_w_out_2, b_w_in_2, b_conv_w_2, b_conv_b_2, b_gate_a_w_2,
    b_gate_a_b_2, b_gate_x_w_2, b_gate_x_b_2, b_lambda_2, b_w_out_2, norm_f_w_2,
):
    x = first_block(
        x, c, ada_w, ada_b, norm_mix_w, norm_mlp_w, w_in, hg_lb_logits, hg_onorm_w, cv_w, cv_b,
        cv_ln_w, cv_ln_b, w_out, mlp_w1, mlp_w2, final_norm_w,
    )
    return second_block(
        x, norm_w_2, a_w_in_2, a_ln_w_2, a_ln_b_2, a_w_s_2, a_b_s_2, a_w_out_2, b_w_in_2,
        b_conv_w_2, b_conv_b_2, b_gate_a_w_2, b_gate_a_b_2, b_gate_x_w_2, b_gate_x_b_2,
        b_lambda_2, b_w_out_2, norm_f_w_2,
    )


_drawn_inputs = setup_inputs


def setup_inputs(seed=0):
    import zlib

    import numpy as np

    out = dict(_drawn_inputs(seed))
    spreads = {}
    factors = {'norm_mix_w': 4.0,
     'hg_onorm_w': 6.915,
     'cv_b': 23.832,
     'cv_ln_w': 30.001,
     'cv_ln_b': 64.0,
     'a_ln_w_2': 4.4,
     'a_ln_b_2': 8.0,
     'a_b_s_2': 3.26,
     'b_gate_a_b_2': 62.244,
     'b_gate_x_b_2': 31.39,
     'norm_mlp_w': 6.442}
    for name, (base, spread) in spreads.items():
        noise = np.random.default_rng([zlib.crc32(name.encode()), seed]).standard_normal(out[name].shape)
        drawn = base * np.exp(spread * noise) if base else spread * noise
        out[name] = __import__('jax').numpy.asarray(drawn.astype(out[name].dtype))
    for name, factor in factors.items():
        out[name] = (out[name] * factor).astype(out[name].dtype)
    return out
```

```python
from contextlib import ExitStack

import concourse.bass as bass
from concourse import mybir

P = 128
ALU = mybir.AluOpType
ACT = mybir.ActivationFunctionType
F32 = mybir.dt.float32
F32R = mybir.dt.float32r
I32 = mybir.dt.int32
AX_X = mybir.AxisListType.X

TOK = 512
D = 1024
KT = D // P
TT = TOK // P
HG_HEADS, HG_D = 4, 128
SA_HEADS, SA_D = 4, 64
IDX_HEADS, IDX_D = 8, 32
TOPK = 128
CV, TAPS = 256, 31
CVT = CV // P
D_FF = 4096
A_WIDTH, A_GROUPS = 2048, 8
AT = A_WIDTH // P
B_WIDTH, B_HEADS, B_TAPS = 1536, 12, 4
EPS, LN_EPS, RG_C = 1e-6, 1e-5, 8.0
NEG_BIG, TINY, TAKEN = -1e30, 1e-30, -3e38
GELU_C, GELU_A = 0.7978845608028654, 0.044715

C_HQ, C_HF, C_HI, C_HG = 0, 512, 1024, 1536
C_SQ, C_SK, C_SV, C_IQ, C_IK, C_IW, C_CU = 2048, 2304, 2560, 2816, 3072, 3104, 3112

RING = 4
LEAD = 3
UNIT = 1024


def ada_unit(group, kt):
    return ("ada", group, kt)


W_IN_UNITS = (
    [("fm", C_IQ), ("fm", C_IQ + P), ("ik", C_IK), ("iw", C_IW)]
    + [("fm", C_CU + P * m + CV * s) for m in range(CVT) for s in range(2)]
    + [("fm", C_SK), ("fm", C_SK + P), ("fm", C_SQ), ("fm", C_SQ + P)]
    + [("tm4", C_SV, kq) for kq in range(2)]
    + [("fm", C_HQ + P * h) for h in range(HG_HEADS)]
    + [("fm", C_HF + P * h) for h in range(HG_HEADS)]
    + [("tm2", C_HI, kp) for kp in range(4)]
    + [("fm", C_HG + P * h) for h in range(HG_HEADS)]
)
N_IN = len(W_IN_UNITS)


def first_stream():
    stream = [ada_unit(1, k) for k in range(KT)] + [ada_unit(0, k) for k in range(KT)]
    later = [ada_unit(g, k) for g in (2, 4, 3, 5) for k in range(KT)]
    for u in range(N_IN):
        stream.append(("w", u))
        for _ in range(2 if u in (3, 4, 5, 6, 7, 8) else 1):
            if u >= 0 and u < N_IN - RING and later:
                stream.append(later.pop(0))
    assert not later
    return stream


STREAM = first_stream()
N_ADA = 6 * KT
assert len(STREAM) == N_IN + N_ADA and N_ADA % RING == 0

U_OUT = N_IN
U_FF = U_OUT + KT
U_V = U_FF + 64
U_UG = U_V + 16
U_B = U_UG + 48
U_BOUT = U_B + 2 * B_HEADS
U_END = U_BOUT + 16

H_MIX, H_OMIX, H_FF, H_HID, H_SGU, H_Y, H_RG, H_YB = 0, 8, 16, 24, 56, 64, 80, 88
X_OUT, X_FF, X_FIN, X_AO, X_BO = 8, 16, 32, 40, 56
Q_OUT, Q_FF, Q_FIN, Q_AO, Q_BO = 8, 16, 24, 32, 40
E_FF, E_V, E_RG = 32, 64, 80
S_FF, S_SGU, S_RG = 8, 16, 24

PARAMS = [
    ("ada_b", 48), ("norm_mix_w", 8), ("norm_mlp_w", 8), ("final_norm_w", 8), ("hg_lb_logits", 4),
    ("hg_onorm_w", 4), ("cv_b", 2), ("cv_ln_w", 2), ("cv_ln_b", 2), ("b_lambda_2", 12), ("norm_f_w_2", 8),
    ("norm_w_2", 16), ("pad0", 6),
    ("cv_w", 62), ("a_ln_w_2", 16), ("a_ln_b_2", 16), ("b_conv_b_2", 12), ("b_gate_a_b_2", 12), ("pad1", 10),
    ("b_gate_x_b_2", 12), ("b_conv_w_2", 48),
]
PCOL = {}
_n = 0
for _name, _rows in PARAMS:
    PCOL[_name] = _n
    _n += _rows
P_TILES = 3
PAR_DMAS = sum(not n.startswith("pad") for n, _ in PARAMS)

U_IK = W_IN_UNITS.index(("ik", C_IK))
U_Q = W_IN_UNITS.index(("fm", C_HQ))
MOD_STEPS = (7, 11, 19, 27)
ATT_STEPS = {14: [0], 15: [1], 16: [2], 17: [3], 22: [4, 5], 23: [6, 7], 24: [8, 9], 25: [10, 11], 26: [12],
             27: [13, 14], 28: [15, 16], 29: [17]}
OMIX_ORDER = (6, 7, 4, 5, 0, 1, 2, 3)
V0 = 2
assert PCOL["cv_w"] == P and PCOL["b_gate_x_b_2"] == 2 * P


class Chain:

    def __init__(self, eng, sem):
        self.eng, self.sem, self.n = eng, sem, 0

    def step(self, ins):
        ins.then_inc(self.sem, 1)
        self.n = self.n + 1
        return self.n

    def wait(self, value=None):
        self.eng.wait_ge(self.sem, self.n if value is None else value)

    def link(self, ins):
        self.step(ins)
        self.wait()

    def loop(self, i, start, steps, first=0):
        self.n = start + (i - first) * steps if first else start + i * steps


def build(nc, a, out):
    with ExitStack() as ctx:
        def sb(name, shape, dt=F32, where=ctx):
            return where.enter_context(nc.sbuf_tensor(name, shape, dt))

        def sem(name):
            return ctx.enter_context(nc.semaphore(name))

        banks = ctx.enter_context(nc.psum_tensor("banks", [P, 8, TOK], F32))

        xT = sb("xT", [P, KT, TOK])
        h_hi = sb("h_hi", [P, KT, TOK], F32R)
        h_lo = sb("h_lo", [P, KT, TOK], F32R)
        raw = sb("raw", [P, RING, UNIT])
        w_hi = sb("w_hi", [P, RING, UNIT], F32R)
        w_lo = sb("w_lo", [P, RING, UNIT], F32R)
        par = sb("par", [P, P_TILES * P])
        mod = sb("mod", [P, 6 * KT])
        ident = sb("ident", [P, P])
        ones_d = sb("ones_d", [P, P])
        ones1 = sb("ones1", [P, P])
        cT = sb("cT", [P, KT])
        c_act = sb("c_act", [P, KT])
        scale1 = sb("scale1", [P, KT])
        scale2 = sb("scale2", [P, KT])
        ssq = sb("ssq", [P, TOK])
        sqb = sb("sqb", [P, 2, TOK])
        rstd = sb("rstd", [P, TOK])
        eps_c = sb("eps_c", [P, 2])

        def pcol(name, n=0, count=1):
            return par[:, PCOL[name] + n:PCOL[name] + n + count]

        mix = ctx.enter_context(ExitStack())
        omix = sb("omix", [P, KT, TOK], F32, mix)
        masks = sb("masks", [P, 7, P], F32, mix)
        ones_m = sb("ones_m", [P, 2, P], F32, mix)
        hf = sb("hf", [P, HG_HEADS, TOK], F32, mix)
        hq = sb("hq", [P, HG_HEADS, TOK], F32, mix)
        hk = sb("hk", [P, HG_HEADS, TOK], F32, mix)
        hv = sb("hv", [P, TT, HG_HEADS * HG_D], F32, mix)
        iw = sb("iw", [P, TT, IDX_HEADS], F32, mix)
        lbt = sb("lbt", [P, 4, HG_HEADS], F32, mix)
        col = sb("col", [P, 8], F32, mix)
        m8 = sb("m8", [P, 3, 8], F32, mix)
        start = ExitStack()
        x_tok = sb("x_tok", [P, TT, D], F32, start)
        acc1 = sb("acc1", [P, 2, UNIT], F32, start)
        par_rows = sb("par_rows", [P, P_TILES, P], F32, start)
        start.close()
        dsa = ExitStack()
        hpad = sb("hpad", [P, CVT, TAPS - 1 + TOK], F32, dsa)
        cacc = sb("cacc", [P, CVT, TOK], F32, dsa)
        acc2 = sb("acc2", [P, 2, UNIT], F32, dsa)
        iqT = sb("iqT", [P, 2, TOK], F32, dsa)
        ikT = sb("ikT", [P, TOK], F32, dsa)
        sqT = sb("sqT", [P, 2, TOK], F32, dsa)
        skT = sb("skT", [P, 2, TOK], F32, dsa)
        sv = sb("sv", [P, TT, SA_HEADS * SA_D], F32, dsa)
        score = [sb(f"score{b}", [P, P * (b + 1)], F32, dsa) for b in range(TT)]
        ring2 = sb("ring2", [P, 2, TOK], F32, dsa)
        pT = sb("pT", [P, 2, TOK], F32, dsa)
        dsa.close()
        hg = ExitStack()
        hgt = sb("hgt", [P, HG_HEADS, TOK - 4], F32, hg)
        hA = sb("hA", [P, HG_HEADS, TT, P], F32, hg)
        hKT = sb("hKT", [P, 2, HG_HEADS, P], F32, hg)
        hS = sb("hS", [P, 3, HG_HEADS, P], F32, hg)
        hg.close()
        mix.close()
        ff = ExitStack()
        hid_hi = sb("hid_hi", [P, 16, TOK], F32R, ff)
        hid_lo = sb("hid_lo", [P, 16, TOK], F32R, ff)
        relu = sb("relu", [P, 2, TOK], F32, ff)
        relu2 = sb("relu2", [P, 2, TOK], F32, ff)
        ff.close()
        sg = ExitStack()
        y_hi = sb("y_hi", [P, 8, TOK], F32R, sg)
        y_lo = sb("y_lo", [P, 8, TOK], F32R, sg)
        vt = sb("vt", [P, TT, A_WIDTH], F32, sg)
        vh = sb("vh", [P, 2, TT, P], F32, sg)
        ws = sb("ws", [P, A_GROUPS, P], F32, sg)
        wcT = sb("wcT", [P, A_GROUPS, P], F32, sg)
        wsum = sb("wsum", [P, A_GROUPS, P], F32, sg)
        bsp = sb("bsp", [P, A_GROUPS, P], F32, sg)
        e0 = sb("e0", [P, 2, TOK], F32, sg)
        e1 = sb("e1", [P, 2, TOK], F32, sg)
        e2 = sb("e2", [P, 2, TOK], F32, sg)
        eb = sb("eb", [P, 2, P], F32, sg)
        vst = sb("vst", [P, TT, 4, 6], F32, sg)
        vmv = sb("vmv", [P, TT, 2], F32, sg)
        vrs = sb("vrs", [P, TT], F32, sg)
        lnw2 = sb("lnw2", [P, AT], F32, sg)
        sg.close()
        rg = ExitStack()
        yb_hi = sb("yb_hi", [P, B_HEADS, TOK], F32R, rg)
        yb_lo = sb("yb_lo", [P, B_HEADS, TOK], F32R, rg)
        xbp = sb("xbp", [P, 2, B_TAPS + TOK], F32, rg)
        gw = sb("gw", [P, 2, 2, P], F32, rg)
        xc, t_r, t_i, t_sg, t_g, t_a, t_s, t_b = [sb(n, [P, 2, TOK], F32, rg) for n in
                                                  ("xc", "t_r", "t_i", "t_sg", "t_g", "t_a", "t_s", "t_b")]
        spt = sb("spt", [P, 5, B_HEADS], F32, rg)
        rg.close()
        y_tok = sb("y_tok", [P, TT, D])

        raw_in = [sem(f"raw_in{i}") for i in range(RING)]
        split_hi = sem("split_hi")
        split_lo = sem("split_lo")
        w_used = sem("w_used")
        evac = sem("evac")
        x_new = sem("x_new")
        h_scaled = sem("h_scaled")
        h_hi_made = sem("h_hi_made")
        h_ready = sem("h_ready")
        sq_made, sq_added = sem("sq_made"), sem("sq_added")
        stat_made, root_made = sem("stat_made"), sem("root_made")
        ada_dve = sem("ada_dve")
        mod_summed, mod_ready = sem("mod_summed"), sem("mod_ready")
        s_dve, s_act, s_pool = sem("s_dve"), sem("s_act"), sem("s_pool")
        c_in, x_in, par_in, consts = sem("c_in"), sem("x_in"), sem("par_in"), sem("consts")
        c_sig, c_ready, par_turned, par_ready = sem("c_sig"), sem("c_ready"), sem("par_turned"), sem("par_ready")
        x_turned, lb_zero, lb_exp = sem("x_turned"), sem("lb_zero"), sem("lb_exp")
        s_made, s_read, score_added = sem("s_made"), sem("s_read"), sem("score_added")
        diag_made, taken_made, bias_made = sem("diag_made"), sem("taken_made"), sem("bias_made")
        l_made, l_read, mx_made, e_made = sem("l_made"), sem("l_read"), sem("mx_made"), sem("e_made")
        p_made, p_turned, pt_read = sem("p_made"), sem("p_turned"), sem("pt_read")
        pv_made, ob_made, oc_made, oa_made = sem("pv_made"), sem("ob_made"), sem("oc_made"), sem("oa_made")
        weighted, tapped, mean_made, cen_made = sem("weighted"), sem("tapped"), sem("mean_made"), sem("cen_made")
        csq_made, var_made, croot_made = sem("csq_made"), sem("var_made"), sem("croot_made")
        cn_made, csig_made = sem("cn_made"), sem("csig_made")
        q_made, g_made, f_made = sem("q_made"), sem("g_made"), sem("f_made")
        lev_made, upd_made = sem("lev_made"), sem("upd_made")
        kt_turned, kt_made, sp_made, st_made = sem("kt_turned"), sem("kt_made"), sem("sp_made"), sem("st_made")
        o_made, osq_made, om_made, oroot_made = sem("o_made"), sem("osq_made"), sem("om_made"), sem("oroot_made")

        ssq_zero, relu_sq, v_gelu, wsum_made = sem("ssq_zero"), sem("relu_sq"), sem("v_gelu"), sem("wsum_made")
        u_aff, u_gelu, eb_made, s_mixed = sem("u_aff"), sem("u_gelu"), sem("eb_made"), sem("s_mixed")
        tap_made, a1_made, a_made, mult_made = sem("tap_made"), sem("a1_made"), sem("a_made"), sem("mult_made")
        bt_made, scanned = sem("bt_made"), sem("scanned")

        bs_in, ws_in, ws_turned, ws_copied = sem("bs_in"), sem("ws_in"), sem("ws_turned"), sem("ws_copied")
        ws_masked, ws_summed = sem("ws_masked"), sem("ws_summed")
        v_copied, v_aff, v_inner, v_tanh, v_stat = sem("v_copied"), sem("v_aff"), sem("v_inner"), sem("v_tanh"), sem("v_stat")
        v_var, v_root, vh_made, mixed = sem("v_var"), sem("v_root"), sem("vh_made"), sem("mixed")
        u_sq, u_inner, u_tanh, g_sig = sem("u_sq"), sem("u_inner"), sem("u_tanh"), sem("g_sig")
        ug_made, ugp_made, y_out = sem("ug_made"), sem("ugp_made"), sem("y_out")
        gw_in, gates_made, xc_made = [sem("gw_in0"), sem("gw_in1")], sem("gates_made"), sem("xc_made")
        sp_abs, sp_exp, sp_ready = sem("sp_abs"), sem("sp_exp"), sem("sp_ready")
        pad_zero, rt_made, ra_made, rs_made = sem("pad_zero"), sem("rt_made"), sem("ra_made"), sem("rs_made")
        ix_made, gg_made, bt_in, yb_out = sem("ix_made"), sem("gg_made"), sem("bt_in"), sem("yb_out")
        fin_scaled, fin_turned, y_made, out_done = sem("fin_scaled"), sem("fin_turned"), sem("y_made"), sem("out_done")

        arrival = {item: d for d, item in enumerate(STREAM)}

        def raw_index(u):
            return arrival[("w", u)] if u < N_IN else u + N_ADA

        def raw_wait(eng, d):
            eng.wait_ge(raw_in[d % RING], 16 * (d // RING + 1))

        def copies(slot):
            return slot.rearrange("p (k r n) -> p k r n", r=4, n=IDX_D)

        def four_times(slot):
            return slot[:, 0:KT * IDX_D].rearrange("p (k n) -> p k n", n=IDX_D).unsqueeze(2).broadcast_to([P, KT, 4, IDX_D])

        def hi_unit(act, u, i=0):
            d = raw_index(u)
            act.wait_ge(raw_in[d % RING], 16 * (d // RING + 1) + 16 * i)
            if u >= RING:
                act.wait_ge(w_used, u - RING + 1 + RING * i)
            src, dst = raw[:, d % RING, :], w_hi[:, u % RING, :]
            if u == U_IK:
                src, dst = four_times(src), copies(dst)
            act.activation(dst, src, ACT.Copy).then_inc(split_hi, 1)

        def lo_unit(dve, u, i=0):
            d = raw_index(u)
            dve.wait_ge(split_hi, u + 1 + RING * i)
            src, hi, dst = raw[:, d % RING, :], w_hi[:, u % RING, :].bitcast(F32), w_lo[:, u % RING, :]
            if u == U_IK:
                src, hi, dst = four_times(src), copies(hi), copies(dst)
            dve.tensor_tensor(dst, src, hi, ALU.subtract).then_inc(split_lo, 1)

        def unit(ring, u, n):
            return ring[:, u % RING, :].rearrange("p (k n) -> p k n", n=n)

        def three(pe, dst, l_hi, l_lo, r_hi, r_lo, first, last):
            pe.matmul(dst, l_hi, r_hi, start=first, stop=False)
            pe.matmul(dst, l_hi, r_lo, start=False, stop=False)
            return pe.matmul(dst, l_lo, r_hi, start=False, stop=last)

        LEVELS = [1, 2, 4, 8, 16, 32, 64]
        T_OFF = {2: 0, 4: 256, 8: 384, 16: 448, 32: 480, 64: 496, 128: 504}

        def t_level(b, p):
            if b == 1:
                v = hf[:, 2 * p:2 * p + 2, :]
            else:
                v = hgt[:, 2 * p:2 * p + 2, T_OFF[b]:T_OFF[b] + TOK // b]
            return v.rearrange("p h (n two) -> p h n two", two=2)

        def halves(buf, b, p):
            return buf[:, 2 * p:2 * p + 2, :].rearrange("p h (n two b) -> p h n two b", two=2, b=b)

        block = ctx.enter_context(nc.Block())

        @block.sync
        def _(sp):
            w_in = a["w_in"][0]
            for d, item in enumerate(STREAM):
                if d >= RING:
                    before = STREAM[d - RING]
                    if before[0] == "w":
                        sp.wait_ge(split_lo, before[1] + 1)
                    else:
                        sp.wait_ge(ada_dve, sum(x[0] == "ada" for x in STREAM[:d - RING + 1]))
                dst = raw[:, d % RING, :]
                if item[0] == "ada":
                    _, g, kt = item
                    src = a["ada_w"][0, kt * P:(kt + 1) * P, g * D:(g + 1) * D]
                else:
                    kind = W_IN_UNITS[item[1]]
                    c = kind[1]
                    if kind[0] == "fm":
                        dst = dst.rearrange("p (k n) -> p k n", n=P)
                        src = w_in[:, c:c + P].rearrange("(k p) n -> p k n", p=P)
                    elif kind[0] == "ik":
                        dst = dst[:, 0:KT * IDX_D].rearrange("p (k n) -> p k n", n=IDX_D)
                        src = w_in[:, c:c + IDX_D].rearrange("(k p) n -> p k n", p=P)
                    elif kind[0] == "iw":
                        dst = dst[:, 0:KT * IDX_HEADS].rearrange("p (k n) -> p k n", n=IDX_HEADS)
                        src = w_in[:, c:c + IDX_HEADS].rearrange("(k p) n -> p k n", p=P)
                    elif kind[0] == "tm4":
                        dst = dst.rearrange("p (k n) -> p k n", n=256)
                        src = w_in[4 * P * kind[2]:4 * P * (kind[2] + 1), c:c + 256].rearrange("(k p) n -> p k n", p=P)
                    else:
                        dst = dst.rearrange("p (k n) -> p k n", n=512)
                        src = w_in[2 * P * kind[2]:2 * P * (kind[2] + 1), c:c + 512].rearrange("(k p) n -> p k n", p=P)
                sp.dma_start(dst, src).then_inc(raw_in[d % RING], 16)

            def stream(base, count, source):
                with sp.Fori(0, count // RING) as i:
                    for j in range(RING):
                        u = base + j
                        sp.wait_ge(split_lo, u - RING + 1 + RING * i)
                        src, n = source(i, j)
                        kt = src.shape[1]
                        sp.dma_start(raw[:, u % RING, 0:kt * n].rearrange("p (k n) -> p k n", n=n), src)\
                          .then_inc(raw_in[u % RING], 16)

            def rows(w, r0, r1):
                return w[r0:r1, :].rearrange("(k p) n -> p k n", p=P)

            stream(U_OUT, KT, lambda i, j: (rows(a["w_out"][0], 0, D)[:, :, bass.ds(i * 4 * P + j * P, P)], P))
            w1, w2 = a["mlp_w1"][0], a["mlp_w2"][0]
            for half in range(2):
                stream(U_FF + 32 * half, 16,
                       lambda i, j: (rows(w1, 0, D)[:, :, bass.ds(i * 4 * P + (16 * half + j) * P, P)], P))
                stream(U_FF + 32 * half + 16, 16,
                       lambda i, j: (rows(w2, (16 * half + 8 * (j % 2)) * P, (16 * half + 8 * (j % 2) + 8) * P)
                                     [:, :, bass.ds(i * 2 * P + (j // 2) * P, P)], P))
            wa = a["a_w_in_2"][0]
            stream(U_V, 16, lambda i, j: (rows(wa, 2 * P * j, 2 * P * (j + 1))[:, :, bass.ds(i * 512 + A_WIDTH, 512)], 512))
            wo = a["a_w_out_2"][0]
            for half in range(2):
                stream(U_UG + 24 * half, 16,
                       lambda i, j: (rows(wa, 0, D)[:, :, bass.ds(i * 2 * P + (8 * half + j // 2) * P
                                                                   + 2 * A_WIDTH * (j % 2), P)], P))
                stream(U_UG + 24 * half + 16, 8,
                       lambda i, j: (rows(wo, half * D, (half + 1) * D)[:, :, bass.ds(i * 4 * P + j * P, P)], P))
            wb = a["b_w_in_2"][0]
            stream(U_B, 2 * B_HEADS, lambda i, j: (rows(wb, 0, D)[:, :, bass.ds(i * 2 * P + (j // 2) * P + B_WIDTH * (j % 2), P)], P))
            wbo = a["b_w_out_2"][0]
            stream(U_BOUT, 16, lambda i, j: (rows(wbo, 6 * (j % 2) * P, (6 * (j % 2) + 6) * P)
                                             [:, :, bass.ds(i * 2 * P + (j // 2) * P, P)], P))
            for t in range(TT):
                sp.wait_ge(y_made, TT + t + 1)
                sp.dma_start(out[0, t * P:(t + 1) * P, :], y_tok[:, t, :]).then_inc(out_done, 16)
            sp.wait_ge(out_done, 16 * TT)

        @block.tensor
        def _(pe):
            pe.wait_ge(consts, 1)
            pe.wait_ge(par_in, PAR_DMAS * 16)
            for t in range(P_TILES):
                last = pe.transpose(banks[:, 4, t * P:(t + 1) * P], par_rows[:, t, :], ident[:, :])
            last.then_inc(par_turned, 1)
            pe.wait_ge(x_in, 16 * TT)
            for m in range(KT):
                if m >= 4:
                    pe.wait_ge(x_new, m - 3)
                for t in range(TT):
                    last = pe.transpose(banks[:, m % 4, t * P:(t + 1) * P], x_tok[:, t, m * P:(m + 1) * P], ident[:, :])
                last.then_inc(x_turned, 1)

            def stat(n, q):
                pe.wait_ge(sq_added, q)
                pe.matmul(banks[:, 7, :], ones_d[:, :], ssq[:, :], start=True, stop=True).then_inc(stat_made, 1)

            stat(1, 8)

            def mod_sums(acc, n):
                for j in range(KT):
                    last = pe.matmul(banks[:, 6 if n < 2 else 7, j:j + 1], acc[:, j * P:(j + 1) * P], ones1[:, 0:1],
                                     start=True, stop=True)
                last.then_inc(mod_summed, 1)

            pe.wait_ge(ada_dve, KT)
            mod_sums(acc1[:, 0, :], 0)
            pe.wait_ge(ada_dve, 2 * KT)
            pe.wait_ge(mod_ready, 1)
            mod_sums(acc1[:, 1, :], 1)

            n_out, summed, turned_out = [0], [2], [0]

            def free_banks(n):
                if n >= 4:
                    pe.wait_ge(evac, n - 3)

            def in_unit(u):
                kind = W_IN_UNITS[u]
                pe.wait_ge(split_lo, u + 1)
                n = n_out[0]
                if kind[0] in ("fm", "ik"):
                    free_banks(n)
                    for k in range(KT):
                        if u == 0:
                            pe.wait_ge(h_ready, H_MIX + k + 1)
                        last = three(pe, banks[:, n % 4, :], unit(w_hi, u, P)[:, k, :], unit(w_lo, u, P)[:, k, :],
                                     h_hi[:, k, :], h_lo[:, k, :], k == 0, k == KT - 1)
                    n_out[0] += 1
                elif kind[0] == "iw":
                    free_banks(n)
                    for t in range(TT):
                        for k in range(KT):
                            c0, c1 = k * IDX_HEADS, (k + 1) * IDX_HEADS
                            last = three(pe, banks[:, n % 4, t * IDX_HEADS:(t + 1) * IDX_HEADS],
                                         h_hi[:, k, t * P:(t + 1) * P], h_lo[:, k, t * P:(t + 1) * P],
                                         w_hi[:, u % RING, c0:c1], w_lo[:, u % RING, c0:c1], k == 0, k == KT - 1)
                    n_out[0] += 1
                else:
                    per, width = (4, 256) if kind[0] == "tm4" else (2, 512)
                    part = kind[2]
                    if part == 0:
                        free_banks(n + 3)
                    for t in range(TT):
                        for kk in range(per):
                            k = per * part + kk
                            last = three(pe, banks[:, t, 0:width],
                                         h_hi[:, k, t * P:(t + 1) * P], h_lo[:, k, t * P:(t + 1) * P],
                                         unit(w_hi, u, width)[:, kk, :], unit(w_lo, u, width)[:, kk, :],
                                         k == 0, k == KT - 1)
                    if part == KT // per - 1:
                        n_out[0] += 4
                last.then_inc(w_used, 1)

            def index_scores():
                pe.wait_ge(evac, 4)
                for s in range(3 * IDX_HEADS):
                    b, h = 1 + s // IDX_HEADS, s % IDX_HEADS
                    if s >= 2:
                        pe.wait_ge(s_read, s - 1)
                    r = slice(IDX_D * (h % 4), IDX_D * (h % 4) + IDX_D)
                    pe.matmul(banks[:, 4 + s % 2, 0:P * (b + 1)], iqT[r, h // 4, b * P:(b + 1) * P],
                              ikT[r, 0:P * (b + 1)], start=True, stop=True).then_inc(s_made, 1)

            def logits(t):
                b, h = t // SA_HEADS, t % SA_HEADS
                if t == 0:
                    pe.wait_ge(evac, 16)
                    pe.wait_ge(s_read, 3 * IDX_HEADS)
                if t >= 2:
                    pe.wait_ge(l_read, t - 1)
                r = slice(SA_D * (h % 2), SA_D * (h % 2) + SA_D)
                pe.matmul(banks[:, 4 + t % 2, 0:P * (b + 1)], sqT[r, h // 2, b * P:(b + 1) * P],
                          skT[r, h // 2, 0:P * (b + 1)], start=True, stop=True).then_inc(l_made, 1)

            def turn_probs(t):
                b = t // SA_HEADS
                pe.wait_ge(p_made, t + 1)
                if t >= 1:
                    pe.wait_ge(pt_read, t)
                for kb in range(b + 1):
                    last = pe.transpose(banks[:, 6, kb * P:(kb + 1) * P], ring2[:, t % 2, kb * P:(kb + 1) * P], ident[:, :])
                last.then_inc(p_turned, 1)

            def probs_v(t):
                b, h = t // SA_HEADS, t % SA_HEADS
                pe.wait_ge(pt_read, t + 1)
                pe.wait_ge(mod_ready, summed[0])
                if t:
                    pe.wait_ge(ob_made, t)
                turned_out[0] = t + 1
                r = slice(SA_D * (h % 2), SA_D * (h % 2) + SA_D)
                for kb in range(b + 1):
                    last = pe.matmul(banks[r, 7, 0:P], sv[:, kb, h * SA_D:(h + 1) * SA_D], pT[:, t % 2, kb * P:(kb + 1) * P],
                                     start=(kb == 0), stop=(kb == b))
                last.then_inc(pv_made, 1)

            def attention(t):
                if t < 16:
                    logits(t)
                if 1 <= t <= 16:
                    turn_probs(t - 1)
                if 2 <= t <= 17:
                    probs_v(t - 2)

            for u in range(N_IN):
                in_unit(u)
                if u == 4:
                    index_scores()
                if u in MOD_STEPS:
                    n = MOD_STEPS.index(u)
                    pe.wait_ge(ada_dve, KT * (n + 3))
                    pe.wait_ge(mod_ready, 2 + n)
                    if turned_out[0]:
                        pe.wait_ge(ob_made, turned_out[0])
                    summed[0] = 3 + n
                    mod_sums(acc2[:, n % 2, :], 2 + n)
                for t in ATT_STEPS.get(u, []):
                    attention(t)
            pe.wait_ge(tapped, CVT * TAPS)
            pe.wait_ge(ob_made, 16)
            for m in range(CVT):
                last = pe.matmul(banks[:, 7, :], ones_m[:, 1, :], cacc[:, m, :], start=(m == 0), stop=(m == CVT - 1))
            last.then_inc(mean_made, 1)
            pe.wait_ge(csq_made, CVT)
            for m in range(CVT):
                last = pe.matmul(banks[:, 7, :], ones_m[:, 1, :], hpad[:, m, 0:TOK], start=(m == 0), stop=(m == CVT - 1))
            last.then_inc(var_made, 1)

            pe.wait_ge(f_made, HG_HEADS)
            pe.wait_ge(q_made, HG_HEADS)
            pe.wait_ge(oc_made, CVT)
            for l in range(8):
                for p in range(2):
                    n = 2 * l + p
                    if l:
                        pe.wait_ge(upd_made, n - 1)
                    for h in (2 * p, 2 * p + 1):
                        for c in range(TT):
                            last = pe.matmul(banks[:, 4 + h, c * P:(c + 1) * P], hk[:, h, c * P:(c + 1) * P],
                                             hq[:, h, c * P:(c + 1) * P], start=True, stop=True)
                    last.then_inc(lev_made, 1)
            pe.wait_ge(upd_made, 16)
            for c in range(3):
                if c:
                    pe.wait_ge(kt_made, c)
                for h in range(HG_HEADS):
                    last = pe.transpose(banks[:, 4, h * P:(h + 1) * P], hk[:, h, c * P:(c + 1) * P], ident[:, :])
                last.then_inc(kt_turned, 1)
                pe.wait_ge(kt_made, c + 1)
                if c:
                    pe.wait_ge(st_made, c)
                for h in range(HG_HEADS):
                    last = pe.matmul(banks[:, 6, h * P:(h + 1) * P], hKT[:, c % 2, h, :], hv[:, c, h * P:(h + 1) * P],
                                     start=True, stop=True)
                last.then_inc(sp_made, 1)
            pe.wait_ge(evac, 32)
            pe.wait_ge(st_made, 3)
            for h in range(HG_HEADS):
                for c in range(TT):
                    o = banks[:, h, c * P:(c + 1) * P]
                    last = pe.matmul(o, hv[:, c, h * P:(h + 1) * P], hA[:, h, c, :], start=True, stop=(c == 0))
                    if c:
                        last = pe.matmul(o, hS[:, c - 1, h, :], hq[:, h, c * P:(c + 1) * P], start=False, stop=True)
                last.then_inc(o_made, 1)
            for h in range(HG_HEADS):
                pe.wait_ge(osq_made, h + 1)
                pe.matmul(banks[:, 4 + h, :], ones_m[:, 0, :], hf[:, h, :], start=True, stop=True).then_inc(om_made, 1)

            def residual_product(i, base, units, nk, src_hi, src_lo, x0):
                for j in range(RING):
                    u = base + j
                    t = j // units
                    pe.wait_ge(split_lo, u + 1 + RING * i)
                    if j % units == 0:
                        pe.wait_ge(x_new, x0 + t - 1 + (RING // units) * i)
                    for k in range(nk):
                        kk = (j % units) * nk + k
                        last = three(pe, banks[:, t, :], unit(w_hi, u, P)[:, k, :], unit(w_lo, u, P)[:, k, :],
                                     src_hi[:, kk, :], src_lo[:, kk, :], kk == 0, kk == units * nk - 1)
                    last.then_inc(w_used, 1)

            def residual(base, count, *rest):
                with pe.Fori(0, count // RING) as i:
                    residual_product(i, base, *rest)

            pe.wait_ge(h_ready, H_OMIX + KT)
            pe.wait_ge(oa_made, HG_HEADS)
            residual(U_OUT, KT, 1, KT, h_hi, h_lo, X_OUT)
            stat(2, Q_OUT + KT)

            for half in range(2):
                pe.wait_ge(h_ready, H_FF + KT)
                pe.wait_ge(x_new, X_FF + KT * half)
                with pe.Fori(0, 4) as i:
                    for j in range(RING):
                        u = U_FF + 32 * half + j
                        pe.wait_ge(split_lo, u + 1 + RING * i)
                        pe.wait_ge(evac, E_FF + 16 * half + j - 1 + RING * i)
                        for k in range(KT):
                            last = three(pe, banks[:, j, :], unit(w_hi, u, P)[:, k, :], unit(w_lo, u, P)[:, k, :],
                                         h_hi[:, k, :], h_lo[:, k, :], k == 0, k == KT - 1)
                        last.then_inc(w_used, 1)
                pe.wait_ge(h_ready, H_HID + 16 * (half + 1))
                pe.wait_ge(evac, E_FF + 16 * (half + 1))
                residual(U_FF + 32 * half + 16, 16, 2, KT, hid_hi, hid_lo, X_FF + KT * half)
            stat(3, Q_FF + KT)
            stat(4, Q_FIN + KT)

            pe.wait_ge(ws_in, 16)
            for g in range(A_GROUPS):
                last = pe.transpose(banks[:, 4 + g // 4, (g % 4) * P:(g % 4 + 1) * P], ws[:, g, :], ident[:, :])
            last.then_inc(ws_turned, 1)
            pe.wait_ge(ws_masked, 1)
            for g in range(2):
                last = pe.matmul(banks[:, 4 + g, :], ones1[:, :], wcT[:, 4 * g:4 * g + 4, :].rearrange("p g t -> p (g t)"),
                                 start=True, stop=True)
            last.then_inc(ws_summed, 1)
            pe.wait_ge(h_ready, H_SGU + KT)
            pe.wait_ge(wsum_made, 2)
            with pe.Fori(0, 4 // 2) as i:
                for cl in range(2):
                    pe.wait_ge(evac, E_V + 4 * (cl - 1) + 8 * i)
                    for j in range(4):
                        u = U_V + 4 * cl + j
                        pe.wait_ge(split_lo, u + 1 + 8 * i)
                        for t in range(TT):
                            for kk in range(2):
                                k = 2 * j + kk
                                last = three(pe, banks[:, 4 * cl + t, :],
                                             h_hi[:, k, t * P:(t + 1) * P], h_lo[:, k, t * P:(t + 1) * P],
                                             unit(w_hi, u, 512)[:, kk, :], unit(w_lo, u, 512)[:, kk, :],
                                             k == 0, k == KT - 1)
                        last.then_inc(w_used, 1)
            for half in range(2):
                pe.wait_ge(evac, E_V + 16)
                pe.wait_ge(x_new, X_AO + KT * half)
                with pe.Fori(0, 4) as i:
                    for cc in range(2):
                        pe.wait_ge(h_ready, H_Y + 8 * half + cc - 1 + 2 * i)
                        for s in range(2):
                            u = U_UG + 24 * half + 2 * cc + s
                            pe.wait_ge(split_lo, u + 1 + RING * i)
                            for k in range(KT):
                                last = three(pe, banks[:, 4 * cc + s, :], unit(w_hi, u, P)[:, k, :],
                                             unit(w_lo, u, P)[:, k, :], h_hi[:, k, :], h_lo[:, k, :],
                                             k == 0, k == KT - 1)
                            last.then_inc(w_used, 1)
                        pe.wait_ge(vh_made, 8 * half + cc + 1 + 2 * i)
                        for t in range(TT):
                            last = pe.matmul(banks[:, 4 * cc + 2, t * P:(t + 1) * P], vh[:, cc, t, :],
                                             wcT[:, bass.ds(i + 4 * half, 1), :].rearrange("p g t -> p (g t)"),
                                             start=True, stop=True)
                        last.then_inc(mixed, 1)
                pe.wait_ge(h_ready, H_Y + 8 * (half + 1))
                residual(U_UG + 24 * half + 16, KT, 1, KT, y_hi, y_lo, X_AO + KT * half)
            stat(5, Q_AO + KT)

            pe.wait_ge(h_ready, H_RG + KT)
            pe.wait_ge(x_new, X_BO)
            with pe.Fori(0, B_HEADS // 2) as i:
                def project(j, dst, read):
                    u = U_B + j
                    pe.wait_ge(split_lo, u + 1 + RING * i)
                    pe.wait_ge(evac, E_RG + read - 8 + 8 * i)
                    for k in range(KT):
                        last = three(pe, banks[:, dst, :], unit(w_hi, u, P)[:, k, :], unit(w_lo, u, P)[:, k, :],
                                     h_hi[:, k, :], h_lo[:, k, :], k == 0, k == KT - 1)
                    last.then_inc(w_used, 1)

                def gates(cc, read):
                    pe.wait_ge(gw_in[cc], 32 + 32 * i)
                    pe.wait_ge(evac, E_RG + read - 8 + 8 * i)
                    pe.wait_ge(xc_made, cc + 1 + 2 * i)
                    pe.matmul(banks[:, 4 * cc + 2, :], gw[:, cc, 0, :], xc[:, cc, :], start=True, stop=True)
                    pe.matmul(banks[:, 4 * cc + 3, :], gw[:, cc, 1, :], xc[:, cc, :], start=True, stop=True)\
                      .then_inc(gates_made, 1)

                project(0, 0, 1)
                project(1, 1, 5)
                project(2, 4, 2)
                gates(0, 4)
                project(3, 5, 8)
                gates(1, 8)
            pe.wait_ge(evac, E_RG + 4 * B_HEADS)
            pe.wait_ge(h_ready, H_YB + B_HEADS)
            residual(U_BOUT, 16, 2, 6, yb_hi, yb_lo, X_BO)
            stat(6, Q_BO + KT)
            for half in range(2):
                for k in range(4):
                    pe.wait_ge(fin_scaled, 4 * half + k + 1)
                if half:
                    pe.wait_ge(y_made, 4)
                for t in range(TT):
                    for k in range(4):
                        last = pe.transpose(banks[:, t, k * P:(k + 1) * P], xT[:, 4 * half + k, t * P:(t + 1) * P], ident[:, :])
                    last.then_inc(fin_turned, 1)

        @block.scalar
        def _(act):
            chain = Chain(act, s_act)

            def plain_wait():
                act.wait_ge(consts, 1)

            act.dma_start(cT[:, :], a["c"].rearrange("o (k p) -> p (o k)", p=P), allow_slow_non_contiguous=True)\
               .then_inc(c_in, 16)
            for t in range(TT):
                act.dma_start(x_tok[:, t, :], a["x"][0, t * P:(t + 1) * P, :]).then_inc(x_in, 16)
            act.wait_ge(c_in, 16)
            act.activation(c_act[:, :], cT[:, :], ACT.Sigmoid).then_inc(c_sig, 1)
            act.wait_ge(par_turned, 1)
            act.activation(par[:, :], banks[:, 4, 0:P_TILES * P], ACT.Copy).then_inc(par_ready, 1)
            act.wait_ge(lb_zero, 1)
            act.activation(lbt[:, 1, :], lbt[:, 0, :], ACT.Exp).then_inc(lb_exp, 1)
            for m in range(KT):
                act.wait_ge(x_turned, m + 1)
                if m >= 2:
                    act.wait_ge(sq_added, m - 1)
                act.activation(sqb[:, m % 2, :], banks[:, m % 4, :], ACT.Square).then_inc(sq_made, 1)
                act.activation(xT[:, m, :], banks[:, m % 4, :], ACT.Copy).then_inc(x_new, 1)

            def root(n):
                act.wait_ge(stat_made, n)
                act.activation(rstd[:, :], banks[:, 7, :], ACT.Sqrt, bias=eps_c[:, 0:1]).then_inc(root_made, 1)

            def shifted(n0, shift):
                for k in range(KT):
                    act.wait_ge(h_scaled, n0 + k + 1)
                    if shift is None:
                        act.activation(h_hi[:, k, :], sqb[:, k % 2, :], ACT.Copy).then_inc(h_hi_made, 1)
                    else:
                        act.activation(h_hi[:, k, :], sqb[:, k % 2, :], ACT.Identity,
                                       bias=mod[:, shift + k:shift + k + 1]).then_inc(h_hi_made, 1)

            root(1)
            act.wait_ge(mod_ready, 2)
            shifted(0, 0)
            for u in range(LEAD):
                hi_unit(act, u)

            def read_out(u):
                kind = W_IN_UNITS[u]
                c, n = kind[1], n_out[0]
                if kind[0] in ("tm4", "tm2") and kind[2] != (1 if kind[0] == "tm4" else 3):
                    return
                act.wait_ge(w_used, u + 1)
                if kind[0] == "tm4":
                    for t in range(TT):
                        act.activation(sv[:, t, :], banks[:, t, 0:256], ACT.Copy).then_inc(evac, 1)
                elif kind[0] == "tm2":
                    for t in range(TT):
                        act.activation(hv[:, t, :], banks[:, t, :], ACT.Copy).then_inc(evac, 1)
                elif kind[0] == "iw":
                    act.activation(iw[:, :, :], banks[:, n % 4, 0:TT * IDX_HEADS].rearrange("p (t h) -> p t h", t=TT),
                                   ACT.Copy, scale=float(IDX_HEADS * IDX_D) ** -0.5).then_inc(evac, 1)
                elif kind[0] == "ik":
                    act.activation(ikT[:, :], banks[:, n % 4, :], ACT.Copy).then_inc(evac, 1)
                elif c in (C_IQ, C_IQ + P):
                    act.activation(iqT[:, (c - C_IQ) // P, :], banks[:, n % 4, :], ACT.Copy).then_inc(evac, 1)
                elif c in (C_SQ, C_SQ + P):
                    act.activation(sqT[:, (c - C_SQ) // P, :], banks[:, n % 4, :], ACT.Copy).then_inc(evac, 1)
                elif c in (C_SK, C_SK + P):
                    act.activation(skT[:, (c - C_SK) // P, :], banks[:, n % 4, :], ACT.Copy).then_inc(evac, 1)
                elif c >= C_CU:
                    m, gate = (c - C_CU) % CV // P, (c - C_CU) // CV
                    if gate:
                        act.activation(cacc[:, m, :], banks[:, n % 4, :], ACT.Sigmoid).then_inc(evac, 1)
                    else:
                        act.activation(hpad[:, m, TAPS - 1:], banks[:, n % 4, :], ACT.Copy).then_inc(evac, 1)
                elif c < C_HF:
                    h = c // P
                    chain.step(act.activation(hq[:, h, :], banks[:, n % 4, :], ACT.Copy, scale=float(HG_D) ** -0.5))
                    act.activation(hk[:, h, :], banks[:, n % 4, :], ACT.Sigmoid).then_inc(evac, 1)
                elif c < C_HI:
                    h = (c - C_HF) // P
                    chain.step(act.activation(hf[:, h, :], banks[:, n % 4, :], ACT.Sigmoid))
                    act.wait_ge(q_made, h + 1)
                    act.activation(hk[:, h, :], banks[:, n % 4, :], ACT.Sigmoid, scale=-1.0).then_inc(evac, 1)
                else:
                    h = (c - C_HG) // P
                    if h >= 2:
                        act.wait_ge(g_made, h - 1)
                    chain.step(act.activation(sqb[:, h % 2, :], banks[:, n % 4, :], ACT.Sigmoid))
                    act.activation(omix[:, h, :], banks[:, n % 4, :], ACT.Copy).then_inc(evac, 1)
                n_out[0] += 4 if kind[0] in ("tm4", "tm2") else 1

            def relu_scores(s):
                b = 1 + s // IDX_HEADS
                act.wait_ge(s_made, s + 1)
                if s >= 2:
                    act.wait_ge(score_added, s - 1)
                act.activation(ring2[:, s % 2, 0:P * (b + 1)], banks[:, 4 + s % 2, 0:P * (b + 1)], ACT.Relu)\
                   .then_inc(s_read, 1)

            def exps(t):
                n = P * (t // SA_HEADS + 1)
                act.wait_ge(mx_made, t + 1)
                act.activation(ring2[:, t % 2, 0:n], ring2[:, t % 2, 0:n], ACT.Exp, bias=col[:, t % 2:t % 2 + 1],
                               accum_out=col[:, 2 + t % 2:3 + t % 2]).then_inc(e_made, 1)

            def read_turned(t):
                n = P * (t // SA_HEADS + 1)
                act.wait_ge(p_turned, t + 1)
                if t >= 2:
                    act.wait_ge(pv_made, t - 1)
                act.activation(pT[:, t % 2, 0:n], banks[:, 6, 0:n], ACT.Copy).then_inc(pt_read, 1)

            def read_o(t):
                b, h = t // SA_HEADS, t % SA_HEADS
                r = slice(SA_D * (h % 2), SA_D * (h % 2) + SA_D)
                act.wait_ge(pv_made, t + 1)
                act.activation(omix[r, 4 + h // 2, b * P:(b + 1) * P], banks[r, 7, 0:P], ACT.Copy).then_inc(ob_made, 1)

            n_out = [0]
            for u in range(N_IN):
                hi_unit(act, u + LEAD)
                read_out(u)
                if u == 4:
                    for s in range(3 * IDX_HEADS):
                        relu_scores(s)
                for t in ATT_STEPS.get(u, []):
                    if t < 16:
                        exps(t)
                    if 1 <= t <= 16:
                        read_turned(t - 1)
                    if 2 <= t <= 17:
                        read_o(t - 2)
            for m in range(CVT):
                act.wait_ge(cen_made, m + 1)
                act.activation(hpad[:, m, 0:TOK], cacc[:, m, :], ACT.Square).then_inc(csq_made, 1)
            act.wait_ge(var_made, 1)
            act.activation(rstd[:, :], banks[:, 7, :], ACT.Sqrt, bias=eps_c[:, 0:1]).then_inc(croot_made, 1)
            for m in range(CVT):
                act.wait_ge(cn_made, m + 1)
                act.activation(hpad[:, m, 0:TOK], cacc[:, m, :], ACT.Sigmoid, bias=pcol("cv_ln_b", m)).then_inc(csig_made, 1)
            for c in range(3):
                act.wait_ge(kt_turned, c + 1)
                if c == 2:
                    act.wait_ge(sp_made, 1)
                act.activation(hKT[:, c % 2, :, :], banks[:, 4, :].rearrange("p (h k) -> p h k", h=HG_HEADS),
                               ACT.Copy).then_inc(kt_made, 1)
            for h in range(HG_HEADS):
                act.wait_ge(o_made, h + 1)
                act.activation(hf[:, h, :], banks[:, h, :], ACT.Square).then_inc(osq_made, 1)
            for h in range(HG_HEADS):
                act.wait_ge(om_made, h + 1)
                act.activation(hk[:, h, :], banks[:, 4 + h, :], ACT.Sqrt, bias=eps_c[:, 0:1]).then_inc(oroot_made, 1)
            act.wait_ge(w_used, N_IN)
            for n, k in enumerate(OMIX_ORDER):
                if n == 0:
                    act.wait_ge(oc_made, CVT)
                    act.wait_ge(ob_made, 16)
                if k < HG_HEADS:
                    act.wait_ge(oa_made, k + 1)
                act.activation(h_hi[:, k, :], omix[:, k, :], ACT.Copy).then_inc(h_hi_made, 1)

            def residual(base, count, units, x0, q0=None, leads=True):
                def turn(i, lead):
                    for j in range(RING):
                        if lead or j + LEAD < RING:
                            hi_unit(act, base + j + LEAD, i)
                        if (j + 1) % units == 0 and q0 is not None:
                            t, per = j // units, RING // units
                            act.wait_ge(x_new, x0 + t + 1 + per * i)
                            act.wait_ge(sq_added, q0 + t - 1 + per * i)
                            plain_wait()
                            act.activation(sqb[:, t % 2, :], xT[:, bass.ds(i * per + t, 1), :].rearrange("p a n -> p (a n)"),
                                           ACT.Square).then_inc(sq_made, 1)
                if leads:
                    with act.Fori(0, count // RING) as i:
                        turn(i, True)
                else:
                    with act.Fori(0, count // RING - 1) as i:
                        turn(i, True)
                    turn(count // RING - 1, False)

            residual(U_OUT, KT, 1, X_OUT, Q_OUT)
            root(2)
            shifted(S_FF, 3 * KT)
            for half in range(2):
                with act.Fori(0, 4) as i:
                    for j in range(RING):
                        u = U_FF + 32 * half + j
                        n = 16 * half + j
                        hi_unit(act, u + LEAD, i)
                        act.wait_ge(w_used, u + 1 + RING * i)
                        act.wait_ge(h_ready, H_HID + n - 1 + RING * i)
                        act.activation(relu[:, j % 2, :], banks[:, j, :], ACT.Relu).then_inc(evac, 1)
                        act.wait_ge(evac, E_FF + n + 1 + RING * i)
                        plain_wait()
                        act.activation(hid_hi[:, bass.ds(i * RING + j, 1), :].rearrange("p a n -> p (a n)"),
                                       relu[:, j % 2, :], ACT.Square).then_inc(h_hi_made, 1)
                residual(U_FF + 32 * half + 16, 16, 2, X_FF + KT * half, Q_FF if half else None)
            root(3)
            for k in range(KT):
                act.wait_ge(x_new, X_FIN + k + 1)
                act.wait_ge(sq_added, Q_FIN + k - 1)
                act.activation(sqb[:, k % 2, :], xT[:, k, :], ACT.Square).then_inc(sq_made, 1)
            act.dma_start(ws[:, :, :], a["a_w_s_2"][0].rearrange("g t s -> t g s")).then_inc(ws_in, 16)
            act.dma_start(bsp[:, :, :], a["a_b_s_2"][0].rearrange("(o g) t -> o g t", o=1).broadcast_to([P, A_GROUPS, P]))\
               .then_inc(bs_in, 16)
            root(4)
            shifted(S_SGU, None)
            act.wait_ge(ws_turned, 1)
            act.activation(wcT[:, :, :].rearrange("p (b g) t -> p b (g t)", b=2), banks[:, 4:6, :], ACT.Copy)\
               .then_inc(ws_copied, 1)
            with act.Fori(0, 2) as i:
                for cl in range(2):
                    def vtile(t):
                        return vt[:, t, bass.ds(i * 1024 + cl * 512, 512)]
                    for j in range(4):
                        hi_unit(act, U_V + 4 * cl + j + LEAD, i * 2)
                    act.wait_ge(w_used, U_V + 4 * cl + 4 + 8 * i)
                    for t in range(TT):
                        v = vtile(t)
                        plain_wait()
                        act.activation(v, banks[:, 4 * cl + t, :], ACT.Copy).then_inc(v_copied, 1)
                        n = 4 * cl + t
                        act.wait_ge(v_stat, V0 + n - 1 + 8 * i)
                        act.activation(e0[:, t % 2, :], banks[:, 4 * cl + t, :], ACT.Square).then_inc(evac, 1)
                        act.wait_ge(v_inner, n + 1 + 8 * i)
                        act.activation(e0[:, t % 2, :], e0[:, t % 2, :], ACT.Tanh).then_inc(v_tanh, 1)
            act.wait_ge(v_var, TT)
            act.activation(vrs[:, :], vmv[:, :, 1], ACT.Sqrt, bias=eps_c[:, 1:2]).then_inc(v_root, 1)
            for half in range(2):
                with act.Fori(0, 4) as i:
                    for cc in range(2):
                        u, c = U_UG + 24 * half + 2 * cc, 8 * half + cc
                        hi_unit(act, u + LEAD, i)
                        act.wait_ge(w_used, u + 1 + RING * i)
                        act.wait_ge(h_ready, H_Y + c - 1 + 2 * i)
                        act.activation(e0[:, cc, :], banks[:, 4 * cc, :], ACT.Square).then_inc(u_sq, 1)
                        act.wait_ge(u_inner, c + 1 + 2 * i)
                        act.activation(e0[:, cc, :], e0[:, cc, :], ACT.Tanh).then_inc(u_tanh, 1)
                        hi_unit(act, u + 1 + LEAD, i)
                        act.wait_ge(w_used, u + 2 + RING * i)
                        act.activation(e1[:, cc, :], banks[:, 4 * cc + 1, :], ACT.Sigmoid).then_inc(g_sig, 1)
                        act.wait_ge(y_out, c + 1 + 2 * i)
                        plain_wait()
                        act.activation(y_hi[:, bass.ds(i * 2 + cc, 1), :].rearrange("p a n -> p (a n)"), e2[:, cc, :],
                                       ACT.Copy).then_inc(h_hi_made, 1)
                residual(U_UG + 24 * half + 16, KT, 1, X_AO + KT * half, Q_AO if half else None)
            root(5)
            shifted(S_RG, None)
            act.wait_ge(sp_abs, 1)
            act.activation(spt[:, 1, :], spt[:, 0, :], ACT.Exp, scale=-1.0).then_inc(sp_exp, 1)
            act.wait_ge(pad_zero, 1)
            with act.Fori(0, B_HEADS // 2) as i:
                def read_x(cc):
                    act.wait_ge(w_used, U_B + 2 * cc + 1 + RING * i)
                    act.activation(xbp[:, cc, B_TAPS:], banks[:, 4 * cc, :], ACT.Copy).then_inc(evac, 1)

                def read_gates(cc):
                    act.wait_ge(gates_made, cc + 1 + 2 * i)
                    plain_wait()
                    act.activation(t_r[:, cc, :], banks[:, 4 * cc + 2, :], ACT.Sigmoid,
                                   bias=par[:, bass.ds(i * 2 + (PCOL["b_gate_a_b_2"] + cc), 1)]).then_inc(evac, 1)
                    plain_wait()
                    act.activation(t_i[:, cc, :], banks[:, 4 * cc + 3, :], ACT.Sigmoid,
                                   bias=par[:, bass.ds(i * 2 + (PCOL["b_gate_x_b_2"] + cc), 1)]).then_inc(evac, 1)

                def read_g(cc):
                    act.wait_ge(w_used, U_B + 2 * cc + 2 + RING * i)
                    act.activation(t_sg[:, cc, :], banks[:, 4 * cc + 1, :], ACT.Sigmoid).then_inc(g_sig, 1)
                    act.activation(t_g[:, cc, :], banks[:, 4 * cc + 1, :], ACT.Copy).then_inc(evac, 1)

                hi_unit(act, U_B + LEAD, i)
                read_x(0)
                hi_unit(act, U_B + 1 + LEAD, i)
                hi_unit(act, U_B + 2 + LEAD, i)
                read_x(1)
                read_gates(0)
                read_g(0)
                hi_unit(act, U_B + 3 + LEAD, i)
                read_gates(1)
                read_g(1)
                act.wait_ge(sp_ready, 1)
                for cc in range(2):
                    act.wait_ge(evac, E_RG + (4, 7)[cc] + 8 * i)
                    plain_wait()
                    act.activation(t_a[:, cc, :], t_r[:, cc, :], ACT.Exp,
                                   scale=spt[:, 1, bass.ds(i * 2 + cc, 1)]).then_inc(ra_made, 1)
                for cc in range(2):
                    act.wait_ge(ra_made, cc + 1 + 2 * i)
                    plain_wait()
                    act.activation(t_r[:, cc, :], t_r[:, cc, :], ACT.Tanh,
                                   scale=spt[:, 4, bass.ds(i * 2 + cc, 1)]).then_inc(rt_made, 1)
                for cc in range(2):
                    act.wait_ge(rt_made, cc + 1 + 2 * i)
                    act.activation(t_s[:, cc, :], t_r[:, cc, :], ACT.Sqrt).then_inc(rs_made, 1)
                for cc in range(2):
                    act.wait_ge(yb_out, cc + 1 + 2 * i)
                    plain_wait()
                    act.activation(yb_hi[:, bass.ds(i * 2 + cc, 1), :].rearrange("p a n -> p (a n)"), xc[:, cc, :],
                                   ACT.Copy).then_inc(h_hi_made, 1)
            residual(U_BOUT, 16, 2, X_BO, Q_BO, leads=False)
            root(6)
            for half in range(2):
                for t in range(TT):
                    act.wait_ge(fin_turned, 4 * half + t + 1)
                    act.activation(y_tok[:, t, 512 * half:512 * (half + 1)], banks[:, t, :], ACT.Copy).then_inc(y_made, 1)

        @block.vector
        def _(dve):
            chain = Chain(dve, s_dve)
            dve.memset(ssq[:, :], 0.0).then_inc(ssq_zero, 1)
            dve.wait_ge(c_sig, 1)
            dve.tensor_tensor(c_act[:, :], c_act[:, :], cT[:, :], ALU.mult).then_inc(c_ready, 1)
            dve.wait_ge(c_ready, 1)

            def ada(n, raw_unit):
                raw_wait(dve, raw_unit)
                acc, r = (acc1 if n < 2 * KT else acc2)[:, n // KT % 2, :], raw[:, raw_unit % RING, :]
                if n % KT == 0:
                    if n >= 4 * KT:
                        dve.wait_ge(mod_summed, n // KT - 1)
                    ins = dve.tensor_scalar(acc, r, c_act[:, 0:1], None, ALU.mult)
                else:
                    dve.wait_ge(ada_dve, n)
                    ins = dve.scalar_tensor_tensor(acc, r, c_act[:, n % KT:n % KT + 1], acc, ALU.mult, ALU.add)
                ins.then_inc(ada_dve, 1)

            def add_square(q, buf):
                dve.wait_ge(sq_made, q + 1)
                if q:
                    dve.wait_ge(sq_added, q)
                dve.tensor_tensor(ssq[:, :], ssq[:, :], buf, ALU.add).then_inc(sq_added, 1)

            def new_sum(n):
                dve.wait_ge(stat_made, n)
                dve.memset(ssq[:, :], 0.0).then_inc(ssq_zero, 1)
                dve.wait_ge(ssq_zero, n + 1)

            dve.wait_ge(ssq_zero, 1)
            for n in range(8):
                ada(n, n)
            dve.wait_ge(par_ready, 1)
            logit = pcol("hg_lb_logits", 0, HG_HEADS)
            dve.tensor_tensor(lbt[:, 0, :], logit, logit, ALU.subtract).then_inc(lb_zero, 1)
            for n in range(8):
                ada(8 + n, 8 + n)
                add_square(n, sqb[:, n % 2, :])
            dve.wait_ge(lb_exp, 1)
            chain.link(dve.reciprocal(lbt[:, 2, :], lbt[:, 1, :]))
            chain.link(dve.tensor_tensor(lbt[:, 1, :], lbt[:, 1, :], lbt[:, 2, :], ALU.mult))
            chain.link(dve.tensor_tensor(lbt[:, 2, :], lbt[:, 1, :], lbt[:, 1, :], ALU.subtract))
            chain.link(dve.tensor_scalar(lbt[:, 3, :], lbt[:, 2, :], -1.0, 1.0, ALU.mult, ALU.add))

            def mod_part(n, group):
                dve.wait_ge(mod_summed, n + 1)
                g0 = group * KT
                dve.tensor_tensor(mod[:, g0:g0 + KT], banks[:, 6 if n < 2 else 7, 0:KT], pcol("ada_b", g0, KT), ALU.add)\
                   .then_inc(mod_ready, 1)

            mod_part(0, 1)
            dve.wait_ge(mod_ready, 1)
            chain.link(dve.scalar_tensor_tensor(scale1[:, :], mod[:, KT:2 * KT], 1.0, pcol("norm_mix_w", 0, KT),
                                                ALU.add, ALU.mult))
            mod_part(1, 0)

            def normalised(n, r0, scale, shift):
                dve.wait_ge(root_made, n)
                chain.link(dve.reciprocal(rstd[:, :], rstd[:, :]))

                def low(k):
                    dve.wait_ge(h_hi_made, r0 + k + 1)
                    t, hi = sqb[:, k % 2, :], h_hi[:, k, :].bitcast(F32)
                    if shift is None:
                        ins = dve.tensor_tensor(h_lo[:, k, :], t, hi, ALU.subtract)
                    else:
                        ins = dve.scalar_tensor_tensor(h_lo[:, k, :], t, mod[:, shift + k:shift + k + 1], hi,
                                                       ALU.add, ALU.subtract)
                    ins.then_inc(h_ready, 1)

                if shift is not None:
                    dve.wait_ge(mod_ready, 2)
                for k in range(KT):
                    if k >= 2:
                        dve.wait_ge(h_ready, r0 + k - 1)
                    dve.scalar_tensor_tensor(sqb[:, k % 2, :], xT[:, k, :], scale(k), rstd[:, :], ALU.mult, ALU.mult)\
                       .then_inc(h_scaled, 1)
                    if k:
                        low(k - 1)
                low(KT - 1)

            normalised(1, H_MIX, lambda k: scale1[:, k:k + 1], 0)

            def next_lo_unit(u):
                if u < N_IN:
                    d = arrival[("w", u)] - 1
                    while STREAM[d][0] == "ada" and d >= 2 * KT:
                        d -= 1
                    for e in range(d + 1, arrival[("w", u)]):
                        ada(sum(x[0] == "ada" for x in STREAM[:e]), e)
                lo_unit(dve, u)

            for u in range(LEAD):
                next_lo_unit(u)

            def add_score(s):
                b, h = 1 + s // IDX_HEADS, s % IDX_HEADS
                n = P * (b + 1)
                dve.wait_ge(s_read, s + 1)
                if s:
                    dve.wait_ge(score_added, s)
                w = iw[:, b, h:h + 1]
                if h == 0:
                    ins = dve.tensor_scalar(score[b][:, :], ring2[:, s % 2, 0:n], w, None, ALU.mult)
                else:
                    ins = dve.scalar_tensor_tensor(score[b][:, :], ring2[:, s % 2, 0:n], w, score[b][:, :], ALU.mult, ALU.add)
                ins.then_inc(score_added, 1)

            def top_round(r):
                if r == 0:
                    dve.wait_ge(diag_made, 3)
                for b in range(3):
                    chain.step(dve.max(m8[:, b, :], score[b + 1][:, :]))
                n = chain.n
                for b in range(3):
                    chain.wait(n - 2 + b)
                    chain.step(dve.match_replace(score[b + 1][:, :], m8[:, b, :], score[b + 1][:, :], TAKEN))
                chain.wait()

            def soft_in(t):
                b = t // SA_HEADS
                n = P * (b + 1)
                dve.wait_ge(l_made, t + 1)
                if t % SA_HEADS == 0:
                    dve.wait_ge(bias_made, b + 1)
                if t >= 2:
                    dve.wait_ge(p_turned, t - 1)
                dve.scalar_tensor_tensor(ring2[:, t % 2, 0:n], banks[:, 4 + t % 2, 0:n], float(SA_D) ** -0.5,
                                         score[b][:, :], ALU.mult, ALU.add).then_inc(l_read, 1)
                dve.wait_ge(l_read, t + 1)
                dve.tensor_reduce(col[:, t % 2:t % 2 + 1], ring2[:, t % 2, 0:n], AX_X, ALU.max, negate=True)\
                   .then_inc(mx_made, 1)

            def soft_out(t):
                n = P * (t // SA_HEADS + 1)
                dve.wait_ge(e_made, t + 1)
                chain.link(dve.reciprocal(col[:, 4 + t % 2:5 + t % 2], col[:, 2 + t % 2:3 + t % 2]))
                dve.tensor_scalar(ring2[:, t % 2, 0:n], ring2[:, t % 2, 0:n], col[:, 4 + t % 2:5 + t % 2], None, ALU.mult)\
                   .then_inc(p_made, 1)

            rounds = list(range(TOPK // 8))
            for u in range(N_IN):
                next_lo_unit(u + LEAD)
                if u == 4:
                    for s in range(3 * IDX_HEADS):
                        add_score(s)
                if u >= 5:
                    if rounds:
                        top_round(rounds.pop(0))
                        if not rounds:
                            for b in range(1, TT):
                                dve.tensor_scalar(score[b][:, :], score[b][:, :], TAKEN, NEG_BIG, ALU.not_equal, ALU.mult)\
                                   .then_inc(taken_made, 1)
                if u in MOD_STEPS:
                    n = MOD_STEPS.index(u)
                    mod_part(2 + n, (2, 4, 3, 5)[n])
                for t in ATT_STEPS.get(u, []):
                    if t < 16:
                        soft_in(t)
                    if 1 <= t <= 16:
                        soft_out(t - 1)
            dve.wait_ge(mod_ready, 6)
            chain.link(dve.scalar_tensor_tensor(scale2[:, :], mod[:, 4 * KT:5 * KT], 1.0, pcol("norm_mlp_w", 0, KT),
                                                ALU.add, ALU.mult))
            dve.wait_ge(mean_made, 1)
            for m in range(CVT):
                dve.tensor_tensor(cacc[:, m, :], cacc[:, m, :], banks[:, 7, :], ALU.subtract).then_inc(cen_made, 1)
            dve.wait_ge(croot_made, 1)
            chain.link(dve.reciprocal(rstd[:, :], rstd[:, :]))
            for m in range(CVT):
                dve.scalar_tensor_tensor(cacc[:, m, :], cacc[:, m, :], pcol("cv_ln_w", m), rstd[:, :], ALU.mult, ALU.mult)\
                   .then_inc(cn_made, 1)
            for m in range(CVT):
                dve.wait_ge(csig_made, m + 1)
                dve.scalar_tensor_tensor(omix[:, 6 + m, :], cacc[:, m, :], pcol("cv_ln_b", m), hpad[:, m, 0:TOK],
                                         ALU.add, ALU.mult).then_inc(oc_made, 1)
            for h in range(HG_HEADS):
                dve.wait_ge(evac, 21 + h)
                lb, om = lbt[:, 2, h:h + 1], lbt[:, 3, h:h + 1]
                chain.step(dve.tensor_scalar(hf[:, h, :], hf[:, h, :], om, lb, ALU.mult, ALU.add))
                chain.step(dve.tensor_scalar(hk[:, h, :], hk[:, h, :], om, None, ALU.mult))
                chain.wait(chain.n - 1)
                dve.tensor_scalar(hf[:, h, :], hf[:, h, :], TINY, None, ALU.max).then_inc(f_made, 1)
            dve.wait_ge(f_made, HG_HEADS)
            dve.wait_ge(q_made, HG_HEADS)
            dve.wait_ge(oc_made, CVT)
            dve.wait_ge(ob_made, 16)
            dve.wait_ge(taken_made, 3)
            for l in range(8):
                for p in range(2):
                    n = 2 * l + p
                    dve.wait_ge(lev_made, n + 1)
                    A = hA[:, 2 * p:2 * p + 2, :, :].rearrange("p h c i -> p (h c) i")
                    S = banks[:, 4 + 2 * p:6 + 2 * p, :].rearrange("p b (c i) -> p (b c) i", c=TT)
                    if l == 0:
                        chain.step(dve.tensor_tensor(A, S, ident[:, :].unsqueeze(1).broadcast_to([P, 8, P]), ALU.mult))
                    else:
                        dve.wait_ge(upd_made, n - 1)
                        dve_mask = masks[:, l - 1, :].bitcast(I32).unsqueeze(1).broadcast_to([P, 8, P])
                        chain.step(dve.copy_predicated(A, dve_mask, S))
                    b = LEVELS[l - 1] if l else None
                    if l == 0:
                        dve.tensor_tensor(hq[:, 2 * p:2 * p + 2, :], hq[:, 2 * p:2 * p + 2, :], hf[:, 2 * p:2 * p + 2, :],
                                          ALU.mult).then_inc(upd_made, 1)
                        continue
                    T = t_level(b, p)
                    for h in range(2):
                        Q, K = halves(hq, b, p)[:, h, :, 1, :], halves(hk, b, p)[:, h, :, 0, :]
                        shape = [P, TOK // (2 * b), b]
                        chain.step(dve.tensor_tensor(Q, Q, T[:, h, :, 0].unsqueeze(2).broadcast_to(shape), ALU.mult))
                        chain.step(dve.tensor_tensor(K, K, T[:, h, :, 1].unsqueeze(2).broadcast_to(shape), ALU.mult))
                    up = hgt[:, 2 * p:2 * p + 2, T_OFF[2 * b]:T_OFF[2 * b] + TOK // (2 * b)]
                    dve.tensor_tensor(up, T[:, :, :, 0], T[:, :, :, 1], ALU.mult).then_inc(upd_made, 1)
            for c in range(3):
                dve.wait_ge(sp_made, c + 1)
                for h in range(HG_HEADS):
                    ps = banks[:, 6, h * P:(h + 1) * P]
                    if c == 0:
                        ins = dve.tensor_copy(hS[:, 0, h, :], ps)
                    else:
                        dve.wait_ge(st_made, c)
                        decay = hgt[:, h, T_OFF[128] + c:T_OFF[128] + c + 1]
                        ins = dve.scalar_tensor_tensor(hS[:, c, h, :], hS[:, c - 1, h, :], decay, ps, ALU.mult, ALU.add)
                ins.then_inc(st_made, 1)
            for h in range(HG_HEADS):
                dve.wait_ge(oroot_made, h + 1)
                chain.link(dve.reciprocal(hk[:, h, :], hk[:, h, :]))
                chain.link(dve.scalar_tensor_tensor(hk[:, h, :], banks[:, h, :], pcol("hg_onorm_w", h), hk[:, h, :],
                                                    ALU.mult, ALU.mult))
                dve.wait_ge(g_made, h + 1)
                dve.tensor_tensor(omix[:, h, :], omix[:, h, :], hk[:, h, :], ALU.mult).then_inc(oa_made, 1)
            dve.wait_ge(w_used, N_IN)
            for n, k in enumerate(OMIX_ORDER):
                dve.wait_ge(h_hi_made, H_OMIX + n + 1)
                dve.tensor_tensor(h_lo[:, k, :], omix[:, k, :], h_hi[:, k, :].bitcast(F32), ALU.subtract).then_inc(h_ready, 1)

            def residual(base, count, units, x0, q0=None, gate=None, leads=True):
                per = RING // units

                def turn(i, lead):
                    for j in range(RING):
                        if lead or j + LEAD < RING:
                            lo_unit(dve, base + j + LEAD, i)
                        if (j + 1) % units == 0:
                            t = j // units
                            dve.wait_ge(w_used, base + j + 1 + RING * i)
                            x = xT[:, bass.ds(i * per + t, 1), :].rearrange("p a n -> p (a n)")
                            if gate is None:
                                ins = dve.tensor_tensor(x, x, banks[:, t, :], ALU.add)
                            else:
                                ins = dve.scalar_tensor_tensor(x, banks[:, t, :], mod[:, bass.ds(i * per + (gate + t), 1)],
                                                               x, ALU.mult, ALU.add)
                            ins.then_inc(x_new, 1)
                            if q0 is not None:
                                dve.wait_ge(sq_made, q0 + t + 1 + per * i)
                                dve.wait_ge(sq_added, q0 + t + per * i)
                                dve.tensor_tensor(ssq[:, :], ssq[:, :], sqb[:, t % 2, :], ALU.add).then_inc(sq_added, 1)
                if leads:
                    with dve.Fori(0, count // RING) as i:
                        turn(i, True)
                else:
                    with dve.Fori(0, count // RING - 1) as i:
                        turn(i, True)
                    turn(count // RING - 1, False)

            new_sum(1)
            residual(U_OUT, KT, 1, X_OUT, Q_OUT, 2 * KT)
            normalised(2, H_FF, lambda k: scale2[:, k:k + 1], 3 * KT)
            new_sum(2)
            for half in range(2):
                with dve.Fori(0, 4) as i:
                    for j in range(RING):
                        n = 16 * half + j
                        lo_unit(dve, U_FF + 32 * half + j + LEAD, i)
                        dve.wait_ge(evac, E_FF + n + 1 + RING * i)
                        dve.wait_ge(h_ready, H_HID + n - 1 + RING * i)
                        dve.tensor_tensor(relu2[:, j % 2, :], relu[:, j % 2, :], relu[:, j % 2, :], ALU.mult)\
                           .then_inc(relu_sq, 1)
                        dve.wait_ge(relu_sq, n + 1 + RING * i)
                        dve.wait_ge(h_hi_made, H_HID + n + 1 + RING * i)
                        dve.tensor_tensor(hid_lo[:, bass.ds(i * RING + j, 1), :].rearrange("p a n -> p (a n)"),
                                          relu2[:, j % 2, :],
                                          hid_hi[:, bass.ds(i * RING + j, 1), :].rearrange("p a n -> p (a n)").bitcast(F32),
                                          ALU.subtract).then_inc(h_ready, 1)
                residual(U_FF + 32 * half + 16, 16, 2, X_FF + KT * half, Q_FF if half else None, 5 * KT)
            dve.wait_ge(root_made, 3)
            chain.link(dve.reciprocal(rstd[:, :], rstd[:, :]))
            new_sum(3)
            for k in range(KT):
                dve.scalar_tensor_tensor(xT[:, k, :], xT[:, k, :], pcol("final_norm_w", k), rstd[:, :], ALU.mult, ALU.mult)\
                   .then_inc(x_new, 1)
                if k:
                    add_square(Q_FIN + k - 1, sqb[:, (k - 1) % 2, :])
            add_square(Q_FIN + KT - 1, sqb[:, 1, :])
            normalised(4, H_SGU, lambda k: pcol("norm_w_2", k), None)
            new_sum(4)
            dve.wait_ge(ws_summed, 1)
            for g in range(2):
                dve.tensor_scalar(wsum[:, 4 * g:4 * g + 4, :].rearrange("p g t -> p (g t)"), banks[:, 4 + g, :], 0.5, None,
                                  ALU.mult).then_inc(wsum_made, 1)
            dve.wait_ge(bs_in, 16)
            dve.tensor_scalar(bsp[:, :, :], bsp[:, :, :], 0.5, None, ALU.mult).then_inc(v_stat, 1)
            dve.tensor_scalar(lnw2[:, :], pcol("a_ln_w_2", 0, AT), 0.5, None, ALU.mult).then_inc(v_stat, 1)
            with dve.Fori(0, 2) as i:
                for cl in range(2):
                    def vtile(t):
                        return vt[:, t, bass.ds(i * 1024 + cl * 512, 512)]
                    for j in range(4):
                        lo_unit(dve, U_V + 4 * cl + j + LEAD, i * 2)
                    for t in range(TT):
                        n = 4 * cl + t
                        e = e0[:, t % 2, :]
                        dve.wait_ge(evac, E_V + n + 1 + 8 * i)
                        dve.wait_ge(v_copied, n + 1 + 8 * i)
                        dve.tensor_scalar(e, e, GELU_C * GELU_A, GELU_C, ALU.mult, ALU.add).then_inc(v_aff, 1)
                        dve.wait_ge(v_aff, n + 1 + 8 * i)
                        dve.tensor_tensor(e, e, vtile(t), ALU.mult).then_inc(v_inner, 1)
                        dve.wait_ge(v_tanh, n + 1 + 8 * i)
                        dve.scalar_tensor_tensor(vtile(t), e, 1.0, vtile(t), ALU.add, ALU.mult).then_inc(v_gelu, 1)
                        dve.wait_ge(v_gelu, n + 1 + 8 * i)
                        dve.bn_stats(vst[:, t, bass.ds(i * 2 + cl, 1), :].rearrange("p a n -> p (a n)"), vtile(t))\
                           .then_inc(v_stat, 1)
            dve.wait_ge(v_stat, V0 + 16)
            for t in range(TT):
                dve.bn_aggr(vmv[:, t, :], vst[:, t, :, :].rearrange("p a n -> p (a n)")).then_inc(v_var, 1)
            dve.wait_ge(v_root, 1)
            chain.link(dve.reciprocal(vrs[:, :], vrs[:, :]))
            for half in range(2):
                with dve.Fori(0, 4) as i:
                    for cc in range(2):
                        u, c = U_UG + 24 * half + 2 * cc, 8 * half + cc
                        dve.wait_ge(h_ready, H_Y + c - 1 + 2 * i)
                        for t in range(TT):
                            ins = dve.tensor_scalar(vh[:, cc, t, :], vt[:, t, bass.ds(i * 2 * P + c * P, P)],
                                                    vmv[:, t, 0:1], vrs[:, t:t + 1], ALU.subtract, ALU.mult)
                        ins.then_inc(vh_made, 1)
                        lo_unit(dve, u + LEAD, i)
                        e = e0[:, cc, :]
                        dve.wait_ge(u_sq, c + 1 + 2 * i)
                        dve.tensor_scalar(e, e, GELU_C * GELU_A, GELU_C, ALU.mult, ALU.add).then_inc(u_aff, 1)
                        dve.wait_ge(u_aff, c + 1 + 2 * i)
                        dve.tensor_tensor(e, e, banks[:, 4 * cc, :], ALU.mult).then_inc(u_inner, 1)
                        dve.scalar_tensor_tensor(eb[:, cc, :], wsum[:, bass.ds(i + 4 * half, 1), :].rearrange("p g t -> p (g t)"),
                                                 par[:, bass.ds(i * 2 + (PCOL["a_ln_b_2"] + c), 1)],
                                                 bsp[:, bass.ds(i + 4 * half, 1), :].rearrange("p g t -> p (g t)"),
                                                 ALU.mult, ALU.add).then_inc(eb_made, 1)
                        lo_unit(dve, u + 1 + LEAD, i)
                        dve.wait_ge(u_tanh, c + 1 + 2 * i)
                        dve.scalar_tensor_tensor(e, e, 1.0, banks[:, 4 * cc, :], ALU.add, ALU.mult).then_inc(u_gelu, 1)
                        dve.wait_ge(g_sig, c + 1 + 2 * i)
                        dve.tensor_tensor(e1[:, cc, :], e1[:, cc, :], banks[:, 4 * cc + 1, :], ALU.mult).then_inc(ug_made, 1)
                        dve.wait_ge(mixed, c + 1 + 2 * i)
                        dve.wait_ge(eb_made, c + 1 + 2 * i)
                        dve.scalar_tensor_tensor(e2[:, cc, :].rearrange("p (n t) -> p n t", t=P),
                                                 banks[:, 4 * cc + 2, :].rearrange("p (n t) -> p n t", t=P),
                                                 lnw2[:, bass.ds(i * 2 + c, 1)],
                                                 eb[:, cc, :].unsqueeze(1).broadcast_to([P, TT, P]),
                                                 ALU.mult, ALU.add).then_inc(s_mixed, 1)
                        dve.wait_ge(s_mixed, c + 1 + 2 * i)
                        dve.wait_ge(ugp_made, c + 1 + 2 * i)
                        dve.tensor_tensor(e2[:, cc, :], e2[:, cc, :], e, ALU.mult).then_inc(y_out, 1)
                        dve.wait_ge(y_out, c + 1 + 2 * i)
                        dve.wait_ge(h_hi_made, H_Y + c + 1 + 2 * i)
                        k = bass.ds(i * 2 + cc, 1)
                        dve.tensor_tensor(y_lo[:, k, :].rearrange("p a n -> p (a n)"), e2[:, cc, :],
                                          y_hi[:, k, :].rearrange("p a n -> p (a n)").bitcast(F32),
                                          ALU.subtract).then_inc(h_ready, 1)
                residual(U_UG + 24 * half + 16, KT, 1, X_AO + KT * half, Q_AO if half else None)
            lam = pcol("b_lambda_2", 0, B_HEADS)
            s_, e_, m_, q_, o_ = (spt[:, k, :] for k in range(5))
            dve.wait_ge(x_new, X_BO)
            chain.link(dve.tensor_scalar(m_, lam, -1.0, 0.0, ALU.mult, ALU.max))
            chain.link(dve.tensor_scalar(s_, lam, 0.0, None, ALU.max))
            dve.tensor_tensor(s_, s_, m_, ALU.add).then_inc(sp_abs, 1)
            normalised(5, H_RG, lambda k: pcol("norm_w_2", KT + k), None)
            new_sum(5)
            dve.memset(xbp[:, :, 0:B_TAPS], 0.0).then_inc(pad_zero, 1)
            dve.wait_ge(sp_exp, 1)
            chain.link(dve.tensor_scalar(s_, e_, 2.0, None, ALU.add))
            chain.link(dve.reciprocal(s_, s_))
            chain.link(dve.tensor_tensor(s_, s_, e_, ALU.mult))
            chain.link(dve.tensor_tensor(q_, s_, s_, ALU.mult))
            chain.link(dve.tensor_scalar(o_, q_, 1.0 / 17, None, ALU.mult))
            for k in (15, 13, 11, 9, 7, 5, 3):
                chain.link(dve.scalar_tensor_tensor(o_, o_, 1.0 / k, q_, ALU.add, ALU.mult))
            chain.link(dve.scalar_tensor_tensor(o_, o_, 1.0, s_, ALU.add, ALU.mult))
            chain.link(dve.scalar_tensor_tensor(o_, o_, 2.0, m_, ALU.mult, ALU.add))
            chain.link(dve.tensor_scalar(e_, o_, -RG_C, None, ALU.mult))
            dve.tensor_scalar(o_, o_, RG_C / 2, None, ALU.mult).then_inc(sp_ready, 1)
            with dve.Fori(0, B_HEADS // 2) as i:
                def conv(cc):
                    dve.wait_ge(evac, E_RG + cc + 1 + 8 * i)
                    dve.wait_ge(h_ready, H_YB + cc - 1 + 2 * i)
                    for k in range(B_TAPS):
                        src = xbp[:, cc, 1 + k:1 + k + TOK]
                        w = par[:, bass.ds(i * 2 + (PCOL["b_conv_w_2"] + B_HEADS * k + cc), 1)]
                        if k == 0:
                            ins = dve.tensor_scalar(xc[:, cc, :], src, w, par[:, bass.ds(i * 2 + (PCOL["b_conv_b_2"] + cc), 1)],
                                                    ALU.mult, ALU.add)
                        else:
                            dve.wait_ge(tap_made, 3 * cc + k + 6 * i)
                            ins = dve.scalar_tensor_tensor(xc[:, cc, :], src, w, xc[:, cc, :], ALU.mult, ALU.add)
                        ins.then_inc(tap_made if k < B_TAPS - 1 else xc_made, 1)

                def decay(cc):
                    n = cc + 1 + 2 * i
                    dve.wait_ge(ra_made, n)
                    dve.wait_ge(rt_made, n)
                    dve.scalar_tensor_tensor(t_a[:, cc, :], t_a[:, cc, :], 1.0, t_r[:, cc, :], ALU.add, ALU.mult)\
                       .then_inc(a1_made, 1)
                    dve.wait_ge(a1_made, n)
                    dve.tensor_scalar(t_a[:, cc, :], t_a[:, cc, :], -1.0, 1.0, ALU.mult, ALU.add).then_inc(a_made, 1)
                    dve.wait_ge(a_made, n)
                    dve.wait_ge(rs_made, n)
                    dve.scalar_tensor_tensor(t_s[:, cc, :], t_a[:, cc, :], 1.0, t_s[:, cc, :], ALU.add, ALU.mult)\
                       .then_inc(mult_made, 1)
                    dve.wait_ge(mult_made, n)
                    dve.wait_ge(ix_made, n)
                    dve.tensor_tensor(t_b[:, cc, :], t_s[:, cc, :], t_i[:, cc, :], ALU.mult).then_inc(bt_made, 1)
                    dve.wait_ge(bt_made, n)
                    dve.tensor_tensor_scan(t_s[:, cc, :], t_a[:, cc, :], t_b[:, cc, :], 0.0, ALU.mult, ALU.add)\
                       .then_inc(scanned, 1)
                    dve.wait_ge(scanned, n)
                    dve.wait_ge(gg_made, n)
                    dve.tensor_tensor(xc[:, cc, :], t_s[:, cc, :], t_g[:, cc, :], ALU.mult).then_inc(yb_out, 1)
                    dve.wait_ge(yb_out, n)
                    dve.wait_ge(h_hi_made, H_YB + n)
                    k = bass.ds(i * 2 + cc, 1)
                    dve.tensor_tensor(yb_lo[:, k, :].rearrange("p a n -> p (a n)"), xc[:, cc, :],
                                      yb_hi[:, k, :].rearrange("p a n -> p (a n)").bitcast(F32),
                                      ALU.subtract).then_inc(h_ready, 1)

                lo_unit(dve, U_B + LEAD, i)
                conv(0)
                lo_unit(dve, U_B + 1 + LEAD, i)
                lo_unit(dve, U_B + 2 + LEAD, i)
                conv(1)
                lo_unit(dve, U_B + 3 + LEAD, i)
                for cc in range(2):
                    decay(cc)
            residual(U_BOUT, 16, 2, X_BO, Q_BO, leads=False)
            dve.wait_ge(root_made, 6)
            chain.link(dve.reciprocal(rstd[:, :], rstd[:, :]))
            for k in range(KT):
                dve.scalar_tensor_tensor(xT[:, k, :], xT[:, k, :], pcol("norm_f_w_2", k), rstd[:, :], ALU.mult, ALU.mult)\
                   .then_inc(fin_scaled, 1)

        @block.gpsimd
        def _(pool):
            chain = Chain(pool, s_pool)
            chain.link(pool.memset(par_rows[:, :, :], 0.0))
            for name, rows in PARAMS:
                if name.startswith("pad"):
                    continue
                src = a[name]
                if name == "norm_f_w_2" or name == "final_norm_w":
                    src = src.rearrange("(r p) -> r p", p=P)
                elif name in ("cv_w", "b_conv_w_2"):
                    src = src[0].rearrange("k (r p) -> (k r) p", p=P)
                else:
                    src = src.rearrange("l (r p) -> (l r) p", p=P)
                c = PCOL[name]
                pool.dma_start(par_rows[c % P:c % P + rows, c // P, :], src).then_inc(par_in, 16)
            chain.step(pool.memset(ident[:, :], 0.0))
            chain.step(pool.memset(ones_d[:, :], 1.0 / D))
            chain.step(pool.memset(ones1[:, :], 1.0))
            chain.step(pool.memset(ones_m[:, 0, :], 1.0 / HG_D))
            chain.step(pool.memset(ones_m[:, 1, :], 1.0 / CV))
            chain.step(pool.memset(eps_c[:, 0:1], EPS))
            chain.step(pool.memset(eps_c[:, 1:2], 4 * LN_EPS))
            chain.link(pool.memset(masks[:, :, :], 0.0))
            pool.affine_select(out=ident[:, :], in_=ident[:, :], compare_op=ALU.not_equal, fill=1.0, base=0,
                               pattern=[[-1, P]], channel_multiplier=1).then_inc(consts, 1)
            for l, b in enumerate(LEVELS):
                v = masks[:, l, :].rearrange("p (n two b) -> p n two b", two=2, b=b)[:, :, 1, :]
                chain.link(pool.memset(v, 1.0))
                chain.link(pool.affine_select(out=v, in_=v, compare_op=ALU.is_ge, fill=0.0, base=0,
                                              pattern=[[-2 * b, P // (2 * b)], [0, b]], channel_multiplier=1))
                chain.link(pool.affine_select(out=v, in_=v, compare_op=ALU.is_ge, fill=0.0, base=b - 1,
                                              pattern=[[2 * b, P // (2 * b)], [0, b]], channel_multiplier=-1))
            pool.wait_ge(x_new, KT)
            pool.wait_ge(mod_summed, 2)
            pool.wait_ge(par_ready, 1)
            chain.step(pool.memset(hpad[:, :, 0:TAPS - 1], 0.0))
            chain.link(pool.memset(score[0][:, :], 0.0))
            pool.affine_select(out=score[0][:, :], in_=score[0][:, :], compare_op=ALU.is_ge, fill=NEG_BIG, base=0,
                               pattern=[[-1, P]], channel_multiplier=1).then_inc(bias_made, 1)
            taps = [(m, k) for m in range(CVT) for k in range(TAPS)]

            def tap(m, k):
                src, w = hpad[:, m, k:k + TOK], pcol("cv_w", CVT * k + m)
                n = TAPS * m + k
                if k == 0:
                    pool.wait_ge(evac, 6 + 2 * m)
                    g = hpad[:, m, TAPS - 1:]
                    chain.link(pool.tensor_tensor(g, g, cacc[:, m, :], ALU.mult))
                    pool.tensor_scalar(cacc[:, m, :], src, w, pcol("cv_b", m), ALU.mult, ALU.add).then_inc(tapped, 1)
                    return
                tmp = (ssq, rstd)[k % 2][:, :]
                pool.wait_ge(tapped, n - 1)
                pool.tensor_scalar(tmp, src, w, 0.0, ALU.mult, ALU.add).then_inc(weighted, 1)
                pool.wait_ge(weighted, n - m)
                pool.wait_ge(tapped, n)
                pool.tensor_tensor(cacc[:, m, :], cacc[:, m, :], tmp, ALU.add).then_inc(tapped, 1)

            for u in range(N_IN):
                if u == 5:
                    for b in range(1, TT):
                        pool.wait_ge(score_added, IDX_HEADS * b)
                        d = score[b][:, b * P:(b + 1) * P]
                        pool.affine_select(out=d, in_=d, compare_op=ALU.is_ge, fill=NEG_BIG, base=0,
                                           pattern=[[-1, P]], channel_multiplier=1).then_inc(diag_made, 1)
                if u >= 9:
                    for _ in range(4):
                        if taps:
                            tap(*taps.pop(0))
                if u in (U_Q + 1, U_Q + 2, U_Q + 3, U_Q + 4):
                    h = u - U_Q - 1
                    pool.wait_ge(evac, 17 + h)
                    pool.tensor_tensor(hq[:, h, :], hq[:, h, :], hk[:, h, :], ALU.mult).then_inc(q_made, 1)
                if u == 21:
                    for b in range(1, TT):
                        pool.wait_ge(taken_made, b)
                        d = score[b][:, b * P:(b + 1) * P]
                        pool.affine_select(out=d, in_=d, compare_op=ALU.is_ge, fill=NEG_BIG, base=0,
                                           pattern=[[-1, P]], channel_multiplier=1).then_inc(bias_made, 1)
            for h in range(HG_HEADS):
                pool.wait_ge(evac, 29 + h)
                pool.tensor_tensor(omix[:, h, :], omix[:, h, :], sqb[:, h % 2, :], ALU.mult).then_inc(g_made, 1)
            pool.wait_ge(ws_copied, 1)
            pool.affine_select(out=wcT[:, :, :], in_=wcT[:, :, :], compare_op=ALU.is_ge, fill=0.0, base=0,
                               pattern=[[0, A_GROUPS], [1, P]], channel_multiplier=-1).then_inc(ws_masked, 1)
            for half in range(2):
                with pool.Fori(0, 4) as i:
                    for cc in range(2):
                        c = 8 * half + cc
                        pool.wait_ge(u_gelu, c + 1 + 2 * i)
                        pool.wait_ge(ug_made, c + 1 + 2 * i)
                        pool.tensor_tensor(e0[:, cc, :], e0[:, cc, :], e1[:, cc, :], ALU.mult).then_inc(ugp_made, 1)
            pool.wait_ge(x_new, X_BO)

            def load_gates(cc, i):
                for n, name in enumerate(("b_gate_a_w_2", "b_gate_x_w_2")):
                    w = a[name][0][bass.ds(i * 2 + cc, 1), :, :].rearrange("h i j -> (h i) j")
                    pool.dma_start(gw[:, cc, n, :], w).then_inc(gw_in[cc], 16)

            def gated(i):
                for cc in range(2):
                    pool.wait_ge(evac, E_RG + (4, 7)[cc] + 8 * i)
                    pool.tensor_tensor(t_i[:, cc, :], t_i[:, cc, :], xc[:, cc, :], ALU.mult).then_inc(ix_made, 1)
                    pool.wait_ge(evac, E_RG + (5, 8)[cc] + 8 * i)
                    pool.tensor_tensor(t_g[:, cc, :], t_g[:, cc, :], t_sg[:, cc, :], ALU.mult).then_inc(gg_made, 1)

            load_gates(0, 0)
            load_gates(1, 0)
            with pool.Fori(0, B_HEADS // 2 - 1) as i:
                gated(i)
                for cc in range(2):
                    pool.wait_ge(gates_made, 2 * i + cc + 1)
                    load_gates(cc, i + 1)
            gated(B_HEADS // 2 - 1)


_INS = [
    "x", "c", "ada_w", "ada_b", "norm_mix_w", "norm_mlp_w", "w_in", "hg_lb_logits", "hg_onorm_w", "cv_w", "cv_b",
    "cv_ln_w", "cv_ln_b", "w_out", "mlp_w1", "mlp_w2", "final_norm_w", "norm_w_2", "a_w_in_2", "a_ln_w_2",
    "a_ln_b_2", "a_w_s_2", "a_b_s_2", "a_w_out_2", "b_w_in_2", "b_conv_w_2", "b_conv_b_2", "b_gate_a_w_2",
    "b_gate_a_b_2", "b_gate_x_w_2", "b_gate_x_b_2", "b_lambda_2", "b_w_out_2", "norm_f_w_2",
]


def program(nc, shapes):
    a = {n: nc.dram_tensor(f"in_{n}", s, F32, kind="ExternalInput").ap() for n, s in shapes.items()}
    out = nc.dram_tensor("out_0", (1, TOK, D), F32, kind="ExternalOutput").ap()
    build(nc, a, out)


def kernel(**inputs):
    import concourse.bacc as bacc
    import numpy as np
    from concourse.bass_utils import run_bass_kernel_spmd

    nc = bacc.Bacc("TRN2", target_bir_lowering=False, num_devices=1)
    arrays = {n: np.ascontiguousarray(inputs[n]) for n in _INS}
    program(nc, {n: v.shape for n, v in arrays.items()})
    r = run_bass_kernel_spmd(nc, [{f"in_{n}": v for n, v in arrays.items()}], core_ids=[0])
    return r.results[0]["out_0"]
```

```python
from contextlib import ExitStack

import concourse.bass as bass
from concourse import mybir

P = 128
ALU = mybir.AluOpType
ACT = mybir.ActivationFunctionType
F32 = mybir.dt.float32
F32R = mybir.dt.float32r
I32 = mybir.dt.int32
AX_X = mybir.AxisListType.X

TOK = 512
D = 1024
KT = D // P
TT = TOK // P
HG_HEADS, HG_D = 4, 128
SA_HEADS, SA_D = 4, 64
IDX_HEADS, IDX_D = 8, 32
TOPK = 128
CV, TAPS = 256, 31
CVT = CV // P
A_WIDTH, A_GROUPS = 2048, 8
AT = A_WIDTH // P
B_WIDTH, B_HEADS, B_TAPS = 1536, 12, 4
EPS, LN_EPS, RG_C = 1e-6, 1e-5, 8.0
NEG_BIG, TINY, TAKEN = -1e30, 1e-30, -3e38
GELU_C, GELU_A = 0.7978845608028654, 0.044715

C_HQ, C_HF, C_HI, C_HG = 0, 512, 1024, 1536
C_SQ, C_SK, C_SV, C_IQ, C_IK, C_IW, C_CU = 2048, 2304, 2560, 2816, 3072, 3104, 3112

RING = 4
LEAD = 3
UNIT = 1024


def ada_unit(group, kt):
    return ("ada", group, kt)


W_IN_UNITS = (
    [("fm", C_IQ), ("fm", C_IQ + P), ("ik", C_IK), ("iw", C_IW)]
    + [("fm", C_CU + P * m + CV * s) for m in range(CVT) for s in range(2)]
    + [("fm", C_HQ + P * h) for h in range(HG_HEADS)]
    + [("fm", C_HF + P * h) for h in range(HG_HEADS)]
    + [("fm", C_SK), ("fm", C_SK + P), ("fm", C_SQ), ("fm", C_SQ + P)]
    + [("tm4", C_SV, kq) for kq in range(2)]
    + [("tm2", C_HI, kp) for kp in range(4)]
    + [("fm", C_HG + P * h) for h in range(HG_HEADS)]
)
N_IN = len(W_IN_UNITS)

N_ADA = 6 * KT
ADA_GROUPS = (1, 0, 2, 4, 3, 5)
ADA = [ada_unit(g, k) for g in ADA_GROUPS for k in range(KT)]
STREAM = ([ADA[g * KT + k] for k in range(KT) for g in range(2)] + [("w", u) for u in range(N_IN + LEAD)]
          + [ADA[(2 + 2 * side) * KT + n] for n in range(2 * KT) for side in range(2)]
          + [("w", u) for u in range(N_IN + LEAD, N_IN + KT)])
assert N_ADA % RING == 0

U_OUT = N_IN
U_FF = U_OUT + KT
U_V = U_FF + 64
U_UG = U_V + 16
U_B = U_UG + 48
U_BOUT = U_B + 2 * B_HEADS

H_MIX, H_OMIX, H_FF, H_HID, H_SGU, H_Y, H_RG, H_YB = 0, 8, 16, 24, 56, 64, 80, 88
X_OUT, X_FF, X_FIN, X_AO, X_BO = 8, 16, 32, 40, 56
Q_OUT, Q_FF, Q_AO, Q_BO = 8, 16, 24, 32
E_FF, E_V, E_RG = 32, 64, 80
S_FF, S_SGU, S_RG = 8, 16, 24

PARAMS = [
    ("ada_b", 48), ("norm_mix_w", 8), ("norm_mlp_w", 8), ("final_norm_w", 8), ("hg_lb_logits", 4),
    ("hg_onorm_w", 4), ("cv_b", 2), ("cv_ln_w", 2), ("cv_ln_b", 2), ("b_lambda_2", 12), ("norm_f_w_2", 8),
    ("norm_w_2", 16), ("pad0", 6),
    ("cv_w", 62), ("a_ln_w_2", 16), ("a_ln_b_2", 16), ("b_conv_b_2", 12), ("b_gate_a_b_2", 12), ("pad1", 10),
    ("b_gate_x_b_2", 12), ("b_conv_w_2", 48),
]
PCOL = {}
_n = 0
for _name, _rows in PARAMS:
    PCOL[_name] = _n
    _n += _rows
P_TILES = 3
PAR_DMAS = sum(not n.startswith("pad") for n, _ in PARAMS)

NARROW = {W_IN_UNITS.index(("ik", C_IK)): IDX_D, W_IN_UNITS.index(("iw", C_IW)): IDX_HEADS}
U_Q = W_IN_UNITS.index(("fm", C_HQ))
TOP_ROUNDS = {5 + k: 1 + k % 2 for k in range(11)}
LEVEL_STEPS = {16: (0, 1), 17: (2, 3), 18: (4,), 19: (5, 6), 20: (7, 8), 21: (9,), 22: (10, 11), 23: (12, 13),
               24: (14,), 25: (15,)}
U_STATE = 26
assert sum(TOP_ROUNDS.values()) == TOPK // 8
N_ATT = 18
S_ADA = {s: 1 for s in range(16)}
S_COLS = {8: 2, 9: 4, 16: 3, 17: 5}
S_HEADS = (0, 2, 4, 6)
S_MEAN, S_VAR = 7, 10
OMIX_ORDER = (0, 1, 2, 3, 6, 7, 4, 5)
S_OMIX = 12
V0 = 2
assert PCOL["cv_w"] == P and PCOL["b_gate_x_b_2"] == 2 * P


class Chain:

    def __init__(self, eng, sem):
        self.eng, self.sem, self.n = eng, sem, 0

    def step(self, ins):
        ins.then_inc(self.sem, 1)
        self.n = self.n + 1
        return self.n

    def wait(self, value=None):
        self.eng.wait_ge(self.sem, self.n if value is None else value)

    def link(self, ins):
        self.step(ins)
        self.wait()

    def loop(self, i, start, steps, first=0):
        self.n = start + (i - first) * steps if first else start + i * steps


def build(nc, a, out):
    with ExitStack() as ctx:
        def sb(name, shape, dt=F32, where=ctx):
            return where.enter_context(nc.sbuf_tensor(name, shape, dt))

        def sem(name):
            return ctx.enter_context(nc.semaphore(name))

        banks = ctx.enter_context(nc.psum_tensor("banks", [P, 8, TOK], F32))

        xT = sb("xT", [P, KT, TOK])
        h_hi = sb("h_hi", [P, KT, TOK], F32R)
        h_lo = sb("h_lo", [P, KT, TOK], F32R)
        raw = sb("raw", [P, RING, UNIT])
        w_hi = sb("w_hi", [P, RING, UNIT], F32R)
        w_lo = sb("w_lo", [P, RING, UNIT], F32R)
        par = sb("par", [P, P_TILES * P])
        mod = sb("mod", [P, 6 * KT])
        ident = sb("ident", [P, P])
        ones_d = sb("ones_d", [P, P])
        ones1 = sb("ones1", [P, P])
        cT = sb("cT", [P, KT])
        c_act = sb("c_act", [P, KT])
        scale1 = sb("scale1", [P, KT])
        scale4 = sb("scale4", [P, KT])
        scale2 = sb("scale2", [P, KT])
        ssq = sb("ssq", [P, TOK])
        sqb = sb("sqb", [P, 2, TOK])
        rstd = sb("rstd", [P, TOK])
        eps_c = sb("eps_c", [P, 3])
        junk = sb("junk", [P, 1])
        rs = sb("rs", [P, TT])

        def pcol(name, n=0, count=1):
            return par[:, PCOL[name] + n:PCOL[name] + n + count]

        mix = ctx.enter_context(ExitStack())
        omix = sb("omix", [P, KT, TOK], F32, mix)
        masks = sb("masks", [P, 7, P], F32, mix)
        ones_m = sb("ones_m", [P, 2, P], F32, mix)
        hf = sb("hf", [P, HG_HEADS, TOK], F32, mix)
        hq = sb("hq", [P, HG_HEADS, TOK], F32, mix)
        hk = sb("hk", [P, HG_HEADS, TOK], F32, mix)
        hv = sb("hv", [P, TT, HG_HEADS * HG_D], F32, mix)
        iw = sb("iw", [P, TT, IDX_HEADS], F32, mix)
        lbt = sb("lbt", [P, 4, HG_HEADS], F32, mix)
        col = sb("col", [P, 8], F32, mix)
        m8 = sb("m8", [P, 3, 8], F32, mix)
        start = ExitStack()
        x_tok = sb("x_tok", [P, TT, D], F32, start)
        row1 = sb("row1", [1, UNIT], F32, start)
        acc1 = sb("acc1", [P, UNIT], F32, start)
        par_rows = sb("par_rows", [P, P_TILES, P], F32, start)
        start.close()
        dsa = ExitStack()
        hpad = sb("hpad", [P, CVT, TAPS - 1 + TOK], F32, dsa)
        cacc = sb("cacc", [P, CVT, TOK], F32, dsa)
        sqT = sb("sqT", [P, 2, TOK], F32, dsa)
        skT = sb("skT", [P, 2, TOK], F32, dsa)
        sv = sb("sv", [P, TT, SA_HEADS * SA_D], F32, dsa)
        score = [sb(f"score{b}", [P, P * (b + 1)], F32, dsa) for b in range(TT)]
        ring2 = sb("ring2", [P, 2, TOK], F32, dsa)
        pT = sb("pT", [P, 2, TOK], F32, dsa)
        hgt = sb("hgt", [P, HG_HEADS, TOK - 4], F32, dsa)
        idx = ExitStack()
        iqT = sb("iqT", [P, 2, TOK], F32, idx)
        ikT = sb("ikT", [P, TOK], F32, idx)
        idx.close()
        hS = sb("hS", [P, 3, HG_HEADS, P], F32, dsa)
        dsa.close()
        mix.close()
        ff = ExitStack()
        hid_hi = sb("hid_hi", [P, 16, TOK], F32R, ff)
        hid_lo = sb("hid_lo", [P, 16, TOK], F32R, ff)
        relu = sb("relu", [P, 2, TOK], F32, ff)
        relu2 = sb("relu2", [P, 2, TOK], F32, ff)
        ff.close()
        sg = ExitStack()
        y_hi = sb("y_hi", [P, 8, TOK], F32R, sg)
        y_lo = sb("y_lo", [P, 8, TOK], F32R, sg)
        vt = sb("vt", [P, TT, A_WIDTH], F32, sg)
        vh = sb("vh", [P, 2, TT, P], F32, sg)
        ws = sb("ws", [P, A_GROUPS, P], F32, sg)
        wcT = sb("wcT", [P, A_GROUPS, P], F32, sg)
        wsum = sb("wsum", [P, A_GROUPS, P], F32, sg)
        bsp = sb("bsp", [P, A_GROUPS, P], F32, sg)
        e0 = sb("e0", [P, 2, TOK], F32, sg)
        e1 = sb("e1", [P, 2, TOK], F32, sg)
        e2 = sb("e2", [P, 2, TOK], F32, sg)
        eb = sb("eb", [P, 2, P], F32, sg)
        vst = sb("vst", [P, TT, 4, 6], F32, sg)
        vmv = sb("vmv", [P, TT, 2], F32, sg)
        vrs = sb("vrs", [P, TT], F32, sg)
        lnw2 = sb("lnw2", [P, AT], F32, sg)
        sg.close()
        rg = ExitStack()
        yb_hi = sb("yb_hi", [P, B_HEADS, TOK], F32R, rg)
        yb_lo = sb("yb_lo", [P, B_HEADS, TOK], F32R, rg)
        xbp = sb("xbp", [P, 2, B_TAPS + TOK], F32, rg)
        gw = sb("gw", [P, 2, 2, P], F32, rg)
        xc, t_r, t_i, t_sg, t_g, t_a, t_s, t_b = [sb(n, [P, 2, TOK], F32, rg) for n in
                                                  ("xc", "t_r", "t_i", "t_sg", "t_g", "t_a", "t_s", "t_b")]
        spt = sb("spt", [P, 5, B_HEADS], F32, rg)
        rg.close()
        y_tok = sb("y_tok", [P, TT, D])

        raw_in = [sem(f"raw_in{i}") for i in range(RING)]
        split_hi = sem("split_hi")
        split_lo = sem("split_lo")
        w_used = sem("w_used")
        evac = sem("evac")
        x_new = sem("x_new")
        h_scaled = sem("h_scaled")
        h_hi_made = sem("h_hi_made")
        h_ready = sem("h_ready")
        sq_made, sq_added = sem("sq_made"), sem("sq_added")
        stat_made, root_made = sem("stat_made"), sem("root_made")
        ada_used, ada_dve, ada_pool, ada_mult = sem("ada_used"), sem("ada_dve"), sem("ada_pool"), sem("ada_mult")
        rows_read, kt_turned = sem("rows_read"), sem("kt_turned")
        mod_summed, mod_ready = sem("mod_summed"), sem("mod_ready")
        s_dve, s_act, s_pool = sem("s_dve"), sem("s_act"), sem("s_pool")
        c_in, x_in, par_in, consts = sem("c_in"), sem("x_in"), sem("par_in"), sem("consts")
        c_sig, c_ready, par_turned, par_ready = sem("c_sig"), sem("c_ready"), sem("par_turned"), sem("par_ready")
        x_turned, lb_zero, lb_exp = sem("x_turned"), sem("lb_zero"), sem("lb_exp")
        s_made, s_read, score_added = sem("s_made"), sem("s_read"), sem("score_added")
        diag_made, taken_made, bias_made = sem("diag_made"), sem("taken_made"), sem("bias_made")
        l_made, l_read, mx_made, e_made = sem("l_made"), sem("l_read"), sem("mx_made"), sem("e_made")
        p_made, p_turned, pt_read = sem("p_made"), sem("p_turned"), sem("pt_read")
        pv_made, ob_made, oc_made, oa_made = sem("pv_made"), sem("ob_made"), sem("oc_made"), sem("oa_made")
        weighted, tapped, mean_made, cen_made = sem("weighted"), sem("tapped"), sem("mean_made"), sem("cen_made")
        csq_made, var_made, croot_made = sem("csq_made"), sem("var_made"), sem("croot_made")
        cn_made, csig_made = sem("cn_made"), sem("csig_made")
        q_made, g_made, f_made = sem("q_made"), sem("g_made"), sem("f_made")
        lev_made, upd_made = sem("lev_made"), sem("upd_made")
        kt_made, sp_made, st_made = sem("kt_made"), sem("sp_made"), sem("st_made")
        o_made, osq_made, om_made, oroot_made = sem("o_made"), sem("osq_made"), sem("om_made"), sem("oroot_made")

        sq1_made, sq2_added = sem("sq1_made"), sem("sq2_added")
        rs_ready, y2_made = sem("rs_ready"), sem("y2_made")
        mean2_made, iw_turned, iw_made = sem("mean2_made"), sem("iw_turned"), sem("iw_made")
        ssq_zero, relu_sq, v_gelu, wsum_made = sem("ssq_zero"), sem("relu_sq"), sem("v_gelu"), sem("wsum_made")
        u_aff, u_gelu, eb_made, s_mixed = sem("u_aff"), sem("u_gelu"), sem("eb_made"), sem("s_mixed")
        tap_made, a1_made, a_made, mult_made = sem("tap_made"), sem("a1_made"), sem("a_made"), sem("mult_made")
        bt_made, scanned = sem("bt_made"), sem("scanned")

        bs_in, ws_in, ws_turned, ws_copied = sem("bs_in"), sem("ws_in"), sem("ws_turned"), sem("ws_copied")
        ws_masked, ws_summed = sem("ws_masked"), sem("ws_summed")
        v_copied, v_aff, v_inner, v_tanh, v_stat = sem("v_copied"), sem("v_aff"), sem("v_inner"), sem("v_tanh"), sem("v_stat")
        v_var, v_root, vh_made, mixed = sem("v_var"), sem("v_root"), sem("vh_made"), sem("mixed")
        u_sq, u_inner, u_tanh, g_sig = sem("u_sq"), sem("u_inner"), sem("u_tanh"), sem("g_sig")
        ug_made, ugp_made, y_out = sem("ug_made"), sem("ugp_made"), sem("y_out")
        gw_in, gates_made, xc_made = [sem("gw_in0"), sem("gw_in1")], sem("gates_made"), sem("xc_made")
        sp_abs, sp_exp, sp_ready = sem("sp_abs"), sem("sp_exp"), sem("sp_ready")
        pad_zero, rt_made, ra_made, rs_made = sem("pad_zero"), sem("rt_made"), sem("ra_made"), sem("rs_made")
        ix_made, gg_made, yb_out = sem("ix_made"), sem("gg_made"), sem("yb_out")
        fin_scaled, fin_turned, y_made, out_done = sem("fin_scaled"), sem("fin_turned"), sem("y_made"), sem("out_done")

        arrival = {item: d for d, item in enumerate(STREAM)}

        def raw_index(u):
            return arrival[("w", u)] if u < U_FF else u + N_ADA

        def raw_wait(eng, d):
            eng.wait_ge(raw_in[d % RING], 16 * (d // RING + 1))

        def copies(slot, n):
            return slot.rearrange("p (k r n) -> p k r n", k=KT, n=n)

        def repeated(slot, n):
            return slot[:, 0:KT * n].rearrange("p (k n) -> p k n", n=n).unsqueeze(2).broadcast_to([P, KT, P // n, n])

        def hi_unit(act, u, i=0):
            d = raw_index(u)
            act.wait_ge(raw_in[d % RING], 16 * (d // RING + 1) + 16 * i)
            if u >= RING:
                act.wait_ge(w_used, u - RING + 1 + RING * i)
            src, dst = raw[:, d % RING, :], w_hi[:, u % RING, :]
            if u in NARROW:
                src, dst = repeated(src, NARROW[u]), copies(dst, NARROW[u])
            act.activation(dst, src, ACT.Copy).then_inc(split_hi, 1)

        def lo_unit(dve, u, i=0):
            d = raw_index(u)
            dve.wait_ge(split_hi, u + 1 + RING * i)
            src, hi, dst = raw[:, d % RING, :], w_hi[:, u % RING, :].bitcast(F32), w_lo[:, u % RING, :]
            if u in NARROW:
                n = NARROW[u]
                src, hi, dst = repeated(src, n), copies(hi, n), copies(dst, n)
            dve.tensor_tensor(dst, src, hi, ALU.subtract).then_inc(split_lo, 1)

        def unit(ring, u, n):
            return ring[:, u % RING, :].rearrange("p (k n) -> p k n", n=n)

        def three(pe, dst, l_hi, l_lo, r_hi, r_lo, first, last):
            pe.matmul(dst, l_hi, r_hi, start=first, stop=False)
            pe.matmul(dst, l_hi, r_lo, start=False, stop=False)
            return pe.matmul(dst, l_lo, r_hi, start=False, stop=last)

        LEVELS = [1, 2, 4, 8, 16, 32, 64]
        T_OFF = {2: 0, 4: 256, 8: 384, 16: 448, 32: 480, 64: 496, 128: 504}

        hA = omix[:, 0:HG_HEADS, :].rearrange("p h (c i) -> p h c i", i=P)
        hKT = ring2[:, :, :].rearrange("p c (h k) -> p c h k", k=P)

        def t_level(b, p):
            if b == 1:
                v = hf[:, 2 * p:2 * p + 2, :]
            else:
                v = hgt[:, 2 * p:2 * p + 2, T_OFF[b]:T_OFF[b] + TOK // b]
            return v.rearrange("p h (n two) -> p h n two", two=2)

        def halves(buf, b, p):
            return buf[:, 2 * p:2 * p + 2, :].rearrange("p h (n two b) -> p h n two b", two=2, b=b)

        block = ctx.enter_context(nc.Block())

        @block.sync
        def _(sp):
            w_in = a["w_in"][0]
            for t in range(TT):
                sp.dma_start(x_tok[:, t, :], a["x"][0, t * P:(t + 1) * P, :]).then_inc(x_in, 16)
            for d, item in enumerate(STREAM):
                if d >= RING:
                    before = STREAM[d - RING]
                    if before[0] == "w":
                        sp.wait_ge(split_lo, before[1] + 1)
                    elif before[1] == ADA_GROUPS[1]:
                        sp.wait_ge(ada_dve, before[2] + 1)
                    elif before[1] in ADA_GROUPS[4:]:
                        sp.wait_ge(ada_pool, ADA.index(before) + 1 - 4 * KT)
                    else:
                        n = ADA.index(before)
                        sp.wait_ge(ada_used, n + 1 if n < KT else n + 1 - KT)
                dst = raw[:, d % RING, :]
                if item[0] == "ada":
                    _, g, kt = item
                    src = a["ada_w"][0, kt * P:(kt + 1) * P, g * D:(g + 1) * D]
                elif item[1] >= N_IN:
                    c = (item[1] - N_IN) * P
                    dst = dst.rearrange("p (k n) -> p k n", n=P)
                    src = a["w_out"][0][:, c:c + P].rearrange("(k p) n -> p k n", p=P)
                else:
                    kind = W_IN_UNITS[item[1]]
                    c = kind[1]
                    if kind[0] == "fm":
                        dst = dst.rearrange("p (k n) -> p k n", n=P)
                        src = w_in[:, c:c + P].rearrange("(k p) n -> p k n", p=P)
                    elif kind[0] == "ik":
                        dst = dst[:, 0:KT * IDX_D].rearrange("p (k n) -> p k n", n=IDX_D)
                        src = w_in[:, c:c + IDX_D].rearrange("(k p) n -> p k n", p=P)
                    elif kind[0] == "iw":
                        dst = dst[:, 0:KT * IDX_HEADS].rearrange("p (k n) -> p k n", n=IDX_HEADS)
                        src = w_in[:, c:c + IDX_HEADS].rearrange("(k p) n -> p k n", p=P)
                    elif kind[0] == "tm4":
                        dst = dst.rearrange("p (k n) -> p k n", n=256)
                        src = w_in[4 * P * kind[2]:4 * P * (kind[2] + 1), c:c + 256].rearrange("(k p) n -> p k n", p=P)
                    else:
                        dst = dst.rearrange("p (k n) -> p k n", n=512)
                        src = w_in[2 * P * kind[2]:2 * P * (kind[2] + 1), c:c + 512].rearrange("(k p) n -> p k n", p=P)
                sp.dma_start(dst, src).then_inc(raw_in[d % RING], 16)

            def stream(base, count, source):
                with sp.Fori(0, count // RING) as i:
                    for j in range(RING):
                        u = base + j
                        sp.wait_ge(split_lo, u - RING + 1 + RING * i)
                        src, n = source(i, j)
                        kt = src.shape[1]
                        sp.dma_start(raw[:, u % RING, 0:kt * n].rearrange("p (k n) -> p k n", n=n), src)\
                          .then_inc(raw_in[u % RING], 16)

            def rows(w, r0, r1):
                return w[r0:r1, :].rearrange("(k p) n -> p k n", p=P)

            w1, w2 = a["mlp_w1"][0], a["mlp_w2"][0]
            for half in range(2):
                stream(U_FF + 32 * half, 16,
                       lambda i, j: (rows(w1, 0, D)[:, :, bass.ds(i * 4 * P + (16 * half + j) * P, P)], P))
                stream(U_FF + 32 * half + 16, 16,
                       lambda i, j: (rows(w2, (16 * half + 8 * (j % 2)) * P, (16 * half + 8 * (j % 2) + 8) * P)
                                     [:, :, bass.ds(i * 2 * P + (j // 2) * P, P)], P))
            wa = a["a_w_in_2"][0]
            stream(U_V, 16, lambda i, j: (rows(wa, 2 * P * j, 2 * P * (j + 1))[:, :, bass.ds(i * 512 + A_WIDTH, 512)], 512))
            wo = a["a_w_out_2"][0]
            for half in range(2):
                stream(U_UG + 24 * half, 16,
                       lambda i, j: (rows(wa, 0, D)[:, :, bass.ds(i * 2 * P + (8 * half + j // 2) * P
                                                                   + 2 * A_WIDTH * (j % 2), P)], P))
                stream(U_UG + 24 * half + 16, 8,
                       lambda i, j: (rows(wo, half * D, (half + 1) * D)[:, :, bass.ds(i * 4 * P + j * P, P)], P))
            wb = a["b_w_in_2"][0]
            stream(U_B, 2 * B_HEADS, lambda i, j: (rows(wb, 0, D)[:, :, bass.ds(i * 2 * P + (j // 2) * P + B_WIDTH * (j % 2), P)], P))
            wbo = a["b_w_out_2"][0]
            stream(U_BOUT, 16, lambda i, j: (rows(wbo, 6 * (j % 2) * P, (6 * (j % 2) + 6) * P)
                                             [:, :, bass.ds(i * 2 * P + (j // 2) * P, P)], P))
            for t in range(TT):
                sp.wait_ge(y_made, t + 1)
                sp.wait_ge(y2_made, t + 1)
                sp.dma_start(out[0, t * P:(t + 1) * P, :], y_tok[:, t, :]).then_inc(out_done, 16)
            sp.wait_ge(out_done, 16 * TT)

        @block.tensor
        def _(pe):
            def ada_product(n):
                g, kt = n // KT, n % KT
                d = arrival[ADA[n if n < KT else n + KT]]
                raw_wait(pe, d)
                if n == 0:
                    pe.wait_ge(c_ready, 1)
                if n == KT:
                    pe.wait_ge(mod_ready, 2)
                    pe.wait_ge(evac, 32)
                if g and kt == 0:
                    pe.wait_ge(rows_read, g)
                for half in range(2):
                    last = pe.matmul(banks[0:1, (0 if g else 5) + half, :], c_act[:, kt:kt + 1],
                                     raw[:, d % RING, 512 * half:512 * (half + 1)], start=(kt == 0), stop=(kt == KT - 1))
                last.then_inc(ada_used, 1)

            def row_columns(row, bank):
                for j in range(KT):
                    c = row(j)
                    last = pe.matmul(banks[:, bank, j:j + 1], c, ones1[0:c.shape[0], 0:1], start=True, stop=True)
                last.then_inc(mod_summed, 1)

            def later_columns(n, place):
                pe.wait_ge(oroot_made, HG_HEADS)
                if n > 2:
                    pe.wait_ge(mod_ready, n)
                if place < 4:
                    pe.wait_ge(rows_read, place)
                    row_columns(lambda j: sqb[0:1, j // 4, (j % 4) * P:(j % 4 + 1) * P], 3)
                else:
                    pe.wait_ge(ada_pool, KT * (place - 3))
                    row_columns(lambda j: hgt[:, j // 2, (j % 2) * P:(j % 2 + 1) * P], 3)

            def stat(n, q):
                pe.wait_ge(sq_added, q)
                pe.matmul(banks[:, 7, :], ones_d[:, :], ssq[:, :], start=True, stop=True).then_inc(stat_made, 1)

            pe.wait_ge(consts, 1)
            pe.wait_ge(x_in, 16 * TT)
            for m in range(KT):
                if m >= 4:
                    pe.wait_ge(x_new, m - 3)
                for t in range(TT):
                    last = pe.transpose(banks[:, m % 4, t * P:(t + 1) * P], x_tok[:, t, m * P:(m + 1) * P], ident[:, :])
                last.then_inc(x_turned, 1)
                if m >= 4:
                    ada_product(m - 4)
            ada_product(4)
            pe.wait_ge(par_in, PAR_DMAS * 16)
            for t in range(P_TILES):
                last = pe.transpose(banks[:, 4, t * P:(t + 1) * P], par_rows[:, t, :], ident[:, :])
            last.then_inc(par_turned, 1)
            ada_product(5)
            stat(1, KT)
            for n in range(6, KT):
                ada_product(n)
            pe.wait_ge(ada_dve, KT)
            pe.wait_ge(x_new, KT)
            for j in range(KT):
                last = pe.matmul(banks[:, 3, j:j + 1], acc1[:, j * P:(j + 1) * P], ones1[:, 0:1], start=True, stop=True)
            last.then_inc(mod_summed, 1)
            pe.wait_ge(rows_read, 1)
            pe.wait_ge(par_ready, 1)
            row_columns(lambda j: row1[0:1, j * P:(j + 1) * P], 4)

            n_out = [0]

            def free_banks(n):
                if n == 3:
                    pe.wait_ge(mod_ready, 1)
                if n >= 4:
                    pe.wait_ge(evac, n - 3)

            def in_unit(u):
                kind = W_IN_UNITS[u]
                pe.wait_ge(split_lo, u + 1)
                n = n_out[0]
                if kind[0] in ("fm", "ik", "iw"):
                    free_banks(n)
                    for k in range(KT):
                        if u == 0:
                            pe.wait_ge(h_ready, H_MIX + k + 1)
                        last = three(pe, banks[:, n % 4, :], unit(w_hi, u, P)[:, k, :], unit(w_lo, u, P)[:, k, :],
                                     h_hi[:, k, :], h_lo[:, k, :], k == 0, k == KT - 1)
                    n_out[0] += 1
                else:
                    per, width = (4, 256) if kind[0] == "tm4" else (2, 512)
                    part = kind[2]
                    if part == 0:
                        free_banks(n + 3)
                    for t in range(TT):
                        for kk in range(per):
                            k = per * part + kk
                            last = three(pe, banks[:, t, 0:width],
                                         h_hi[:, k, t * P:(t + 1) * P], h_lo[:, k, t * P:(t + 1) * P],
                                         unit(w_hi, u, width)[:, kk, :], unit(w_lo, u, width)[:, kk, :],
                                         k == 0, k == KT - 1)
                    if part == KT // per - 1:
                        n_out[0] += 4
                last.then_inc(w_used, 1)

            def index_scores():
                pe.wait_ge(evac, 4)
                pe.wait_ge(mod_ready, 2)
                for t in range(TT):
                    last = pe.transpose(banks[:, 6, t * IDX_HEADS:(t + 1) * IDX_HEADS],
                                        pT[0:IDX_HEADS, 0, t * P:(t + 1) * P], ident[0:IDX_HEADS, 0:IDX_HEADS])
                last.then_inc(iw_turned, 1)
                for s in range(3 * IDX_HEADS):
                    b, h = 1 + s // IDX_HEADS, s % IDX_HEADS
                    if s >= 2:
                        pe.wait_ge(s_read, s - 1)
                    r = slice(IDX_D * (h % 4), IDX_D * (h % 4) + IDX_D)
                    pe.matmul(banks[:, 4 + s % 2, 0:P * (b + 1)], iqT[r, h // 4, b * P:(b + 1) * P],
                              ikT[r, 0:P * (b + 1)], start=True, stop=True).then_inc(s_made, 1)

            def logits(t):
                b, h = t // SA_HEADS, t % SA_HEADS
                if t == 0:
                    pe.wait_ge(evac, 24)
                    pe.wait_ge(upd_made, 16)
                    pe.wait_ge(st_made, 3)
                if t >= 2:
                    pe.wait_ge(l_read, t - 1)
                r = slice(SA_D * (h % 2), SA_D * (h % 2) + SA_D)
                pe.matmul(banks[:, 4 + t % 2, 0:P * (b + 1)], sqT[r, h // 2, b * P:(b + 1) * P],
                          skT[r, h // 2, 0:P * (b + 1)], start=True, stop=True).then_inc(l_made, 1)

            def turn_probs(t):
                b = t // SA_HEADS
                pe.wait_ge(p_made, t + 1)
                if t >= 1:
                    pe.wait_ge(pt_read, t)
                for kb in range(b + 1):
                    last = pe.transpose(banks[:, 6, kb * P:(kb + 1) * P], ring2[:, t % 2, kb * P:(kb + 1) * P], ident[:, :])
                last.then_inc(p_turned, 1)

            def probs_v(t):
                b, h = t // SA_HEADS, t % SA_HEADS
                pe.wait_ge(pt_read, t + 1)
                if t:
                    pe.wait_ge(ob_made, t)
                r = slice(SA_D * (h % 2), SA_D * (h % 2) + SA_D)
                for kb in range(b + 1):
                    last = pe.matmul(banks[r, 7, 0:P], sv[:, kb, h * SA_D:(h + 1) * SA_D], pT[:, t % 2, kb * P:(kb + 1) * P],
                                     start=(kb == 0), stop=(kb == b))
                last.then_inc(pv_made, 1)

            def attention(t):
                if 1 <= t <= 16:
                    turn_probs(t - 1)
                if t < 16:
                    logits(t)
                if 2 <= t <= 17:
                    probs_v(t - 2)

            def level(n):
                l, p = n // 2, n % 2
                if n == 0:
                    pe.wait_ge(f_made, HG_HEADS)
                    pe.wait_ge(q_made, HG_HEADS)
                    pe.wait_ge(s_read, 3 * IDX_HEADS)
                    pe.wait_ge(iw_made, 1)
                if l:
                    pe.wait_ge(upd_made, n - 1)
                for h in (2 * p, 2 * p + 1):
                    for c in range(TT):
                        last = pe.matmul(banks[:, 4 + h, c * P:(c + 1) * P], hk[:, h, c * P:(c + 1) * P],
                                         hq[:, h, c * P:(c + 1) * P], start=True, stop=True)
                last.then_inc(lev_made, 1)

            def turn_keys(c):
                pe.wait_ge(upd_made, 16)
                if c:
                    pe.wait_ge(kt_made, c)
                for h in range(HG_HEADS):
                    last = pe.transpose(banks[:, 4, h * P:(h + 1) * P], hk[:, h, c * P:(c + 1) * P], ident[:, :])
                last.then_inc(kt_turned, 1)

            def state(c):
                pe.wait_ge(kt_made, c + 1)
                pe.wait_ge(evac, 28)
                if c:
                    pe.wait_ge(st_made, c)
                for h in range(HG_HEADS):
                    last = pe.matmul(banks[:, 6, h * P:(h + 1) * P], hKT[:, c % 2, h, :], hv[:, c, h * P:(h + 1) * P],
                                     start=True, stop=True)
                last.then_inc(sp_made, 1)

            for u in range(N_IN):
                in_unit(u)
                if u == 4:
                    index_scores()
                for n in LEVEL_STEPS.get(u, ()):
                    level(n)
                if 0 <= u - 1 - U_STATE < 3:
                    state(u - 1 - U_STATE)
                if 0 <= u - U_STATE < 3:
                    turn_keys(u - U_STATE)

            def recurrence_out(h):
                if h == 0:
                    pe.wait_ge(evac, 32)
                    pe.wait_ge(st_made, 3)
                if h >= 2:
                    pe.wait_ge(oroot_made, h - 1)
                for c in range(TT):
                    o = banks[:, 2 + h % 2, c * P:(c + 1) * P]
                    last = pe.matmul(o, hv[:, c, h * P:(h + 1) * P], hA[:, h, c, :], start=True, stop=(c == 0))
                    if c:
                        last = pe.matmul(o, hS[:, c - 1, h, :], hq[:, h, c * P:(c + 1) * P], start=False, stop=True)
                last.then_inc(o_made, 1)

            def recurrence_mean(h):
                pe.wait_ge(osq_made, h + 1)
                pe.matmul(banks[:, 2 + h % 2, :], ones_m[:, 0, :], hq[:, h, :], start=True, stop=True).then_inc(om_made, 1)

            n_ada = KT
            for s in range(N_ATT):
                attention(s)
                if s in S_HEADS:
                    recurrence_out(S_HEADS.index(s))
                if s - 1 in S_HEADS:
                    recurrence_mean(S_HEADS.index(s - 1))
                if s == S_MEAN:
                    pe.wait_ge(tapped, CVT * TAPS)
                    pe.wait_ge(oroot_made, HG_HEADS - 1)
                    for m in range(CVT):
                        last = pe.matmul(banks[:, 2, :], ones_m[:, 1, :], cacc[:, m, :], start=(m == 0), stop=(m == CVT - 1))
                    last.then_inc(mean_made, 1)
                if s == S_VAR:
                    pe.wait_ge(csq_made, CVT)
                    for m in range(CVT):
                        last = pe.matmul(banks[:, 2, :], ones_m[:, 1, :], hpad[:, m, 0:TOK], start=(m == 0),
                                         stop=(m == CVT - 1))
                    last.then_inc(var_made, 1)
                if s in S_COLS:
                    later_columns(2 + list(S_COLS).index(s), S_COLS[s])
                for _ in range(S_ADA.get(s, 0)):
                    ada_product(n_ada)
                    n_ada += 1

            def residual_product(i, base, units, nk, src_hi, src_lo, x0, ready=None, order=None):
                for j in range(RING):
                    u = base + j
                    t = j // units
                    pe.wait_ge(split_lo, u + 1 + RING * i)
                    if j % units == 0:
                        pe.wait_ge(x_new, x0 + t - 1 + (RING // units) * i)
                    for n in range(nk):
                        k = order[n] if order else n
                        nn, kk = (j % units) * nk + n, (j % units) * nk + k
                        if ready is not None and t == 0:
                            pe.wait_ge(h_ready, ready + nn + 1)
                        last = three(pe, banks[:, t, :], unit(w_hi, u, P)[:, k, :], unit(w_lo, u, P)[:, k, :],
                                     src_hi[:, kk, :], src_lo[:, kk, :], nn == 0, nn == units * nk - 1)
                    last.then_inc(w_used, 1)

            def residual(base, count, *rest):
                with pe.Fori(0, count // RING) as i:
                    residual_product(i, base, *rest)

            residual(U_OUT, KT, 1, KT, h_hi, h_lo, X_OUT, H_OMIX, OMIX_ORDER)
            stat(2, Q_OUT + KT)

            for half in range(2):
                pe.wait_ge(x_new, X_FF + KT * half)
                with pe.Fori(0, 4) as i:
                    for j in range(RING):
                        u = U_FF + 32 * half + j
                        pe.wait_ge(split_lo, u + 1 + RING * i)
                        pe.wait_ge(evac, E_FF + 16 * half + j - 1 + RING * i)
                        for k in range(KT):
                            if half == 0 and j == 0:
                                pe.wait_ge(h_ready, H_FF + k + 1)
                            last = three(pe, banks[:, j, :], unit(w_hi, u, P)[:, k, :], unit(w_lo, u, P)[:, k, :],
                                         h_hi[:, k, :], h_lo[:, k, :], k == 0, k == KT - 1)
                        last.then_inc(w_used, 1)
                pe.wait_ge(evac, E_FF + 16 * (half + 1) - 2)
                residual(U_FF + 32 * half + 16, 16, 2, KT, hid_hi, hid_lo, X_FF + KT * half, H_HID + 16 * half)
            stat(3, Q_FF + KT)
            pe.wait_ge(sq2_added, 2 + KT)
            pe.matmul(banks[:, 6, :], ones_d[:, :], relu2[:, 0, :], start=True, stop=True).then_inc(stat_made, 1)

            pe.wait_ge(ws_in, 16)
            for g in range(A_GROUPS):
                last = pe.transpose(banks[:, 4 + g // 4, (g % 4) * P:(g % 4 + 1) * P], ws[:, g, :], ident[:, :])
            last.then_inc(ws_turned, 1)
            with pe.Fori(0, 4 // 2) as i:
                for cl in range(2):
                    pe.wait_ge(evac, E_V + 4 * (cl - 1) + 8 * i)
                    if cl == 1:
                        pe.wait_ge(ws_copied, 1)
                    for j in range(4):
                        u = U_V + 4 * cl + j
                        pe.wait_ge(split_lo, u + 1 + 8 * i)
                        if cl == 0:
                            pe.wait_ge(h_ready, H_SGU + 2 * j + 2)
                        for t in range(TT):
                            for kk in range(2):
                                k = 2 * j + kk
                                last = three(pe, banks[:, 4 * cl + t, :],
                                             h_hi[:, k, t * P:(t + 1) * P], h_lo[:, k, t * P:(t + 1) * P],
                                             unit(w_hi, u, 512)[:, kk, :], unit(w_lo, u, 512)[:, kk, :],
                                             k == 0, k == KT - 1)
                        last.then_inc(w_used, 1)
            pe.wait_ge(evac, E_V + 12)
            pe.wait_ge(ws_masked, 1)
            for g in range(2):
                last = pe.matmul(banks[:, 2 + g, :], ones1[:, :], wcT[:, 4 * g:4 * g + 4, :].rearrange("p g t -> p (g t)"),
                                 start=True, stop=True)
            last.then_inc(ws_summed, 1)
            for half in range(2):
                pe.wait_ge(x_new, X_AO + KT * half)
                with pe.Fori(0, 4) as i:
                    for cc in range(2):
                        pe.wait_ge(h_ready, H_Y + 8 * half + cc - 1 + 2 * i)
                        if cc == 1:
                            pe.wait_ge(evac, E_V + 16)
                        for s in range(2):
                            u = U_UG + 24 * half + 2 * cc + s
                            pe.wait_ge(split_lo, u + 1 + RING * i)
                            for k in range(KT):
                                last = three(pe, banks[:, 4 * cc + s, :], unit(w_hi, u, P)[:, k, :],
                                             unit(w_lo, u, P)[:, k, :], h_hi[:, k, :], h_lo[:, k, :],
                                             k == 0, k == KT - 1)
                            last.then_inc(w_used, 1)
                        pe.wait_ge(vh_made, 8 * half + cc + 1 + 2 * i)
                        pe.wait_ge(wsum_made, 2)
                        for t in range(TT):
                            last = pe.matmul(banks[:, 4 * cc + 2, t * P:(t + 1) * P], vh[:, cc, t, :],
                                             wcT[:, bass.ds(i + 4 * half, 1), :].rearrange("p g t -> p (g t)"),
                                             start=True, stop=True)
                        last.then_inc(mixed, 1)
                pe.wait_ge(h_ready, H_Y + 8 * half + 7)
                residual(U_UG + 24 * half + 16, KT, 1, KT, y_hi, y_lo, X_AO + KT * half, H_Y + 8 * half)
            stat(5, Q_AO + KT)

            pe.wait_ge(x_new, X_BO)
            with pe.Fori(0, B_HEADS // 2) as i:
                def project(j, dst, read):
                    u = U_B + j
                    pe.wait_ge(split_lo, u + 1 + RING * i)
                    pe.wait_ge(evac, E_RG + read - 8 + 8 * i)
                    for k in range(KT):
                        if j == 0:
                            pe.wait_ge(h_ready, H_RG + k + 1)
                        last = three(pe, banks[:, dst, :], unit(w_hi, u, P)[:, k, :], unit(w_lo, u, P)[:, k, :],
                                     h_hi[:, k, :], h_lo[:, k, :], k == 0, k == KT - 1)
                    last.then_inc(w_used, 1)

                def gates(cc, read):
                    pe.wait_ge(gw_in[cc], 32 + 32 * i)
                    pe.wait_ge(evac, E_RG + read - 8 + 8 * i)
                    pe.wait_ge(xc_made, cc + 1 + 2 * i)
                    pe.matmul(banks[:, 4 * cc + 2, :], gw[:, cc, 0, :], xc[:, cc, :], start=True, stop=True)
                    pe.matmul(banks[:, 4 * cc + 3, :], gw[:, cc, 1, :], xc[:, cc, :], start=True, stop=True)\
                      .then_inc(gates_made, 1)

                project(0, 0, 1)
                project(1, 1, 5)
                project(2, 4, 2)
                gates(0, 4)
                project(3, 5, 8)
                gates(1, 8)
            pe.wait_ge(evac, E_RG + 4 * B_HEADS)
            pe.wait_ge(h_ready, H_YB + B_HEADS - 2)
            def part(j, t, k0, k1):
                for k in range(k0, k1):
                    kk = (j % 2) * 6 + k
                    last = three(pe, banks[:, t, :], unit(w_hi, U_BOUT + j, P)[:, k, :], unit(w_lo, U_BOUT + j, P)[:, k, :],
                                 yb_hi[:, kk, :], yb_lo[:, kk, :], kk == 0, kk == 11)
                return last

            pe.wait_ge(split_lo, U_BOUT + 3)
            part(0, 0, 0, 6).then_inc(w_used, 1)
            part(2, 1, 0, 6)
            part(1, 0, 0, 4)
            pe.wait_ge(h_ready, H_YB + B_HEADS)
            part(1, 0, 4, 6).then_inc(w_used, 1)
            pe.wait_ge(split_lo, U_BOUT + 4)
            part(3, 1, 0, 1).then_inc(w_used, 1)
            part(3, 1, 1, 6).then_inc(w_used, 1)
            with pe.Fori(1, 4) as i:
                residual_product(i, U_BOUT, 2, 6, yb_hi, yb_lo, X_BO)
            def turn_back(half, t, k):
                bank = (2, 3, 4, 5, 7, 0, 1, 6)[TT * half + t]
                return pe.transpose(banks[:, bank, k * P:(k + 1) * P], xT[:, 4 * half + k, t * P:(t + 1) * P], ident[:, :])

            for k in range(4):
                pe.wait_ge(fin_scaled, k + 1)
                for t in range(TT):
                    last = turn_back(0, t, k)
            last.then_inc(fin_turned, 1)
            pe.wait_ge(sq_added, Q_BO + KT)
            for t in range(TT):
                last = pe.matmul(banks[:, 6, t:t + 1], ssq[:, t * P:(t + 1) * P], ones_d[:, 0:1], start=True, stop=True)
            last.then_inc(stat_made, 1)
            pe.wait_ge(fin_scaled, KT)
            for t in range(TT):
                if t == 3:
                    pe.wait_ge(root_made, 6)
                for k in range(4):
                    last = turn_back(1, t, k)
                last.then_inc(fin_turned, 1)

        @block.scalar
        def _(act):
            chain = Chain(act, s_act)

            def plain_wait():
                act.wait_ge(consts, 1)

            act.dma_start(cT[:, :], a["c"].rearrange("o (k p) -> p (o k)", p=P), allow_slow_non_contiguous=True)\
               .then_inc(c_in, 16)
            act.wait_ge(c_in, 16)
            act.activation(c_act[:, :], cT[:, :], ACT.Sigmoid).then_inc(c_sig, 1)
            for m in range(KT):
                act.wait_ge(x_turned, m + 1)
                if m >= 2:
                    act.wait_ge(sq_added, m - 1)
                act.activation(sqb[:, m % 2, :], banks[:, m % 4, :], ACT.Square).then_inc(sq_made, 1)
                act.activation(xT[:, m, :], banks[:, m % 4, :], ACT.Copy).then_inc(x_new, 1)

            def root(n):
                chain.link(act.activation(junk[:, :], eps_c[:, 0:1], ACT.Sqrt))
                act.wait_ge(stat_made, n)
                act.activation(rstd[:, :], banks[:, 7, :], ACT.Sqrt, bias=eps_c[:, 0:1]).then_inc(root_made, 1)

            def shifted(n0, shift):
                for k in range(KT):
                    act.wait_ge(h_scaled, n0 + k + 1)
                    if shift is None:
                        act.activation(h_hi[:, k, :], sqb[:, k % 2, :], ACT.Copy).then_inc(h_hi_made, 1)
                    else:
                        act.activation(h_hi[:, k, :], sqb[:, k % 2, :], ACT.Identity,
                                       bias=mod[:, shift + k:shift + k + 1]).then_inc(h_hi_made, 1)

            act.wait_ge(par_turned, 1)
            act.activation(par[:, :], banks[:, 4, 0:P_TILES * P], ACT.Copy).then_inc(par_ready, 1)
            root(1)
            act.wait_ge(lb_zero, 1)
            act.activation(lbt[:, 1, :], lbt[:, 0, :], ACT.Exp).then_inc(lb_exp, 1)
            act.wait_ge(ada_used, KT)
            act.activation(row1[0:1, :].rearrange("p (b n) -> p b n", b=2), banks[0:1, 5:7, :], ACT.Copy)\
               .then_inc(rows_read, 1)
            for u in range(LEAD):
                hi_unit(act, u)
            act.wait_ge(mod_ready, 2)
            shifted(0, 0)

            def read_out(u):
                kind = W_IN_UNITS[u]
                c, n = kind[1], n_out[0]
                if kind[0] in ("tm4", "tm2") and kind[2] != (1 if kind[0] == "tm4" else 3):
                    return
                act.wait_ge(w_used, u + 1)
                if kind[0] == "tm4":
                    for t in range(TT):
                        act.activation(sv[:, t, :], banks[:, t, 0:256], ACT.Copy).then_inc(evac, 1)
                elif kind[0] == "tm2":
                    for t in range(TT):
                        act.activation(hv[:, t, :], banks[:, t, :], ACT.Copy).then_inc(evac, 1)
                elif kind[0] == "iw":
                    act.activation(pT[0:IDX_HEADS, 0, :], banks[0:IDX_HEADS, n % 4, :], ACT.Copy,
                                   scale=float(IDX_HEADS * IDX_D) ** -0.5).then_inc(evac, 1)
                elif kind[0] == "ik":
                    act.activation(ikT[:, :], banks[:, n % 4, :], ACT.Copy).then_inc(evac, 1)
                elif c in (C_IQ, C_IQ + P):
                    act.activation(iqT[:, (c - C_IQ) // P, :], banks[:, n % 4, :], ACT.Copy).then_inc(evac, 1)
                elif c in (C_SQ, C_SQ + P):
                    act.activation(sqT[:, (c - C_SQ) // P, :], banks[:, n % 4, :], ACT.Copy).then_inc(evac, 1)
                elif c in (C_SK, C_SK + P):
                    act.activation(skT[:, (c - C_SK) // P, :], banks[:, n % 4, :], ACT.Copy).then_inc(evac, 1)
                elif c >= C_CU:
                    m, gate = (c - C_CU) % CV // P, (c - C_CU) // CV
                    if gate:
                        act.activation(cacc[:, m, :], banks[:, n % 4, :], ACT.Sigmoid).then_inc(evac, 1)
                    else:
                        act.activation(hpad[:, m, TAPS - 1:], banks[:, n % 4, :], ACT.Copy).then_inc(evac, 1)
                elif c < C_HF:
                    h = c // P
                    chain.step(act.activation(hq[:, h, :], banks[:, n % 4, :], ACT.Copy, scale=float(HG_D) ** -0.5))
                    act.activation(hk[:, h, :], banks[:, n % 4, :], ACT.Sigmoid).then_inc(evac, 1)
                elif c < C_HI:
                    h = (c - C_HF) // P
                    chain.step(act.activation(hf[:, h, :], banks[:, n % 4, :], ACT.Sigmoid))
                    act.wait_ge(q_made, h + 1)
                    act.activation(hk[:, h, :], banks[:, n % 4, :], ACT.Sigmoid, scale=-1.0).then_inc(evac, 1)
                else:
                    h = (c - C_HG) // P
                    if h >= 2:
                        act.wait_ge(g_made, h - 1)
                    chain.step(act.activation(sqb[:, h % 2, :], banks[:, n % 4, :], ACT.Sigmoid))
                    if h == 0:
                        act.wait_ge(upd_made, 16)
                    act.activation(hf[:, h, :], banks[:, n % 4, :], ACT.Copy).then_inc(evac, 1)
                n_out[0] += 4 if kind[0] in ("tm4", "tm2") else 1

            def relu_scores(s):
                b = 1 + s // IDX_HEADS
                act.wait_ge(s_made, s + 1)
                if s >= 2:
                    act.wait_ge(score_added, s - 1)
                act.activation(ring2[:, s % 2, 0:P * (b + 1)], banks[:, 4 + s % 2, 0:P * (b + 1)], ACT.Relu)\
                   .then_inc(s_read, 1)

            def exps(t):
                n = P * (t // SA_HEADS + 1)
                act.wait_ge(mx_made, t + 1)
                act.activation(ring2[:, t % 2, 0:n], ring2[:, t % 2, 0:n], ACT.Exp, bias=col[:, t % 2:t % 2 + 1],
                               accum_out=col[:, 2 + t % 2:3 + t % 2]).then_inc(e_made, 1)

            def read_turned(t):
                n = P * (t // SA_HEADS + 1)
                act.wait_ge(p_turned, t + 1)
                if t >= 2:
                    act.wait_ge(pv_made, t - 1)
                act.activation(pT[:, t % 2, 0:n], banks[:, 6, 0:n], ACT.Copy).then_inc(pt_read, 1)

            def read_o(t):
                b, h = t // SA_HEADS, t % SA_HEADS
                r = slice(SA_D * (h % 2), SA_D * (h % 2) + SA_D)
                act.wait_ge(pv_made, t + 1)
                act.activation(omix[r, 4 + h // 2, b * P:(b + 1) * P], banks[r, 7, 0:P], ACT.Copy).then_inc(ob_made, 1)

            def omix_hi(n):
                k = OMIX_ORDER[n]
                if k < HG_HEADS:
                    act.wait_ge(oa_made, k + 1)
                elif k < 6:
                    act.wait_ge(ob_made, 16)
                else:
                    act.wait_ge(oc_made, k - 5)
                act.activation(h_hi[:, k, :], omix[:, k, :], ACT.Copy).then_inc(h_hi_made, 1)

            n_out = [0]
            for u in range(N_IN):
                hi_unit(act, u + LEAD)
                read_out(u)
                if u == 4:
                    act.wait_ge(iw_turned, 1)
                    act.activation(iw[:, :, :], banks[:, 6, 0:TT * IDX_HEADS].rearrange("p (t h) -> p t h", t=TT),
                                   ACT.Copy).then_inc(iw_made, 1)
                    for s in range(3 * IDX_HEADS):
                        relu_scores(s)
                if 0 <= u - U_STATE < 3:
                    c = u - U_STATE
                    act.wait_ge(kt_turned, c + 1)
                    if c == 2:
                        act.wait_ge(sp_made, 1)
                    act.activation(hKT[:, c % 2, :, :], banks[:, 4, :].rearrange("p (h k) -> p h k", h=HG_HEADS),
                                   ACT.Copy).then_inc(kt_made, 1)
            act.wait_ge(w_used, N_IN)
            for s in range(N_ATT):
                if 1 <= s <= 16:
                    read_turned(s - 1)
                if s < 16:
                    exps(s)
                if S_COLS.get(s, 4) < 4:
                    n = S_COLS[s] - 1
                    act.wait_ge(ada_used, KT * n)
                    act.wait_ge(g_made, HG_HEADS)
                    act.activation(sqb[0:1, :, :], banks[0:1, 0:2, :], ACT.Copy).then_inc(rows_read, 1)
                if 2 <= s <= 17:
                    read_o(s - 2)
                if s in S_HEADS:
                    h = S_HEADS.index(s)
                    act.wait_ge(o_made, h + 1)
                    chain.step(act.activation(hk[:, h, :], banks[:, 2 + h % 2, :], ACT.Copy))
                    chain.wait()
                    act.activation(hq[:, h, :], banks[:, 2 + h % 2, :], ACT.Square).then_inc(osq_made, 1)
                if s - 1 in S_HEADS:
                    h = S_HEADS.index(s - 1)
                    act.wait_ge(om_made, h + 1)
                    act.activation(hq[:, h, :], banks[:, 2 + h % 2, :], ACT.Sqrt, bias=eps_c[:, 0:1]).then_inc(oroot_made, 1)
                if s == S_MEAN + 2:
                    for m in range(CVT):
                        act.wait_ge(cen_made, m + 1)
                        act.activation(hpad[:, m, 0:TOK], cacc[:, m, :], ACT.Square).then_inc(csq_made, 1)
                if s == S_VAR:
                    act.wait_ge(var_made, 1)
                    act.activation(rstd[:, :], banks[:, 2, :], ACT.Sqrt, bias=eps_c[:, 0:1]).then_inc(croot_made, 1)
                if s == S_VAR + 2:
                    for m in range(CVT):
                        act.wait_ge(cn_made, m + 1)
                        act.activation(hpad[:, m, 0:TOK], cacc[:, m, :], ACT.Sigmoid, bias=pcol("cv_ln_b", m))\
                           .then_inc(csig_made, 1)
                if s >= S_OMIX:
                    omix_hi(s - S_OMIX)
            for n in range(N_ATT - S_OMIX, KT):
                omix_hi(n)

            def residual(base, count, units, x0, q0=None, leads=True, scaled=False):
                def turn(i, lead):
                    for j in range(RING):
                        if lead or j + LEAD < RING:
                            hi_unit(act, base + j + LEAD, i)
                        if (j + 1) % units == 0 and q0 is not None:
                            t, per = j // units, RING // units
                            act.wait_ge(x_new, x0 + t + 1 + per * i)
                            act.wait_ge(sq_added, q0 + t - 1 + per * i)
                            x = xT[:, bass.ds(i * per + t, 1), :].rearrange("p a n -> p (a n)")
                            plain_wait()
                            act.activation(sqb[:, t % 2, :], x, ACT.Square).then_inc(sq_made, 1)
                            if scaled:
                                w = par[:, bass.ds(i * per + (PCOL["final_norm_w"] + t), 1)]
                                act.wait_ge(sq2_added, t + 1 + per * i)
                                plain_wait()
                                act.activation(relu[:, t % 2, :], x, ACT.Square, scale=w).then_inc(sq1_made, 1)
                if leads:
                    with act.Fori(0, count // RING) as i:
                        turn(i, True)
                else:
                    with act.Fori(0, count // RING - 1) as i:
                        turn(i, True)
                    turn(count // RING - 1, False)

            residual(U_OUT, KT, 1, X_OUT, Q_OUT)
            root(2)
            shifted(S_FF, 3 * KT)
            for half in range(2):
                with act.Fori(0, 4) as i:
                    for j in range(RING):
                        u = U_FF + 32 * half + j
                        n = 16 * half + j
                        hi_unit(act, u + LEAD, i)
                        act.wait_ge(w_used, u + 1 + RING * i)
                        act.wait_ge(h_ready, H_HID + n - 1 + RING * i)
                        act.activation(relu[:, j % 2, :], banks[:, j, :], ACT.Relu).then_inc(evac, 1)
                        act.wait_ge(evac, E_FF + n + 1 + RING * i)
                        plain_wait()
                        act.activation(hid_hi[:, bass.ds(i * RING + j, 1), :].rearrange("p a n -> p (a n)"),
                                       relu[:, j % 2, :], ACT.Square).then_inc(h_hi_made, 1)
                residual(U_FF + 32 * half + 16, 16, 2, X_FF + KT * half, Q_FF if half else None, scaled=half == 1)
            chain.link(act.activation(junk[:, :], eps_c[:, 0:1], ACT.Sqrt))
            act.wait_ge(x_new, X_FIN)
            act.wait_ge(stat_made, 4)
            act.dma_start(ws[:, :, :], a["a_w_s_2"][0].rearrange("g t s -> t g s")).then_inc(ws_in, 16)
            act.dma_start(bsp[:, :, :], a["a_b_s_2"][0].rearrange("(o g) t -> o g t", o=1).broadcast_to([P, A_GROUPS, P]))\
               .then_inc(bs_in, 16)
            act.wait_ge(mean2_made, 1)
            act.activation(rstd[:, :], rstd[:, :], ACT.Sqrt, bias=eps_c[:, 2:3]).then_inc(root_made, 1)
            act.activation(e2[:, 0, :], banks[:, 7, :], ACT.Sqrt, bias=eps_c[:, 0:1]).then_inc(root_made, 1)
            act.wait_ge(ws_turned, 1)
            act.activation(wcT[:, :, :].rearrange("p (b g) t -> p b (g t)", b=2), banks[:, 4:6, :], ACT.Copy)\
               .then_inc(ws_copied, 1)
            shifted(S_SGU, None)
            with act.Fori(0, 2) as i:
                for cl in range(2):
                    def vtile(t):
                        return vt[:, t, bass.ds(i * 1024 + cl * 512, 512)]
                    for j in range(4):
                        hi_unit(act, U_V + 4 * cl + j + LEAD, i * 2)
                    act.wait_ge(w_used, U_V + 4 * cl + 4 + 8 * i)
                    for t in range(TT):
                        v = vtile(t)
                        plain_wait()
                        act.activation(v, banks[:, 4 * cl + t, :], ACT.Copy).then_inc(v_copied, 1)
                        n = 4 * cl + t
                        act.wait_ge(v_stat, V0 + n - 1 + 8 * i)
                        act.activation(e0[:, t % 2, :], banks[:, 4 * cl + t, :], ACT.Square).then_inc(evac, 1)
                        act.wait_ge(v_inner, n + 1 + 8 * i)
                        act.activation(e0[:, t % 2, :], e0[:, t % 2, :], ACT.Tanh).then_inc(v_tanh, 1)
            act.wait_ge(v_var, TT)
            act.activation(vrs[:, :], vmv[:, :, 1], ACT.Sqrt, bias=eps_c[:, 1:2]).then_inc(v_root, 1)
            for half in range(2):
                with act.Fori(0, 4) as i:
                    for cc in range(2):
                        u, c = U_UG + 24 * half + 2 * cc, 8 * half + cc
                        hi_unit(act, u + LEAD, i)
                        act.wait_ge(w_used, u + 1 + RING * i)
                        act.wait_ge(h_ready, H_Y + c - 1 + 2 * i)
                        act.activation(e0[:, cc, :], banks[:, 4 * cc, :], ACT.Square).then_inc(u_sq, 1)
                        act.wait_ge(u_inner, c + 1 + 2 * i)
                        act.activation(e0[:, cc, :], e0[:, cc, :], ACT.Tanh).then_inc(u_tanh, 1)
                        hi_unit(act, u + 1 + LEAD, i)
                        act.wait_ge(w_used, u + 2 + RING * i)
                        act.activation(e1[:, cc, :], banks[:, 4 * cc + 1, :], ACT.Sigmoid).then_inc(g_sig, 1)
                        act.wait_ge(y_out, c + 1 + 2 * i)
                        plain_wait()
                        act.activation(y_hi[:, bass.ds(i * 2 + cc, 1), :].rearrange("p a n -> p (a n)"), e2[:, cc, :],
                                       ACT.Copy).then_inc(h_hi_made, 1)
                residual(U_UG + 24 * half + 16, KT, 1, X_AO + KT * half, Q_AO if half else None)
            root(5)
            shifted(S_RG, None)
            act.wait_ge(sp_abs, 1)
            act.activation(spt[:, 1, :], spt[:, 0, :], ACT.Exp, scale=-1.0).then_inc(sp_exp, 1)
            act.wait_ge(pad_zero, 1)
            act.wait_ge(sp_ready, 1)

            def read_x(cc, i):
                act.wait_ge(w_used, U_B + 2 * cc + 1 + RING * i)
                act.activation(xbp[:, cc, B_TAPS:], banks[:, 4 * cc, :], ACT.Copy).then_inc(evac, 1)

            def read_gates(cc, i):
                act.wait_ge(gates_made, cc + 1 + 2 * i)
                plain_wait()
                act.activation(t_r[:, cc, :], banks[:, 4 * cc + 2, :], ACT.Sigmoid,
                               bias=par[:, bass.ds(i * 2 + (PCOL["b_gate_a_b_2"] + cc), 1)]).then_inc(evac, 1)
                plain_wait()
                act.activation(t_i[:, cc, :], banks[:, 4 * cc + 3, :], ACT.Sigmoid,
                               bias=par[:, bass.ds(i * 2 + (PCOL["b_gate_x_b_2"] + cc), 1)]).then_inc(evac, 1)

            def read_g(cc, i):
                act.wait_ge(w_used, U_B + 2 * cc + 2 + RING * i)
                act.activation(t_sg[:, cc, :], banks[:, 4 * cc + 1, :], ACT.Sigmoid).then_inc(g_sig, 1)
                act.activation(t_g[:, cc, :], banks[:, 4 * cc + 1, :], ACT.Copy).then_inc(evac, 1)

            def decay_curves(i):
                for cc in range(2):
                    act.wait_ge(evac, E_RG + (4, 7)[cc] + 8 * i)
                    plain_wait()
                    act.activation(t_a[:, cc, :], t_r[:, cc, :], ACT.Exp,
                                   scale=spt[:, 1, bass.ds(i * 2 + cc, 1)]).then_inc(ra_made, 1)
                for cc in range(2):
                    act.wait_ge(ra_made, cc + 1 + 2 * i)
                    plain_wait()
                    act.activation(t_r[:, cc, :], t_r[:, cc, :], ACT.Tanh,
                                   scale=spt[:, 4, bass.ds(i * 2 + cc, 1)]).then_inc(rt_made, 1)
                for cc in range(2):
                    act.wait_ge(rt_made, cc + 1 + 2 * i)
                    act.activation(t_s[:, cc, :], t_r[:, cc, :], ACT.Sqrt).then_inc(rs_made, 1)

            def yb_high(cc, i):
                act.wait_ge(yb_out, cc + 1 + 2 * i)
                plain_wait()
                act.activation(yb_hi[:, bass.ds(i * 2 + cc, 1), :].rearrange("p a n -> p (a n)"), t_b[:, cc, :],
                               ACT.Copy).then_inc(h_hi_made, 1)

            def turn(i, before):
                hi_unit(act, U_B + LEAD, i)
                read_x(0, i)
                if before is not None:
                    decay_curves(before)
                hi_unit(act, U_B + 1 + LEAD, i)
                hi_unit(act, U_B + 2 + LEAD, i)
                read_x(1, i)
                if before is not None:
                    for cc in range(2):
                        yb_high(cc, before)
                read_gates(0, i)
                read_g(0, i)
                hi_unit(act, U_B + 3 + LEAD, i)
                read_gates(1, i)
                read_g(1, i)

            turn(0, None)
            with act.Fori(1, B_HEADS // 2) as i:
                turn(i, i - 1)
            decay_curves(B_HEADS // 2 - 1)
            for cc in range(2):
                yb_high(cc, B_HEADS // 2 - 1)
            residual(U_BOUT, 16, 2, X_BO, Q_BO, leads=False)
            chain.link(act.activation(junk[:, :], eps_c[:, 0:1], ACT.Sqrt))
            act.wait_ge(stat_made, 6)
            act.activation(rs[:, :], banks[:, 6, 0:TT], ACT.Sqrt, bias=eps_c[:, 0:1]).then_inc(root_made, 1)
            act.wait_ge(rs_ready, 1)
            for t in range(TT):
                act.wait_ge(fin_turned, 1)
                act.activation(y_tok[:, t, 0:512], banks[:, 2 + t, :], ACT.Copy, scale=rs[:, t:t + 1]).then_inc(y_made, 1)

        @block.vector
        def _(dve):
            chain = Chain(dve, s_dve)
            dve.memset(ssq[:, :], 0.0).then_inc(ssq_zero, 1)
            dve.wait_ge(c_sig, 1)
            dve.tensor_tensor(c_act[:, :], c_act[:, :], cT[:, :], ALU.mult).then_inc(c_ready, 1)
            dve.wait_ge(c_ready, 1)

            def add_square(q, buf):
                dve.wait_ge(sq_made, q + 1)
                if q:
                    dve.wait_ge(sq_added, q)
                dve.tensor_tensor(ssq[:, :], ssq[:, :], buf, ALU.add).then_inc(sq_added, 1)

            def new_sum(n):
                dve.wait_ge(stat_made, n)
                dve.memset(ssq[:, :], 0.0).then_inc(ssq_zero, 1)
                dve.wait_ge(ssq_zero, min(n, 4) + 1)

            dve.wait_ge(ssq_zero, 1)
            for k in range(KT):
                d = arrival[ADA[KT + k]]
                raw_wait(dve, d)
                if k:
                    dve.wait_ge(ada_dve, k)
                    ins = dve.scalar_tensor_tensor(acc1[:, :], raw[:, d % RING, :], c_act[:, k:k + 1], acc1[:, :],
                                                   ALU.mult, ALU.add)
                else:
                    ins = dve.tensor_scalar(acc1[:, :], raw[:, d % RING, :], c_act[:, 0:1], None, ALU.mult)
                ins.then_inc(ada_dve, 1)
                if k < KT // 2:
                    for q in (2 * k, 2 * k + 1):
                        add_square(q, sqb[:, q % 2, :])
            dve.wait_ge(par_ready, 1)
            logit = pcol("hg_lb_logits", 0, HG_HEADS)
            dve.tensor_tensor(lbt[:, 0, :], logit, logit, ALU.subtract).then_inc(lb_zero, 1)
            dve.wait_ge(root_made, 1)
            chain.link(dve.reciprocal(rstd[:, :], rstd[:, :]))
            dve.wait_ge(lb_exp, 1)
            chain.link(dve.reciprocal(lbt[:, 2, :], lbt[:, 1, :]))
            chain.link(dve.tensor_tensor(lbt[:, 1, :], lbt[:, 1, :], lbt[:, 2, :], ALU.mult))
            chain.link(dve.tensor_tensor(lbt[:, 2, :], lbt[:, 1, :], lbt[:, 1, :], ALU.subtract))
            chain.link(dve.tensor_scalar(lbt[:, 3, :], lbt[:, 2, :], -1.0, 1.0, ALU.mult, ALU.add))

            def mod_part(n, group):
                dve.wait_ge(mod_summed, n + 1)
                g0 = group * KT
                dve.tensor_tensor(mod[:, g0:g0 + KT], banks[:, 4 if n == 1 else 3, 0:KT], pcol("ada_b", g0, KT), ALU.add)\
                   .then_inc(mod_ready, 1)

            mod_part(0, 0)
            mod_part(1, 1)
            dve.wait_ge(mod_ready, 2)
            chain.link(dve.scalar_tensor_tensor(scale1[:, :], mod[:, KT:2 * KT], 1.0, pcol("norm_mix_w", 0, KT),
                                                ALU.add, ALU.mult))

            def normalised(n, r0, scale, shift):
                if n > 1:
                    dve.wait_ge(root_made, n)
                    chain.link(dve.reciprocal(rstd[:, :], rstd[:, :]))

                def low(k):
                    dve.wait_ge(h_hi_made, r0 + k + 1)
                    t, hi = sqb[:, k % 2, :], h_hi[:, k, :].bitcast(F32)
                    if shift is None:
                        ins = dve.tensor_tensor(h_lo[:, k, :], t, hi, ALU.subtract)
                    else:
                        ins = dve.scalar_tensor_tensor(h_lo[:, k, :], t, mod[:, shift + k:shift + k + 1], hi,
                                                       ALU.add, ALU.subtract)
                    ins.then_inc(h_ready, 1)

                if shift is not None:
                    dve.wait_ge(mod_ready, 2)
                for k in range(KT):
                    if k >= 2:
                        dve.wait_ge(h_ready, r0 + k - 1)
                    dve.scalar_tensor_tensor(sqb[:, k % 2, :], xT[:, k, :], scale(k), rstd[:, :], ALU.mult, ALU.mult)\
                       .then_inc(h_scaled, 1)
                    if k:
                        low(k - 1)
                    if n == 1 and k < LEAD:
                        lo_unit(dve, k)
                low(KT - 1)

            normalised(1, H_MIX, lambda k: scale1[:, k:k + 1], 0)


            def add_score(s):
                b, h = 1 + s // IDX_HEADS, s % IDX_HEADS
                n = P * (b + 1)
                dve.wait_ge(s_read, s + 1)
                if s:
                    dve.wait_ge(score_added, s)
                if s == 0:
                    dve.wait_ge(iw_made, 1)
                w = iw[:, b, h:h + 1]
                if h == 0:
                    ins = dve.tensor_scalar(score[b][:, :], ring2[:, s % 2, 0:n], w, None, ALU.mult)
                else:
                    ins = dve.scalar_tensor_tensor(score[b][:, :], ring2[:, s % 2, 0:n], w, score[b][:, :], ALU.mult, ALU.add)
                ins.then_inc(score_added, 1)

            def top_round(r):
                if r == 0:
                    dve.wait_ge(diag_made, 3)
                for b in range(3):
                    chain.step(dve.max(m8[:, b, :], score[b + 1][:, :]))
                n = chain.n
                for b in range(3):
                    chain.wait(n - 2 + b)
                    chain.step(dve.match_replace(score[b + 1][:, :], m8[:, b, :], score[b + 1][:, :], TAKEN))
                chain.wait()

            def soft_in(t):
                b = t // SA_HEADS
                n = P * (b + 1)
                dve.wait_ge(l_made, t + 1)
                if t % SA_HEADS == 0:
                    dve.wait_ge(bias_made, b + 1)
                if t >= 2:
                    dve.wait_ge(p_turned, t - 1)
                dve.scalar_tensor_tensor(ring2[:, t % 2, 0:n], banks[:, 4 + t % 2, 0:n], float(SA_D) ** -0.5,
                                         score[b][:, :], ALU.mult, ALU.add).then_inc(l_read, 1)
                dve.wait_ge(l_read, t + 1)
                dve.tensor_reduce(col[:, t % 2:t % 2 + 1], ring2[:, t % 2, 0:n], AX_X, ALU.max, negate=True)\
                   .then_inc(mx_made, 1)

            def soft_out(t):
                n = P * (t // SA_HEADS + 1)
                dve.wait_ge(e_made, t + 1)
                chain.link(dve.reciprocal(col[:, 4 + t % 2:5 + t % 2], col[:, 2 + t % 2:3 + t % 2]))
                dve.tensor_scalar(ring2[:, t % 2, 0:n], ring2[:, t % 2, 0:n], col[:, 4 + t % 2:5 + t % 2], None, ALU.mult)\
                   .then_inc(p_made, 1)

            rounds = list(range(TOPK // 8))

            def decays():
                for h in range(HG_HEADS):
                    dve.wait_ge(evac, 13 + h)
                    lb, om = lbt[:, 2, h:h + 1], lbt[:, 3, h:h + 1]
                    chain.step(dve.tensor_scalar(hf[:, h, :], hf[:, h, :], om, lb, ALU.mult, ALU.add))
                    chain.step(dve.tensor_scalar(hk[:, h, :], hk[:, h, :], om, None, ALU.mult))
                    chain.wait(chain.n - 1)
                    dve.tensor_scalar(hf[:, h, :], hf[:, h, :], TINY, None, ALU.max).then_inc(f_made, 1)
                dve.wait_ge(f_made, HG_HEADS)
                dve.wait_ge(q_made, HG_HEADS)

            def level(n):
                l, p = n // 2, n % 2
                dve.wait_ge(lev_made, n + 1)
                A = hA[:, 2 * p:2 * p + 2, :, :].rearrange("p h c i -> p (h c) i")
                S = banks[:, 4 + 2 * p:6 + 2 * p, :].rearrange("p b (c i) -> p (b c) i", c=TT)
                if l == 0:
                    chain.step(dve.tensor_tensor(A, S, ident[:, :].unsqueeze(1).broadcast_to([P, 8, P]), ALU.mult))
                    dve.tensor_tensor(hq[:, 2 * p:2 * p + 2, :], hq[:, 2 * p:2 * p + 2, :], hf[:, 2 * p:2 * p + 2, :],
                                      ALU.mult).then_inc(upd_made, 1)
                    return
                dve.wait_ge(upd_made, n - 1)
                chain.step(dve.copy_predicated(A, masks[:, l - 1, :].bitcast(I32).unsqueeze(1).broadcast_to([P, 8, P]), S))
                b = LEVELS[l - 1]
                T = t_level(b, p)
                for h in range(2):
                    Q, K = halves(hq, b, p)[:, h, :, 1, :], halves(hk, b, p)[:, h, :, 0, :]
                    shape = [P, TOK // (2 * b), b]
                    chain.step(dve.tensor_tensor(Q, Q, T[:, h, :, 0].unsqueeze(2).broadcast_to(shape), ALU.mult))
                    chain.step(dve.tensor_tensor(K, K, T[:, h, :, 1].unsqueeze(2).broadcast_to(shape), ALU.mult))
                up = hgt[:, 2 * p:2 * p + 2, T_OFF[2 * b]:T_OFF[2 * b] + TOK // (2 * b)]
                dve.tensor_tensor(up, T[:, :, :, 0], T[:, :, :, 1], ALU.mult).then_inc(upd_made, 1)

            def state(c):
                dve.wait_ge(sp_made, c + 1)
                for h in range(HG_HEADS):
                    ps = banks[:, 6, h * P:(h + 1) * P]
                    if c == 0:
                        ins = dve.tensor_copy(hS[:, 0, h, :], ps)
                    else:
                        dve.wait_ge(st_made, c)
                        decay = hgt[:, h, T_OFF[128] + c:T_OFF[128] + c + 1]
                        ins = dve.scalar_tensor_tensor(hS[:, c, h, :], hS[:, c - 1, h, :], decay, ps, ALU.mult, ALU.add)
                ins.then_inc(st_made, 1)

            for u in range(N_IN):
                lo_unit(dve, u + LEAD)
                if u == 4:
                    for s in range(3 * IDX_HEADS):
                        add_score(s)
                if u >= 5:
                    for _ in range(TOP_ROUNDS.get(u, 0)):
                        top_round(rounds.pop(0))
                        if not rounds:
                            for b in range(1, TT):
                                dve.tensor_scalar(score[b][:, :], score[b][:, :], TAKEN, NEG_BIG, ALU.not_equal, ALU.mult)\
                                   .then_inc(taken_made, 1)
                if u == min(LEVEL_STEPS):
                    decays()
                for n in LEVEL_STEPS.get(u, ()):
                    level(n)
                if 0 <= u - 1 - U_STATE < 3:
                    state(u - 1 - U_STATE)
            dve.wait_ge(w_used, N_IN)

            def omix_lo(n):
                k = OMIX_ORDER[n]
                dve.wait_ge(h_hi_made, H_OMIX + n + 1)
                dve.tensor_tensor(h_lo[:, k, :], omix[:, k, :], h_hi[:, k, :].bitcast(F32), ALU.subtract).then_inc(h_ready, 1)

            for s in range(N_ATT):
                if 1 <= s <= 16:
                    soft_out(s - 1)
                if s < 16:
                    soft_in(s)
                if s - 2 in S_HEADS:
                    h = S_HEADS.index(s - 2)
                    dve.wait_ge(oroot_made, h + 1)
                    chain.link(dve.reciprocal(hq[:, h, :], hq[:, h, :]))
                    chain.link(dve.scalar_tensor_tensor(hk[:, h, :], hk[:, h, :], pcol("hg_onorm_w", h), hq[:, h, :],
                                                        ALU.mult, ALU.mult))
                    dve.wait_ge(g_made, h + 1)
                    dve.tensor_tensor(omix[:, h, :], hf[:, h, :], hk[:, h, :], ALU.mult).then_inc(oa_made, 1)
                if s == S_MEAN + 1:
                    dve.wait_ge(mean_made, 1)
                    for m in range(CVT):
                        dve.tensor_tensor(cacc[:, m, :], cacc[:, m, :], banks[:, 2, :], ALU.subtract).then_inc(cen_made, 1)
                if s == S_VAR + 1:
                    dve.wait_ge(croot_made, 1)
                    chain.link(dve.reciprocal(rstd[:, :], rstd[:, :]))
                    for m in range(CVT):
                        dve.scalar_tensor_tensor(cacc[:, m, :], cacc[:, m, :], pcol("cv_ln_w", m), rstd[:, :], ALU.mult,
                                                 ALU.mult).then_inc(cn_made, 1)
                if s == S_VAR + 3:
                    for m in range(CVT):
                        dve.wait_ge(csig_made, m + 1)
                        dve.scalar_tensor_tensor(omix[:, 6 + m, :], cacc[:, m, :], pcol("cv_ln_b", m), hpad[:, m, 0:TOK],
                                                 ALU.add, ALU.mult).then_inc(oc_made, 1)
                if s - 1 in S_COLS:
                    mod_part(2 + list(S_COLS).index(s - 1), ADA_GROUPS[S_COLS[s - 1]])
                if s > S_OMIX:
                    omix_lo(s - S_OMIX - 1)
            mod_part(5, ADA_GROUPS[S_COLS[17]])
            dve.wait_ge(mod_ready, 6)
            chain.link(dve.scalar_tensor_tensor(scale2[:, :], mod[:, 4 * KT:5 * KT], 1.0, pcol("norm_mlp_w", 0, KT),
                                                ALU.add, ALU.mult))
            for n in range(N_ATT - S_OMIX - 1, KT):
                omix_lo(n)

            def residual(base, count, units, x0, q0=None, gate=None, leads=True, scaled=False, last=False):
                per = RING // units

                def turn(i, lead):
                    for j in range(RING):
                        if lead or j + LEAD < RING:
                            lo_unit(dve, base + j + LEAD, i)
                        if (j + 1) % units == 0:
                            t = j // units
                            dve.wait_ge(w_used, base + j + 1 + RING * i)
                            x = xT[:, bass.ds(i * per + t, 1), :].rearrange("p a n -> p (a n)")
                            if gate is None:
                                ins = dve.tensor_tensor(x, x, banks[:, t, :], ALU.add)
                            else:
                                ins = dve.scalar_tensor_tensor(x, banks[:, t, :], mod[:, bass.ds(i * per + (gate + t), 1)],
                                                               x, ALU.mult, ALU.add)
                            ins.then_inc(x_new, 1)
                            if q0 is not None:
                                dve.wait_ge(sq_made, q0 + t + 1 + per * i)
                                dve.wait_ge(sq_added, q0 + t + per * i)
                                dve.tensor_tensor(ssq[:, :], ssq[:, :], sqb[:, t % 2, :], ALU.add).then_inc(sq_added, 1)
                            if last:
                                w = par[:, bass.ds(i * per + (PCOL["norm_f_w_2"] + t), 1)]
                                dve.wait_ge(x_new, x0 + t + 1 + per * i)
                                dve.tensor_scalar(x, x, w, None, ALU.mult).then_inc(fin_scaled, 1)
                            if scaled:
                                dve.wait_ge(sq1_made, t + 1 + per * i)
                                dve.wait_ge(sq2_added, 2 + t + per * i)
                                dve.tensor_tensor(relu2[:, 0, :], relu2[:, 0, :], relu[:, t % 2, :], ALU.add)\
                                   .then_inc(sq2_added, 1)
                if leads:
                    with dve.Fori(0, count // RING) as i:
                        turn(i, True)
                else:
                    with dve.Fori(0, count // RING - 1) as i:
                        turn(i, True)
                    turn(count // RING - 1, False)

            new_sum(1)
            residual(U_OUT, KT, 1, X_OUT, Q_OUT, 2 * KT)
            normalised(2, H_FF, lambda k: scale2[:, k:k + 1], 3 * KT)
            new_sum(2)
            for half in range(2):
                with dve.Fori(0, 4) as i:
                    for j in range(RING):
                        n = 16 * half + j
                        lo_unit(dve, U_FF + 32 * half + j + LEAD, i)
                        dve.wait_ge(evac, E_FF + n + 1 + RING * i)
                        dve.wait_ge(h_ready, H_HID + n - 1 + RING * i)
                        dve.tensor_tensor(relu2[:, j % 2, :], relu[:, j % 2, :], relu[:, j % 2, :], ALU.mult)\
                           .then_inc(relu_sq, 1)
                        dve.wait_ge(relu_sq, n + 1 + RING * i)
                        dve.wait_ge(h_hi_made, H_HID + n + 1 + RING * i)
                        dve.tensor_tensor(hid_lo[:, bass.ds(i * RING + j, 1), :].rearrange("p a n -> p (a n)"),
                                          relu2[:, j % 2, :],
                                          hid_hi[:, bass.ds(i * RING + j, 1), :].rearrange("p a n -> p (a n)").bitcast(F32),
                                          ALU.subtract).then_inc(h_ready, 1)
                if half:
                    dve.memset(relu2[:, 0, :], 0.0).then_inc(sq2_added, 2)
                residual(U_FF + 32 * half + 16, 16, 2, X_FF + KT * half, Q_FF if half else None, 5 * KT, scaled=half == 1)
            dve.wait_ge(stat_made, 3)
            chain.link(dve.tensor_scalar(rstd[:, :], banks[:, 7, :], EPS, None, ALU.mult))
            dve.wait_ge(stat_made, 4)
            dve.tensor_tensor(rstd[:, :], rstd[:, :], banks[:, 6, :], ALU.add).then_inc(mean2_made, 1)
            chain.link(dve.tensor_tensor(scale4[:, :], pcol("final_norm_w", 0, KT), pcol("norm_w_2", 0, KT), ALU.mult))
            new_sum(3)
            normalised(3, H_SGU, lambda k: scale4[:, k:k + 1], None)
            dve.wait_ge(root_made, 4)
            chain.link(dve.reciprocal(e2[:, 0, :], e2[:, 0, :]))
            for k in range(KT):
                dve.scalar_tensor_tensor(xT[:, k, :], xT[:, k, :], pcol("final_norm_w", k), e2[:, 0, :], ALU.mult, ALU.mult)\
                   .then_inc(x_new, 1)
            dve.wait_ge(bs_in, 16)
            dve.tensor_scalar(bsp[:, :, :], bsp[:, :, :], 0.5, None, ALU.mult).then_inc(v_stat, 1)
            dve.tensor_scalar(lnw2[:, :], pcol("a_ln_w_2", 0, AT), 0.5, None, ALU.mult).then_inc(v_stat, 1)
            with dve.Fori(0, 2) as i:
                for cl in range(2):
                    def vtile(t):
                        return vt[:, t, bass.ds(i * 1024 + cl * 512, 512)]
                    for j in range(4):
                        lo_unit(dve, U_V + 4 * cl + j + LEAD, i * 2)
                    for t in range(TT):
                        n = 4 * cl + t
                        e = e0[:, t % 2, :]
                        dve.wait_ge(evac, E_V + n + 1 + 8 * i)
                        dve.wait_ge(v_copied, n + 1 + 8 * i)
                        dve.tensor_scalar(e, e, GELU_C * GELU_A, GELU_C, ALU.mult, ALU.add).then_inc(v_aff, 1)
                        dve.wait_ge(v_aff, n + 1 + 8 * i)
                        dve.tensor_tensor(e, e, vtile(t), ALU.mult).then_inc(v_inner, 1)
                        dve.wait_ge(v_tanh, n + 1 + 8 * i)
                        dve.scalar_tensor_tensor(vtile(t), e, 1.0, vtile(t), ALU.add, ALU.mult).then_inc(v_gelu, 1)
                        dve.wait_ge(v_gelu, n + 1 + 8 * i)
                        dve.bn_stats(vst[:, t, bass.ds(i * 2 + cl, 1), :].rearrange("p a n -> p (a n)"), vtile(t))\
                           .then_inc(v_stat, 1)
            dve.wait_ge(v_stat, V0 + 16)
            for t in range(TT):
                dve.bn_aggr(vmv[:, t, :], vst[:, t, :, :].rearrange("p a n -> p (a n)")).then_inc(v_var, 1)
            dve.wait_ge(ws_summed, 1)
            for g in range(2):
                dve.tensor_scalar(wsum[:, 4 * g:4 * g + 4, :].rearrange("p g t -> p (g t)"), banks[:, 2 + g, :], 0.5, None,
                                  ALU.mult).then_inc(wsum_made, 1)
            dve.wait_ge(v_root, 1)
            chain.link(dve.reciprocal(vrs[:, :], vrs[:, :]))
            for half in range(2):
                with dve.Fori(0, 4) as i:
                    for cc in range(2):
                        u, c = U_UG + 24 * half + 2 * cc, 8 * half + cc
                        dve.wait_ge(h_ready, H_Y + c - 1 + 2 * i)
                        for t in range(TT):
                            ins = dve.tensor_scalar(vh[:, cc, t, :], vt[:, t, bass.ds(i * 2 * P + c * P, P)],
                                                    vmv[:, t, 0:1], vrs[:, t:t + 1], ALU.subtract, ALU.mult)
                        ins.then_inc(vh_made, 1)
                        lo_unit(dve, u + LEAD, i)
                        e = e0[:, cc, :]
                        dve.wait_ge(u_sq, c + 1 + 2 * i)
                        dve.tensor_scalar(e, e, GELU_C * GELU_A, GELU_C, ALU.mult, ALU.add).then_inc(u_aff, 1)
                        dve.wait_ge(u_aff, c + 1 + 2 * i)
                        dve.tensor_tensor(e, e, banks[:, 4 * cc, :], ALU.mult).then_inc(u_inner, 1)
                        dve.scalar_tensor_tensor(eb[:, cc, :], wsum[:, bass.ds(i + 4 * half, 1), :].rearrange("p g t -> p (g t)"),
                                                 par[:, bass.ds(i * 2 + (PCOL["a_ln_b_2"] + c), 1)],
                                                 bsp[:, bass.ds(i + 4 * half, 1), :].rearrange("p g t -> p (g t)"),
                                                 ALU.mult, ALU.add).then_inc(eb_made, 1)
                        lo_unit(dve, u + 1 + LEAD, i)
                        dve.wait_ge(u_tanh, c + 1 + 2 * i)
                        dve.scalar_tensor_tensor(e, e, 1.0, banks[:, 4 * cc, :], ALU.add, ALU.mult).then_inc(u_gelu, 1)
                        dve.wait_ge(g_sig, c + 1 + 2 * i)
                        dve.tensor_tensor(e1[:, cc, :], e1[:, cc, :], banks[:, 4 * cc + 1, :], ALU.mult).then_inc(ug_made, 1)
                        dve.wait_ge(mixed, c + 1 + 2 * i)
                        dve.wait_ge(eb_made, c + 1 + 2 * i)
                        dve.scalar_tensor_tensor(e2[:, cc, :].rearrange("p (n t) -> p n t", t=P),
                                                 banks[:, 4 * cc + 2, :].rearrange("p (n t) -> p n t", t=P),
                                                 lnw2[:, bass.ds(i * 2 + c, 1)],
                                                 eb[:, cc, :].unsqueeze(1).broadcast_to([P, TT, P]),
                                                 ALU.mult, ALU.add).then_inc(s_mixed, 1)
                        dve.wait_ge(s_mixed, c + 1 + 2 * i)
                        dve.wait_ge(ugp_made, c + 1 + 2 * i)
                        dve.tensor_tensor(e2[:, cc, :], e2[:, cc, :], e, ALU.mult).then_inc(y_out, 1)
                        dve.wait_ge(y_out, c + 1 + 2 * i)
                        dve.wait_ge(h_hi_made, H_Y + c + 1 + 2 * i)
                        k = bass.ds(i * 2 + cc, 1)
                        dve.tensor_tensor(y_lo[:, k, :].rearrange("p a n -> p (a n)"), e2[:, cc, :],
                                          y_hi[:, k, :].rearrange("p a n -> p (a n)").bitcast(F32),
                                          ALU.subtract).then_inc(h_ready, 1)
                residual(U_UG + 24 * half + 16, KT, 1, X_AO + KT * half, Q_AO if half else None)
            lam = pcol("b_lambda_2", 0, B_HEADS)
            s_, e_, m_, q_, o_ = (spt[:, k, :] for k in range(5))
            dve.wait_ge(x_new, X_BO)
            chain.link(dve.tensor_scalar(m_, lam, -1.0, 0.0, ALU.mult, ALU.max))
            chain.link(dve.tensor_scalar(s_, lam, 0.0, None, ALU.max))
            dve.tensor_tensor(s_, s_, m_, ALU.add).then_inc(sp_abs, 1)
            normalised(5, H_RG, lambda k: pcol("norm_w_2", KT + k), None)
            new_sum(5)
            dve.memset(xbp[:, :, 0:B_TAPS], 0.0).then_inc(pad_zero, 1)
            dve.wait_ge(sp_exp, 1)
            chain.link(dve.tensor_scalar(s_, e_, 2.0, None, ALU.add))
            chain.link(dve.reciprocal(s_, s_))
            chain.link(dve.tensor_tensor(s_, s_, e_, ALU.mult))
            chain.link(dve.tensor_tensor(q_, s_, s_, ALU.mult))
            chain.link(dve.tensor_scalar(o_, q_, 1.0 / 17, None, ALU.mult))
            for k in (15, 13, 11, 9, 7, 5, 3):
                chain.link(dve.scalar_tensor_tensor(o_, o_, 1.0 / k, q_, ALU.add, ALU.mult))
            chain.link(dve.scalar_tensor_tensor(o_, o_, 1.0, s_, ALU.add, ALU.mult))
            chain.link(dve.scalar_tensor_tensor(o_, o_, 2.0, m_, ALU.mult, ALU.add))
            chain.link(dve.tensor_scalar(e_, o_, -RG_C, None, ALU.mult))
            dve.tensor_scalar(o_, o_, RG_C / 2, None, ALU.mult).then_inc(sp_ready, 1)

            def conv(cc, i, first=False):
                dve.wait_ge(evac, E_RG + cc + 1 + 8 * i)
                if not first:
                    dve.wait_ge(gates_made, cc - 1 + 2 * i)
                    dve.wait_ge(ix_made, cc - 1 + 2 * i)
                for k in range(B_TAPS):
                    src = xbp[:, cc, 1 + k:1 + k + TOK]
                    w = par[:, bass.ds(i * 2 + (PCOL["b_conv_w_2"] + B_HEADS * k + cc), 1)]
                    if k == 0:
                        ins = dve.tensor_scalar(xc[:, cc, :], src, w, par[:, bass.ds(i * 2 + (PCOL["b_conv_b_2"] + cc), 1)],
                                                ALU.mult, ALU.add)
                    else:
                        dve.wait_ge(tap_made, 3 * cc + k + 6 * i)
                        ins = dve.scalar_tensor_tensor(xc[:, cc, :], src, w, xc[:, cc, :], ALU.mult, ALU.add)
                    ins.then_inc(tap_made if k < B_TAPS - 1 else xc_made, 1)

            def recurrence(cc, i):
                n = cc + 1 + 2 * i
                dve.wait_ge(ra_made, n)
                dve.wait_ge(rt_made, n)
                dve.scalar_tensor_tensor(t_a[:, cc, :], t_a[:, cc, :], 1.0, t_r[:, cc, :], ALU.add, ALU.mult)\
                   .then_inc(a1_made, 1)
                dve.wait_ge(a1_made, n)
                dve.tensor_scalar(t_a[:, cc, :], t_a[:, cc, :], -1.0, 1.0, ALU.mult, ALU.add).then_inc(a_made, 1)
                dve.wait_ge(a_made, n)
                dve.wait_ge(rs_made, n)
                dve.scalar_tensor_tensor(t_s[:, cc, :], t_a[:, cc, :], 1.0, t_s[:, cc, :], ALU.add, ALU.mult)\
                   .then_inc(mult_made, 1)
                dve.wait_ge(mult_made, n)
                dve.wait_ge(ix_made, n)
                dve.tensor_tensor(t_b[:, cc, :], t_s[:, cc, :], t_i[:, cc, :], ALU.mult).then_inc(bt_made, 1)
                dve.wait_ge(bt_made, n)
                dve.tensor_tensor_scan(t_s[:, cc, :], t_a[:, cc, :], t_b[:, cc, :], 0.0, ALU.mult, ALU.add)\
                   .then_inc(scanned, 1)
                dve.wait_ge(scanned, n)
                dve.wait_ge(gg_made, n)
                dve.tensor_tensor(t_b[:, cc, :], t_s[:, cc, :], t_g[:, cc, :], ALU.mult).then_inc(yb_out, 1)

            def yb_low(cc, i):
                dve.wait_ge(h_hi_made, H_YB + cc + 1 + 2 * i)
                k = bass.ds(i * 2 + cc, 1)
                dve.tensor_tensor(yb_lo[:, k, :].rearrange("p a n -> p (a n)"), t_b[:, cc, :],
                                  yb_hi[:, k, :].rearrange("p a n -> p (a n)").bitcast(F32),
                                  ALU.subtract).then_inc(h_ready, 1)

            def turn(i, before):
                lo_unit(dve, U_B + LEAD, i)
                conv(0, i, before is None)
                if before is not None:
                    recurrence(0, before)
                lo_unit(dve, U_B + 1 + LEAD, i)
                lo_unit(dve, U_B + 2 + LEAD, i)
                conv(1, i, before is None)
                if before is not None:
                    recurrence(1, before)
                    for cc in range(2):
                        yb_low(cc, before)
                lo_unit(dve, U_B + 3 + LEAD, i)

            turn(0, None)
            with dve.Fori(1, B_HEADS // 2) as i:
                turn(i, i - 1)
            for cc in range(2):
                recurrence(cc, B_HEADS // 2 - 1)
            for cc in range(2):
                yb_low(cc, B_HEADS // 2 - 1)
            residual(U_BOUT, 16, 2, X_BO, Q_BO, leads=False, last=True)
            dve.wait_ge(root_made, 6)
            dve.reciprocal(rs[:, :], rs[:, :]).then_inc(rs_ready, 1)
            dve.wait_ge(rs_ready, 1)
            for t in range(TT):
                dve.wait_ge(fin_turned, t + 2)
                dve.tensor_scalar(y_tok[:, t, 512:1024], banks[:, (7, 0, 1, 6)[t], :], rs[:, t:t + 1], None, ALU.mult)\
                   .then_inc(y2_made, 1)

        @block.gpsimd
        def _(pool):
            chain = Chain(pool, s_pool)
            chain.step(pool.memset(ident[:, :], 0.0))
            chain.step(pool.memset(ones_d[:, :], 1.0 / D))
            chain.step(pool.memset(ones1[:, :], 1.0))
            chain.step(pool.memset(ones_m[:, 0, :], 1.0 / HG_D))
            chain.step(pool.memset(ones_m[:, 1, :], 1.0 / CV))
            chain.step(pool.memset(eps_c[:, 0:1], EPS))
            chain.step(pool.memset(eps_c[:, 1:2], 4 * LN_EPS))
            chain.step(pool.memset(eps_c[:, 2:3], EPS * EPS))
            chain.wait()
            pool.affine_select(out=ident[:, :], in_=ident[:, :], compare_op=ALU.not_equal, fill=1.0, base=0,
                               pattern=[[-1, P]], channel_multiplier=1).then_inc(consts, 1)
            chain.link(pool.memset(par_rows[:, :, :], 0.0))
            for name, rows in PARAMS:
                if name.startswith("pad"):
                    continue
                src = a[name]
                if name == "norm_f_w_2" or name == "final_norm_w":
                    src = src.rearrange("(r p) -> r p", p=P)
                elif name in ("cv_w", "b_conv_w_2"):
                    src = src[0].rearrange("k (r p) -> (k r) p", p=P)
                else:
                    src = src.rearrange("l (r p) -> (l r) p", p=P)
                c = PCOL[name]
                pool.dma_start(par_rows[c % P:c % P + rows, c // P, :], src).then_inc(par_in, 16)
            chain.link(pool.memset(masks[:, :, :], 0.0))
            for l, b in enumerate(LEVELS):
                v = masks[:, l, :].rearrange("p (n two b) -> p n two b", two=2, b=b)[:, :, 1, :]
                chain.link(pool.memset(v, 1.0))
                chain.link(pool.affine_select(out=v, in_=v, compare_op=ALU.is_ge, fill=0.0, base=0,
                                              pattern=[[-2 * b, P // (2 * b)], [0, b]], channel_multiplier=1))
                chain.link(pool.affine_select(out=v, in_=v, compare_op=ALU.is_ge, fill=0.0, base=b - 1,
                                              pattern=[[2 * b, P // (2 * b)], [0, b]], channel_multiplier=-1))
            pool.wait_ge(x_new, KT)
            pool.wait_ge(mod_summed, 2)
            pool.wait_ge(par_ready, 1)
            chain.step(pool.memset(hpad[:, :, 0:TAPS - 1], 0.0))
            chain.link(pool.memset(score[0][:, :], 0.0))
            pool.affine_select(out=score[0][:, :], in_=score[0][:, :], compare_op=ALU.is_ge, fill=NEG_BIG, base=0,
                               pattern=[[-1, P]], channel_multiplier=1).then_inc(bias_made, 1)
            taps = [(m, k) for m in range(CVT) for k in range(TAPS)]

            def tap(m, k):
                src, w = hpad[:, m, k:k + TOK], pcol("cv_w", CVT * k + m)
                n = TAPS * m + k
                if k == 0:
                    pool.wait_ge(evac, 6 + 2 * m)
                    g = hpad[:, m, TAPS - 1:]
                    chain.link(pool.tensor_tensor(g, g, cacc[:, m, :], ALU.mult))
                    pool.tensor_scalar(cacc[:, m, :], src, w, pcol("cv_b", m), ALU.mult, ALU.add).then_inc(tapped, 1)
                    return
                tmp = (ssq, rstd)[k % 2][:, :]
                pool.wait_ge(tapped, n - 1)
                pool.tensor_scalar(tmp, src, w, 0.0, ALU.mult, ALU.add).then_inc(weighted, 1)
                pool.wait_ge(weighted, n - m)
                pool.wait_ge(tapped, n)
                pool.tensor_tensor(cacc[:, m, :], cacc[:, m, :], tmp, ALU.add).then_inc(tapped, 1)

            for u in range(N_IN):
                if u == 5:
                    for b in range(1, TT):
                        pool.wait_ge(score_added, IDX_HEADS * b)
                        d = score[b][:, b * P:(b + 1) * P]
                        pool.affine_select(out=d, in_=d, compare_op=ALU.is_ge, fill=NEG_BIG, base=0,
                                           pattern=[[-1, P]], channel_multiplier=1).then_inc(diag_made, 1)
                if u >= 6:
                    for _ in range(3):
                        if taps:
                            tap(*taps.pop(0))
                if u in (U_Q + 1, U_Q + 2, U_Q + 3, U_Q + 4):
                    h = u - U_Q - 1
                    pool.wait_ge(evac, 9 + h)
                    pool.tensor_tensor(hq[:, h, :], hq[:, h, :], hk[:, h, :], ALU.mult).then_inc(q_made, 1)
                if u == max(TOP_ROUNDS) + 1:
                    for b in range(1, TT):
                        pool.wait_ge(taken_made, b)
                        d = score[b][:, b * P:(b + 1) * P]
                        pool.affine_select(out=d, in_=d, compare_op=ALU.is_ge, fill=NEG_BIG, base=0,
                                           pattern=[[-1, P]], channel_multiplier=1).then_inc(bias_made, 1)
            for h in range(HG_HEADS):
                pool.wait_ge(evac, 29 + h)
                pool.tensor_tensor(hf[:, h, :], hf[:, h, :], sqb[:, h % 2, :], ALU.mult).then_inc(g_made, 1)
            pool.wait_ge(upd_made, 16)
            pool.wait_ge(c_ready, 1)
            for n in range(2 * KT):
                g, kt = n // KT, n % KT
                d = arrival[ADA[4 * KT + n]]
                raw_wait(pool, d)
                if n == KT:
                    pool.wait_ge(mod_summed, 4)
                for half in range(2):
                    r = raw[:, d % RING, 512 * half:512 * (half + 1)].rearrange("p (c n) -> p c n", c=2)
                    acc = hgt[:, 2 * half:2 * half + 2, 0:256]
                    if kt == 0:
                        ins = pool.tensor_scalar(acc, r, c_act[:, 0:1], 0.0, ALU.mult, ALU.add)
                    else:
                        tmp = masks[:, 0:4, :].rearrange("p (c l) n -> p c (l n)", c=2)
                        if half == 0:
                            pool.wait_ge(ada_pool, n)
                        pool.tensor_scalar(tmp, r, c_act[:, kt:kt + 1], 0.0, ALU.mult, ALU.add).then_inc(ada_mult, 1)
                        pool.wait_ge(ada_mult, 2 * (n - g) + half - 1)
                        ins = pool.tensor_tensor(acc, acc, tmp, ALU.add)
                    if half:
                        ins.then_inc(ada_pool, 1)
                    else:
                        chain.step(ins)
                        chain.wait()
            pool.wait_ge(ws_copied, 1)
            pool.affine_select(out=wcT[:, :, :], in_=wcT[:, :, :], compare_op=ALU.is_ge, fill=0.0, base=0,
                               pattern=[[0, A_GROUPS], [1, P]], channel_multiplier=-1).then_inc(ws_masked, 1)
            for half in range(2):
                with pool.Fori(0, 4) as i:
                    for cc in range(2):
                        c = 8 * half + cc
                        pool.wait_ge(u_gelu, c + 1 + 2 * i)
                        pool.wait_ge(ug_made, c + 1 + 2 * i)
                        pool.tensor_tensor(e0[:, cc, :], e0[:, cc, :], e1[:, cc, :], ALU.mult).then_inc(ugp_made, 1)
            pool.wait_ge(x_new, X_BO)

            def load_gates(cc, i):
                for n, name in enumerate(("b_gate_a_w_2", "b_gate_x_w_2")):
                    w = a[name][0][bass.ds(i * 2 + cc, 1), :, :].rearrange("h i j -> (h i) j")
                    pool.dma_start(gw[:, cc, n, :], w).then_inc(gw_in[cc], 16)

            def gated(i):
                for cc in range(2):
                    pool.wait_ge(evac, E_RG + (4, 7)[cc] + 8 * i)
                    pool.tensor_tensor(t_i[:, cc, :], t_i[:, cc, :], xc[:, cc, :], ALU.mult).then_inc(ix_made, 1)
                    pool.wait_ge(evac, E_RG + (5, 8)[cc] + 8 * i)
                    pool.tensor_tensor(t_g[:, cc, :], t_g[:, cc, :], t_sg[:, cc, :], ALU.mult).then_inc(gg_made, 1)

            load_gates(0, 0)
            load_gates(1, 0)
            with pool.Fori(0, B_HEADS // 2 - 1) as i:
                gated(i)
                for cc in range(2):
                    pool.wait_ge(gates_made, 2 * i + cc + 1)
                    load_gates(cc, i + 1)
            gated(B_HEADS // 2 - 1)


_INS = [
    "x", "c", "ada_w", "ada_b", "norm_mix_w", "norm_mlp_w", "w_in", "hg_lb_logits", "hg_onorm_w", "cv_w", "cv_b",
    "cv_ln_w", "cv_ln_b", "w_out", "mlp_w1", "mlp_w2", "final_norm_w", "norm_w_2", "a_w_in_2", "a_ln_w_2",
    "a_ln_b_2", "a_w_s_2", "a_b_s_2", "a_w_out_2", "b_w_in_2", "b_conv_w_2", "b_conv_b_2", "b_gate_a_w_2",
    "b_gate_a_b_2", "b_gate_x_w_2", "b_gate_x_b_2", "b_lambda_2", "b_w_out_2", "norm_f_w_2",
]


def program(nc, shapes):
    a = {n: nc.dram_tensor(f"in_{n}", s, F32, kind="ExternalInput").ap() for n, s in shapes.items()}
    out = nc.dram_tensor("out_0", (1, TOK, D), F32, kind="ExternalOutput").ap()
    build(nc, a, out)


def kernel(**inputs):
    import concourse.bacc as bacc
    import numpy as np
    from concourse.bass_utils import run_bass_kernel_spmd

    nc = bacc.Bacc("TRN2", target_bir_lowering=False, num_devices=1)
    arrays = {n: np.ascontiguousarray(inputs[n]) for n in _INS}
    program(nc, {n: v.shape for n, v in arrays.items()})
    r = run_bass_kernel_spmd(nc, [{f"in_{n}": v for n, v in arrays.items()}], core_ids=[0])
    return r.results[0]["out_0"]
```
